# Optimizing a Trainium2 kernel written in Bass

```python
import jax
import jax.numpy as jnp
from jax import lax
import numpy as np

D_MODEL = 1024
BATCH = 1
SEQ = 2048
DEPTH = 2

MIX_WIDTH = D_MODEL
POOL_WINDOWS = (2, 4, 8, 16)
POOL_WIDTH = MIX_WIDTH // 2
POOL_GROUP = POOL_WIDTH // len(POOL_WINDOWS)
HGRN_WIDTH = MIX_WIDTH - POOL_WIDTH
HGRN_EXPAND = 128
HGRN_HEADS = HGRN_WIDTH // HGRN_EXPAND
HGRN_HEAD_I = HGRN_WIDTH // HGRN_HEADS
HGRN_FDIM = HGRN_HEADS * HGRN_EXPAND
HGRN_CHUNK = 64
EVEN_IN = POOL_WIDTH + 2 * HGRN_FDIM + HGRN_WIDTH + MIX_WIDTH
RWKV_HEAD = 64
RWKV_HEADS = MIX_WIDTH // RWKV_HEAD
DECAY_LORA = 64
ICL_LORA = 64
VALUE_LORA = 32
N_EVEN = (DEPTH + 1) // 2
N_ODD = DEPTH // 2
NORM_EPS = 1e-6
LNX_EPS = 64e-5
F32 = jnp.float32

kernel_name = "hybrid_pool_hgrn2_rwkv7_adaln"

def rms_norm(x, g):
    xf = x.astype(F32)
    return xf * lax.rsqrt(jnp.mean(xf * xf, axis=-1, keepdims=True) + NORM_EPS) * g.astype(F32)

def token_shift(x):
    return jnp.pad(x, ((0, 0), (1, 0), (0, 0)))[:, :-1]

def causal_pool_mixer(u, pool_w, pool_scale):
    b, t, _ = u.shape
    count = jnp.arange(1, t + 1, dtype=F32)
    outs = []
    for gi, win in enumerate(POOL_WINDOWS):
        ug = u[..., gi * POOL_GROUP:(gi + 1) * POOL_GROUP]
        cs = jnp.cumsum(ug, axis=1)
        lagged = jnp.pad(cs, ((0, 0), (win, 0), (0, 0)))[:, :t]
        mean = (cs - lagged) / jnp.minimum(count, float(win))[None, :, None]
        outs.append(mean - ug)
    p = jnp.stack(outs, axis=2)
    y = jnp.einsum("btgc,gcd->btgd", p, pool_w.astype(F32)).reshape(b, t, POOL_WIDTH)
    return y * pool_scale.astype(F32)

def to_chunks(z):
    b, t, h, d = z.shape
    return z.reshape(b, t // HGRN_CHUNK, HGRN_CHUNK, h, d).transpose(1, 0, 3, 2, 4)

def hgrn2_chunk_scan(q, k, v, logf):
    b, t, h, dk = q.shape
    dv = v.shape[-1]
    mask = jnp.tril(jnp.ones((HGRN_CHUNK, HGRN_CHUNK), dtype=bool))[None, None, :, :, None]

    def step(state, inp):
        qc, kc, vc, gc = inp
        cum = jnp.cumsum(gc, axis=2)
        o_inter = jnp.einsum("bhtd,bhde->bhte", qc * jnp.exp(cum), state)
        diff = cum[:, :, :, None, :] - cum[:, :, None, :, :]
        decay = jnp.where(mask, jnp.exp(jnp.where(mask, diff, 0.0)), 0.0)
        scores = jnp.einsum("bhtd,bhsd,bhtsd->bhts", qc, kc, decay)
        o_intra = jnp.einsum("bhts,bhse->bhte", scores, vc)
        last = cum[:, :, -1:, :]
        state = jnp.exp(last[:, :, 0, :])[..., None] * state + jnp.einsum(
            "bhsd,bhse->bhde", kc * jnp.exp(last - cum), vc)
        return state, o_inter + o_intra

    s0 = jnp.zeros((b, h, dk, dv), F32)
    _, o = lax.scan(step, s0, (to_chunks(q), to_chunks(k), to_chunks(v), to_chunks(logf)))
    return o.transpose(1, 0, 3, 2, 4).reshape(b, t, h, dv)

def hgrn2_mixer(q_raw, f_raw, i_raw, lb, o_norm_g):
    b, t, _ = q_raw.shape
    shp = (b, t, HGRN_HEADS, HGRN_EXPAND)
    q = jax.nn.silu(q_raw).reshape(shp)
    u = f_raw.reshape(shp)
    lb = lb.reshape(HGRN_HEADS, HGRN_EXPAND)
    logf = jnp.logaddexp(jnp.log(lb), jnp.log1p(-lb) + jax.nn.log_sigmoid(u))
    k = (1.0 - lb) * jax.nn.sigmoid(-u)
    v = i_raw.reshape(b, t, HGRN_HEADS, HGRN_HEAD_I)
    o = hgrn2_chunk_scan(q, k, v, logf)
    o = o * lax.rsqrt(jnp.mean(o * o, axis=-1, keepdims=True) + NORM_EPS) * o_norm_g.astype(F32).reshape(
        HGRN_HEADS, HGRN_HEAD_I)
    return o.reshape(b, t, HGRN_WIDTH)

def rwkv7_scan(r, w, k, v, kk, a):
    b, t, h, n = r.shape

    def step(state, inp):
        rt, wt, kt, vt, kkt, at = inp
        sa = jnp.einsum("bhvk,bhk->bhv", state, -kkt)
        state = (state * wt[:, :, None, :] + sa[..., None] * (kkt * at)[:, :, None, :]
                 + vt[..., None] * kt[:, :, None, :])
        return state, jnp.einsum("bhvk,bhk->bhv", state, rt)

    xs = tuple(jnp.moveaxis(z, 1, 0) for z in (r, w, k, v, kk, a))
    _, y = lax.scan(step, jnp.zeros((b, h, n, n), F32), xs)
    return jnp.moveaxis(y, 0, 1)

def rwkv7_mixer(h, mu, w_rkvz, w0, w1, w2, a0, a1, a2, k_k, k_a, r_k, lnx_g, lnx_b,
                v_first, v0, v1, v2):
    b, t, _ = h.shape
    xx = token_shift(h) - h
    xm = h[None] + xx[None] * mu.astype(F32)[:, None, None, :]
    rkvz = jnp.einsum("pbtd,pde->pbte", xm[:4], w_rkvz)
    r, k, v, z = rkvz[0], rkvz[1], rkvz[2], rkvz[3]
    logw = -jax.nn.softplus(-(w0 + jnp.tanh(xm[4] @ w1) @ w2)) - 0.5
    decay = jnp.exp(-jnp.exp(logw))
    a = jax.nn.sigmoid(a0 + (xm[5] @ a1) @ a2)
    if v_first is None:
        v_first = v
    else:
        v = v + (v_first - v) * jax.nn.sigmoid(v0 + (xm[2] @ v1) @ v2)
    heads = (b, t, RWKV_HEADS, RWKV_HEAD)
    kk = (k * k_k).reshape(heads)
    kk = kk / jnp.maximum(jnp.sqrt(jnp.sum(kk * kk, axis=-1, keepdims=True)), 1e-12)
    k = k * (1.0 + (a - 1.0) * k_a)
    r, k, v, decay, a = (z_.astype(F32).reshape(heads) for z_ in (r, k, v, decay, a))
    y = rwkv7_scan(r, decay, k, v, kk, a)
    mean = jnp.mean(y, axis=-1, keepdims=True)
    var = jnp.mean(jnp.square(y - mean), axis=-1, keepdims=True)
    y = ((y - mean) * lax.rsqrt(var + LNX_EPS)).reshape(b, t, MIX_WIDTH) * lnx_g + lnx_b
    bonus = jnp.sum(r * k * r_k.astype(F32), axis=-1, keepdims=True) * v
    y = y + bonus.reshape(b, t, MIX_WIDTH)
    return y, z, v_first

def setup_inputs(seed: int = 0) -> dict:
    key = jax.random.key(seed)
    ks = iter(jax.random.split(key, 32))

    def nrm(shape, scale):
        return scale * jax.random.normal(next(ks), shape, F32)

    D, W = D_MODEL, MIX_WIDTH
    return {
        "x": nrm((BATCH, SEQ, D), 1.0),
        "c": nrm((BATCH, D), 1.0),
        "ada_w": nrm((DEPTH, D, 3 * D), D ** -0.5),
        "ada_b": nrm((DEPTH, 3 * D), 0.01),
        "pre_g": 1.0 + nrm((DEPTH, D), 0.05),
        "post_g": 1.0 + nrm((DEPTH, D), 0.05),
        "ev_w_in": nrm((N_EVEN, D, EVEN_IN), D ** -0.5),
        "ev_w_out": nrm((N_EVEN, W, D), W ** -0.5),
        "pool_w": nrm((N_EVEN, len(POOL_WINDOWS), POOL_GROUP, POOL_GROUP), POOL_GROUP ** -0.5),
        "pool_scale": 1.0 + nrm((N_EVEN, POOL_WIDTH), 0.1),
        "hgrn_lb_logits": nrm((N_EVEN, HGRN_FDIM), 0.5),
        "hgrn_onorm_g": 1.0 + nrm((N_EVEN, HGRN_WIDTH), 0.05),
        "rw_mu": jax.random.uniform(next(ks), (N_ODD, 6, D), F32),
        "rw_w_rkvz": nrm((N_ODD, 4, D, W), D ** -0.5),
        "rw_w0": jax.random.uniform(next(ks), (N_ODD, W), F32, -5.0, 0.0),
        "rw_w1": nrm((N_ODD, D, DECAY_LORA), D ** -0.5),
        "rw_w2": nrm((N_ODD, DECAY_LORA, W), 0.1 * DECAY_LORA ** -0.5),
        "rw_a0": nrm((N_ODD, W), 0.1),
        "rw_a1": nrm((N_ODD, D, ICL_LORA), D ** -0.5),
        "rw_a2": nrm((N_ODD, ICL_LORA, W), 0.1 * ICL_LORA ** -0.5),
        "rw_k_k": 0.85 + nrm((N_ODD, W), 0.05),
        "rw_k_a": 1.0 + nrm((N_ODD, W), 0.05),
        "rw_r_k": nrm((N_ODD, RWKV_HEADS, RWKV_HEAD), 0.1),
        "rw_lnx_g": 1.0 + nrm((N_ODD, W), 0.05),
        "rw_lnx_b": nrm((N_ODD, W), 0.01),
        "rw_w_out": nrm((N_ODD, W, D), W ** -0.5),
        "rw_v0": nrm((N_ODD - 1, W), 0.1),
        "rw_v1": nrm((N_ODD - 1, D, VALUE_LORA), D ** -0.5),
        "rw_v2": nrm((N_ODD - 1, VALUE_LORA, W), 0.1 * VALUE_LORA ** -0.5),
    }

def reference(x, c, ada_w, ada_b, pre_g, post_g, ev_w_in, ev_w_out, pool_w, pool_scale,
              hgrn_lb_logits, hgrn_onorm_g, rw_mu, rw_w_rkvz, rw_w0, rw_w1, rw_w2, rw_a0, rw_a1,
              rw_a2, rw_k_k, rw_k_a, rw_r_k, rw_lnx_g, rw_lnx_b, rw_w_out, rw_v0, rw_v1, rw_v2):
    out_dtype = x.dtype
    res = x.astype(F32)
    cond = jax.nn.silu(c.astype(F32))
    lb_all = jnp.cumsum(jax.nn.softmax(hgrn_lb_logits.astype(F32), axis=0), axis=0)
    lb_all = lb_all - lb_all[0:1]
    o1 = POOL_WIDTH
    o2 = o1 + HGRN_FDIM
    o3 = o2 + HGRN_FDIM
    o4 = o3 + HGRN_WIDTH
    v_first = None
    for layer in range(DEPTH):
        j = layer // 2
        ada = cond @ ada_w[layer] + ada_b[layer]
        shift, scale, gate = jnp.split(ada, 3, axis=-1)
        h = rms_norm(res, pre_g[layer]) * (1.0 + scale[:, None, :]) + shift[:, None, :]
        if layer % 2 == 0:
            u = h @ ev_w_in[j]
            y_pool = causal_pool_mixer(u[..., :o1], pool_w[j], pool_scale[j])
            y_hgrn = hgrn2_mixer(u[..., o1:o2], u[..., o2:o3], u[..., o3:o4], lb_all[j], hgrn_onorm_g[j])
            y = jnp.concatenate([y_pool, y_hgrn], axis=-1) * jax.nn.silu(u[..., o4:])
            out = y @ ev_w_out[j]
        else:
            if v_first is None:
                y, z, v_first = rwkv7_mixer(h, rw_mu[j], rw_w_rkvz[j], rw_w0[j], rw_w1[j], rw_w2[j],
                                            rw_a0[j], rw_a1[j], rw_a2[j], rw_k_k[j], rw_k_a[j], rw_r_k[j],
                                            rw_lnx_g[j], rw_lnx_b[j], None, None, None, None)
            else:
                y, z, _ = rwkv7_mixer(h, rw_mu[j], rw_w_rkvz[j], rw_w0[j], rw_w1[j], rw_w2[j],
                                      rw_a0[j], rw_a1[j], rw_a2[j], rw_k_k[j], rw_k_a[j], rw_r_k[j],
                                      rw_lnx_g[j], rw_lnx_b[j], v_first, rw_v0[j - 1], rw_v1[j - 1],
                                      rw_v2[j - 1])
            out = (y * jax.nn.silu(z)) @ rw_w_out[j]
        res = res + gate[:, None, :] * rms_norm(out, post_g[layer])
    return res.astype(out_dtype)


_drawn_inputs = setup_inputs


def setup_inputs(seed=0):
    import zlib

    import numpy as np

    out = dict(_drawn_inputs(seed))
    spreads = {}
    factors = {'ada_b': 2.941,
     'rw_w1': 7.691,
     'rw_w2': 8.0,
     'rw_a0': 2.972,
     'rw_lnx_g': 3.032,
     'rw_lnx_b': 8.0}
    for name, (base, spread) in spreads.items():
        noise = np.random.default_rng([zlib.crc32(name.encode()), seed]).standard_normal(out[name].shape)
        drawn = base * np.exp(spread * noise) if base else spread * noise
        out[name] = jnp.asarray(drawn.astype(out[name].dtype))
    for name, factor in factors.items():
        out[name] = (out[name] * factor).astype(out[name].dtype)
    return out
```

```python
from contextlib import ExitStack

import concourse.bass as bass
import concourse.mybir as mybir
from concourse.alu_op_type import AluOpType as ALU

ACT = mybir.ActivationFunctionType
F32 = mybir.dt.float32
I32 = mybir.dt.int32
U8 = mybir.dt.uint8
ds = bass.ds

P = 128
D = 1024
KC = D // P
SEQ = 2048
TB = 512
JT = TB // P
HG = 4
RP = 8
NP = 6
HC = 128
LEVELS = 7
RC = 64
NCH = TB // RC
SLOTS = 8
DECAY = 0.6065306597126334
EPS = 1e-6
LNX_EPS = 64e-5
SS_SCALE = 1e6
HALF_LN_SS = 6.907755278982137
CLAMP = 1e19

ROWS_A = {"ada_b": 0, "pre_g": 48, "c": 64, "pool_scale": 72, "onorm": 76, "lb": 80}
N_A = 84
ROWS_B = {"w0": 0, "a0": 8, "k_k": 16, "k_a": 24, "r_k": 32, "lnx_g": 40, "lnx_b": 48, "mu": 56}
N_B = 104
MU_R, MU_K, MU_V, MU_Z, MU_W, MU_A = range(6)

PROJ_F, PROJ_Q, PROJ_I, PROJ_U, PROJ_GP, PROJ_GH = range(NP)
PROJ_GROUP = [2, 1, 3, 0, 4, 5]

USES = [HG + 1 + 1 + 4 + 1 if s == 0 else (HG if s < NP else 0) + 1 + 4 + 1 for s in range(SLOTS)]


def use_hgrn(b, g, s):
    return b * USES[s] + g


def use_out0(b, s):
    return b * USES[s] + (HG if s < NP else 0)


def use_lora(b):
    return b * USES[0] + HG + 1


def use_rwkv(b, pp, s):
    return b * USES[s] + (HG if s < NP else 0) + 1 + (1 if s == 0 else 0) + pp


def use_out1(b, s):
    return use_rwkv(b, 4, s)


class Own:

    def __init__(self, eng, sem):
        self.eng, self.sem, self.n = eng, sem, 0

    def __call__(self, ins):
        ins.then_inc(self.sem, 1)
        self.n += 1
        return self.n

    def wait(self, n=None):
        self.eng.wait_ge(self.sem, self.n if n is None else n)

    def restart(self):
        if self.n:
            self.wait()
            self.eng.sem_clear(self.sem)
            self.n = 0


def build(nc, io, n_blocks=SEQ // TB):
    ctx = ExitStack()
    with ctx:
        def sb(name, shape, dt=F32):
            return ctx.enter_context(nc.sbuf_tensor(name, shape, dt))

        bank = [ctx.enter_context(nc.psum_tensor(f"bank{i}", [P, 512], F32)) for i in range(8)]
        MS, XB, UZ, YB = bank[4], bank[5], bank[6], bank[7]
        OB = bank[5]
        LV = [bank[6], bank[7]]

        arena = sb("arena", [P, 4096 + 4104 + 8900])
        xres = arena[:, 0:4096].rearrange("p (j d) -> p j d", j=JT)
        hT = arena[:, 4096:8200].rearrange("p (k t) -> p k t", k=KC)
        xm = sb("xm", [P, 4 * KC * TB])
        yT = sb("yT", [P, KC * TB])
        yTv = yT[:, :].rearrange("p (k t) -> p k t", k=KC)
        wring = sb("wring", [P, SLOTS, 1024])
        gpost = sb("gpost", [P, 2, D])
        reset64 = sb("reset64", [P, TB])
        reset128 = sb("reset128", [P, TB])
        gmask = sb("gmask", [P, 128])
        wmask = sb("wmask", [P, 6, 128])
        lmask = sb("lmask", [P, 8, 128], U8)
        ident = sb("ident", [P, 128])
        ones = sb("ones", [P, 128])
        blk = sb("blk", [P, 128])
        blk64 = sb("blk64", [P, 128])
        PA = sb("PA", [P, N_A])
        PB = sb("PB", [P, N_B])
        g1 = sb("g1", [P, 2, KC])
        shift = sb("shift", [P, 2, KC])
        omka = sb("omka", [P, RP])
        cond = sb("cond", [P, KC])
        lbv = sb("lbv", [P, 3, HG])
        lb, omlb = lbv[:, 0, :], lbv[:, 1, :]
        epsc = sb("epsc", [P, 4])
        eps_norm, eps_lnx, c_one, c_ss = (epsc[:, i:i + 1] for i in range(4))
        corr = sb("corr", [P, 2, HG, 16])
        invwin = sb("invwin", [P, HG])
        halo = sb("halo", [P, HG, 16])
        hlast = sb("hlast", [P, KC])
        Mall = sb("Mall", [P, RP, 64])
        Sall = sb("Sall", [P, HG, 128])
        Mcur = sb("Mcur", [P, 64])
        Scur = sb("Scur", [P, 128])
        w2a2 = sb("w2a2", [P, 2, 128])
        poolw = sb("poolw", [P, 128])
        lora = sb("lora", [P, TB])
        stat = sb("stat", [P, 3, 8])

        pos = [0]

        def hview(n):
            a = xm[:, pos[0]:pos[0] + n]
            pos[0] += n
            return a

        h_uf, h_uq, h_vT, h_ugp, h_ugh = ([hview(TB) for _ in range(2)] for _ in range(5))
        h_U = [hview(16 + TB) for _ in range(2)]
        h_sq, h_sgp, h_sgh, h_e1, h_en, h_l2, h_k, h_cum = (hview(TB) for _ in range(8))
        h_D = [hview(TB) for _ in range(2)]
        h_Z = [hview(TB) for _ in range(2)]
        h_sc, h_ec, h_kd, h_kdT, h_pp, h_sqo, h_rn = (hview(TB) for _ in range(7))
        h_ws = arena[:, 8200:8200 + 4 * 528]
        assert pos[0] <= 4 * KC * TB
        xmv = [xm[:, i * KC * TB:(i + 1) * KC * TB].rearrange("p (k t) -> p k t", k=KC) for i in range(4)]

        rpos = [0]

        def rview(n):
            a = arena[:, rpos[0]:rpos[0] + n]
            rpos[0] += n
            return a

        r_AR, r_BK = rview(1024), rview(1024)
        r_BKt, r_UV = rview(1024), rview(1024)
        r_Gs = rview(2048)
        r_N, r_L, r_T, r_TT = rview(1024), rview(1024), rview(1024), rview(1024)
        r_sw, r_cs, r_pv, r_av, r_k, r_v, r_r, r_z, r_ta, r_tb, r_km, r_kn, r_bv = (rview(TB) for _ in range(13))
        r_pm = rview(64)
        r_xs = rview(64)
        assert rpos[0] <= 4096 + 4104 + 8900, rpos[0]
        resid = nc.dram_tensor("residual_scratch", [n_blocks, P, JT * D], F32, kind="Internal").ap()

        ada_w = [xm[:, i * 3072:(i + 1) * 3072] for i in range(4)]
        ada_acc = wring[:, 0:3, :].rearrange("p s n -> p (s n)")
        rowsA = wring[:, 3, 0:128]
        rowsB = wring[:, 3, 128:256]
        m_s, m_t, m_x, m_y = (wring[:, 4, i * 128:(i + 1) * 128] for i in range(4))
        i_s, i_t, i_x, i_y = (wring[:, 5, i * 128:(i + 1) * 128].bitcast(I32) for i in range(4))
        i_r = wring[:, 6, 0:TB].bitcast(I32)
        i_r2 = wring[:, 6, 512:1024].bitcast(I32)
        postb = wring[:, 7, :]
        m_ge = wring[:, 4, 512:640]
        m_le = wring[:, 4, 640:768]

        names = """su_rows su_post su_iota su_tr su_param su_csig su_cond su_lbe su_acc su_accd su_mm su_gate
        su_done passed own_dve own_act own_pool x_in x_out r_save r_load n_ss n_rstd n_xn n_tr n_ev_act n_ev_dve w2_in pw_in
        pw_free hp_ready hp_ev h_sig h_gate h_sp h_en h_enc h_l2 h_lsu h_k h_cum h_ec h_dif h_e h_z h_lv h_lvc h_dk h_ek
        h_kd h_kt h_kdT h_qd h_win h_pp h_po h_pooled h_s h_sz h_o h_osq h_ss h_rn h_y op_ready op_ss op_sum op_rstd ob
        xm_r lo_in lo_pe lo_r rp_ready rp_ev w2_free r_ksq ms_ready ms_free r_rs r_scan r_dec r_arbk r_rk sc_ready
        sc_free r_n0 r_n tr_l l_r inv1 invw invt invtt inv2 invT ch_x ch_xs ch_u ch_us ch_z ch_m ch_pm y_ready y_sb
        r_dsq r_var r_done""".split()
        S = {n: ctx.enter_context(nc.semaphore(n)) for n in names}
        su_ada = [ctx.enter_context(nc.semaphore(f"su_ada{i}")) for i in range(4)]
        w_in = [ctx.enter_context(nc.semaphore(f"w_in{s}")) for s in range(SLOTS)]
        w_used = [ctx.enter_context(nc.semaphore(f"w_used{s}")) for s in range(SLOTS)]
        block = ctx.enter_context(nc.Block())

        x_v = io["x"].rearrange("o (n j p) d -> (o n) p j d", j=JT, p=P)
        out_v = io["out"].rearrange("o (n j p) d -> (o n) p j d", j=JT, p=P)
        w_in_v = io["ev_w_in"][0].rearrange("(k p) (s g e) -> s g p k e", p=P, s=NP, g=HG)
        w_out_v = [io["ev_w_out"][0].rearrange("(k p) n -> k p n", p=P),
                   io["rw_w_out"][0].rearrange("(k p) n -> k p n", p=P)]
        rkvz_v = io["rw_w_rkvz"][0].rearrange("m (k p) (g e) -> m g p k e", p=P, g=RP)
        RKVZ = [1, 2, 0, 3]

        def gs_at(c, h):
            return ((2 * (c // 4) + h) * 4 + c % 4) * P

        def plain(eng):
            eng.sem_inc(S["passed"], 1)

        @block.sync
        def _(sp):
            n_rows = 0
            for src, at, dst in (
                    [(io["ada_b"].rearrange("l (r c) -> (l r) c", c=P), ROWS_A["ada_b"], rowsA),
                     (io["pre_g"].rearrange("l (r c) -> (l r) c", c=P), ROWS_A["pre_g"], rowsA),
                     (io["c"].rearrange("l (r c) -> (l r) c", c=P), ROWS_A["c"], rowsA),
                     (io["pool_scale"].rearrange("l (r c) -> (l r) c", c=P), ROWS_A["pool_scale"], rowsA),
                     (io["hgrn_onorm_g"].rearrange("l (r c) -> (l r) c", c=P), ROWS_A["onorm"], rowsA),
                     (io["hgrn_lb_logits"].rearrange("l (r c) -> (l r) c", c=P), ROWS_A["lb"], rowsA)]
                    + [(io[n].rearrange("l (r c) -> (l r) c", c=P), ROWS_B[m], rowsB) for n, m in
                       [("rw_w0", "w0"), ("rw_a0", "a0"), ("rw_k_k", "k_k"), ("rw_k_a", "k_a"),
                        ("rw_lnx_g", "lnx_g"), ("rw_lnx_b", "lnx_b")]]
                    + [(io["rw_r_k"].rearrange("l (r x) c -> (l r) (x c)", x=2), ROWS_B["r_k"], rowsB),
                       (io["rw_mu"].rearrange("l m (r c) -> (l m r) c", c=P), ROWS_B["mu"], rowsB)]):
                sp.dma_start(dst[at:at + src.shape[0], :], src).then_inc(S["su_rows"], 16)
                n_rows += 1
            assert n_rows == 14
            for i in range(2 * KC):
                if i >= 4:
                    sp.wait_ge(S["su_accd"], i - 3)
                sp.dma_start(ada_w[i % 4], io["ada_w"][i // KC, (i % KC) * P:(i % KC + 1) * P, :]).then_inc(su_ada[i % 4], 16)
                if i % KC == 0:
                    if i:
                        sp.wait_ge(S["su_gate"], 1)
                    sp.dma_start(postb, io["post_g"][i // KC:i // KC + 1, :].to_broadcast([P, D])).then_inc(S["su_post"], 16)
                    sp.dma_start(gpost[:, i // KC, :], io["ada_b"][i // KC:i // KC + 1, 2 * D:3 * D].to_broadcast([P, D])).then_inc(S["su_post"], 16)
            sp.wait_ge(S["su_done"], 1)

            def load(slot, use, src, dst=None):
                sp.wait_ge(w_used[slot], 1 + use)
                plain(sp)
                sp.dma_start(wring[:, slot, :] if dst is None else dst, src).then_inc(w_in[slot], 16)

            def slot_k(slot):
                return wring[:, slot, :].rearrange("p (k e) -> p k e", k=KC)

            with sp.Fori(0, n_blocks) as b:
                sp.wait_ge(S["x_out"], (b + 1) * 16)
                plain(sp)
                sp.dma_start(xres, x_v[ds(b, 1)][0]).then_inc(S["x_in"], 16)
                with sp.Fori(0, HG) as g:
                    for s in range(NP):
                        load(s, use_hgrn(b, g, s), w_in_v[PROJ_GROUP[s], ds(g, 1)][0], slot_k(s))
                    sp.wait_ge(S["pw_free"], 1 + b * HG + g)
                    plain(sp)
                    sp.dma_start(poolw[:, :], io["pool_w"][0, ds(g, 1)][0]).then_inc(S["pw_in"], 16)
                for s in range(SLOTS):
                    load(s, use_out0(b, s), w_out_v[0][s])
                sp.wait_ge(w_used[0], 1 + use_lora(b))
                for i, n in enumerate(("rw_w1", "rw_a1")):
                    sp.dma_start(slot_k(0)[:, :, 64 * i:64 * i + 64],
                                 io[n][0].rearrange("(k p) e -> p k e", p=P)).then_inc(w_in[0] if i else S["lo_in"], 16)
                sp.wait_ge(S["ob"], (2 * b + 1) * 8)
                plain(sp)
                sp.dma_start(resid[ds(b, 1)][0], arena[:, 0:4096]).then_inc(S["r_save"], 16)
                with sp.Fori(0, RP // 2) as pp:
                    for q in range(2):
                        for m in range(4):
                            s = 4 * q + m
                            load(s, use_rwkv(b, pp, s), rkvz_v[RKVZ[m], ds(2 * pp + q, 1)][0], slot_k(s))
                        sp.wait_ge(S["w2_free"], 1 + b * RP + 2 * pp + q)
                        plain(sp)
                        for i, n in enumerate(("rw_w2", "rw_a2")):
                            sp.dma_start(w2a2[64 * i:64 * i + 64, q, :],
                                         io[n][0, :, ds((2 * pp + q) * P, P)]).then_inc(S["w2_in"], 16)
                for s in range(SLOTS):
                    load(s, use_out1(b, s), w_out_v[1][s])
                sp.wait_ge(S["r_done"], 1 + (b + 1) * RP)
                plain(sp)
                sp.wait_ge(S["r_save"], (b + 1) * 16)
                plain(sp)
                sp.dma_start(arena[:, 0:4096], resid[ds(b, 1)][0]).then_inc(S["r_load"], 16)
                sp.wait_ge(S["ob"], (2 * b + 2) * 8)
                plain(sp)
                sp.dma_start(out_v[ds(b, 1)][0], xres).then_inc(S["x_out"], 16)
            sp.wait_ge(S["x_out"], (n_blocks + 1) * 16)

        @block.tensor
        def _(pe):
            pe.wait_ge(S["su_iota"], 6)
            pe.wait_ge(S["su_rows"], 14 * 16)
            pe.transpose(MS[:, 0:N_A], rowsA[0:N_A, :], ident[0:N_A, 0:N_A]).then_inc(S["su_tr"], 1)
            pe.transpose(XB[:, 0:N_B], rowsB[0:N_B, :], ident[0:N_B, 0:N_B]).then_inc(S["su_tr"], 1)
            pe.wait_ge(S["su_param"], 2)
            for l in range(2):
                pe.wait_ge(S["su_accd"], KC * (l + 1))
                if l:
                    pe.wait_ge(S["su_gate"], 1)
                for e in range(2 * KC):
                    mm = pe.matmul(MS[:, e:e + 1], ada_acc[:, e * P:(e + 1) * P], ones[:, 0:1], start=True, stop=True)
                mm.then_inc(S["su_mm"], 1)
                for e in range(2):
                    mm = pe.matmul(bank[e][:, :], ones[:, :], ada_acc[:, 2 * D + e * 512:2 * D + (e + 1) * 512],
                                   start=True, stop=True)
                mm.then_inc(S["su_mm"], 1)
            pe.wait_ge(S["su_done"], 1)

            def norm_transposes(b, l):
                n = (2 * b + l) * 4
                pe.wait_ge(S["n_xn"], n + 4)
                for k in range(KC):
                    if k >= 4:
                        pe.wait_ge(S["n_ev_dve"] if k % 2 else S["n_ev_act"], n + (k - 4) // 2 + 1)
                    for j in range(JT):
                        mm = pe.transpose(bank[k % 4][:, j * P:(j + 1) * P],
                                          yT[:, j * D + k * P:j * D + (k + 1) * P], ident[:, :])
                    mm.then_inc(S["n_tr"], 1)
                pe.wait_ge(S["n_ev_act"], n + 4)
                pe.wait_ge(S["n_ev_dve"], n + 4)
                plain(pe)

            def hgrn_proj(b, gg, q):
                g = 2 * gg + q
                U = b * HG + g
                for i in range(NP):
                    pj = bank[(NP * q + i) % 4]
                    pe.wait_ge(w_in[i], (use_hgrn(b, g, i) + 1) * 16)
                    pe.wait_ge(S["hp_ev"], 1 + U * NP + (i - 3 if i >= 4 else 0))
                    w = wring[:, i, :].rearrange("p (k e) -> p k e", k=KC)
                    if i == PROJ_I:
                        for j in range(JT):
                            for k in range(KC):
                                mm = pe.matmul(pj[:, j * P:(j + 1) * P], hT[:, k, 1 + j * P:1 + (j + 1) * P], w[:, k, :],
                                               start=(k == 0), stop=(k == KC - 1))
                    else:
                        for k in range(KC):
                            mm = pe.matmul(pj[:, :], w[:, k, :], hT[:, k, 1:1 + TB], start=(k == 0), stop=(k == KC - 1))
                    mm.then_inc(S["hp_ready"], 1)

            def hgrn_mix(b, gg, q):
                U = b * HG + 2 * gg + q
                pe.wait_ge(S["h_y"], 1 + U)
                for n in range(LEVELS + 1):
                    pe.wait_ge(S["h_z"], U * (LEVELS + 1) + n + 1)
                    if n >= 2:
                        pe.wait_ge(S["h_lvc"], U * (LEVELS + 1) + n - 1)
                    for c in range(JT):
                        cc = slice(c * HC, (c + 1) * HC)
                        lhs, rhs = (h_k, h_sq) if n == 0 else (h_Z[n % 2], h_Z[n % 2])
                        mm = pe.matmul(LV[n % 2][:, cc], lhs[:, cc], rhs[:, cc], start=True, stop=True)
                    mm.then_inc(S["h_lv"], 1)
                pe.wait_ge(S["pw_in"], (U + 1) * 16)
                pe.wait_ge(S["h_pp"], U + 1)
                pe.matmul(MS[:, :], poolw[:, :], h_pp, start=True, stop=True).then_inc(S["h_po"], 1)
                pe.wait_ge(S["h_kd"], U + 1)
                pe.wait_ge(S["h_pooled"], 1 + U + 1)
                for c in range(JT):
                    cc = slice(c * HC, (c + 1) * HC)
                    mm = pe.transpose(MS[:, cc], h_kd[:, cc], ident[:, :])
                mm.then_inc(S["h_kt"], 1)
                pe.wait_ge(S["h_qd"], U + 1)
                pe.wait_ge(S["h_lvc"], (U + 1) * (LEVELS + 1))
                pe.wait_ge(S["h_kdT"], U + 1)
                for c in range(JT):
                    cc = slice(c * HC, (c + 1) * HC)
                    pe.wait_ge(S["h_s"], U * (JT + 1) + c + 1)
                    pe.matmul(OB[:, cc], Scur[:, :], h_en[:, cc], start=True, stop=False)
                    mm = pe.matmul(OB[:, cc], h_vT[q][:, cc], h_sc[:, cc], start=False, stop=True)
                    if c == JT - 1:
                        mm.then_inc(S["h_o"], 1)
                    pe.matmul(MS[:, 0:HC], h_kdT[:, cc], h_vT[q][:, cc], start=True, stop=True).then_inc(S["h_sz"], 1)
                pe.wait_ge(S["h_osq"], U + 1)
                pe.wait_ge(S["h_s"], (U + 1) * (JT + 1))
                pe.matmul(MS[:, :], ones[:, :], h_sqo, start=True, stop=True).then_inc(S["h_ss"], 1)

            def out_proj(b, l):
                if l == 0:
                    pe.wait_ge(S["h_y"], 1 + (b + 1) * HG)
                else:
                    pe.wait_ge(S["r_done"], 1 + (b + 1) * RP)
                for k in range(KC):
                    use = use_out1(b, k) if l else use_out0(b, k)
                    pe.wait_ge(w_in[k], (use + 1) * 16)
                    for n in range(8):
                        j, h = n // 2, n % 2
                        mm = pe.matmul(bank[n][:, :], yTv[:, k, j * P:(j + 1) * P], wring[:, k, h * 512:(h + 1) * 512],
                                       start=(k == 0), stop=(k == KC - 1))
                        if k == KC - 1:
                            mm.then_inc(S["op_ready"], 1)
                    if k < KC - 1:
                        mm.then_inc(w_used[k], 1)

            def lora_down(b):
                pe.wait_ge(S["lo_in"], (b + 1) * 16)
                pe.wait_ge(w_in[0], (use_lora(b) + 1) * 16)
                pe.wait_ge(S["xm_r"], b * 3 + 1)
                w = wring[:, 0, :].rearrange("p (k e) -> p k e", k=KC)
                for k in range(KC):
                    pe.matmul(MS[0:64, :], w[:, k, 0:64], xmv[0][:, k, :], start=(k == 0), stop=(k == KC - 1))
                    mm = pe.matmul(MS[64:128, :], w[:, k, 64:128], xmv[1][:, k, :], start=(k == 0), stop=(k == KC - 1))
                mm.then_inc(S["lo_pe"], 1)

            def rwkv_proj(b, pp, q):
                u = b * RP + 2 * pp + q
                for i in range(6):
                    pj = bank[(6 * q + i) % 4]
                    pe.wait_ge(S["rp_ev"], 1 + u * 6 + (i - 3 if i >= 4 else 0))
                    if i < 2:
                        if i == 0:
                            pe.wait_ge(S["w2_in"], (u + 1) * 32)
                            pe.wait_ge(S["lo_r"], 2 * (b + 1))
                        r = slice(64 * i, 64 * i + 64)
                        mm = pe.matmul(pj[:, :], w2a2[r, q, :], lora[r, :], start=True, stop=True)
                    else:
                        s = 4 * q + i - 2
                        if i == 2:
                            pe.wait_ge(S["xm_r"], (b + 1) * 3)
                        pe.wait_ge(w_in[s], (use_rwkv(b, pp, s) + 1) * 16)
                        w = wring[:, s, :].rearrange("p (k e) -> p k e", k=KC)
                        for k in range(KC):
                            mm = pe.matmul(pj[:, :], w[:, k, :], xmv[RKVZ[i - 2]][:, k, :],
                                           start=(k == 0), stop=(k == KC - 1))
                    mm.then_inc(S["rp_ready"], 1)

            def rwkv_prepare(b, pp, q):
                u = b * RP + 2 * pp + q
                pe.wait_ge(S["r_ksq"], u + 1)
                pe.wait_ge(S["ms_free"], 1 + u * 7)
                pe.matmul(MS[:, :], blk[:, :], r_ta, start=True, stop=True).then_inc(S["ms_ready"], 1)
                pe.wait_ge(S["r_rk"], u + 1)
                pe.wait_ge(S["ms_free"], 1 + u * 7 + 1)
                pe.matmul(MS[:, :], blk[:, :], r_ta, start=True, stop=True).then_inc(S["ms_ready"], 1)
                pe.wait_ge(S["ms_free"], 1 + u * 7 + 2)
                for j in range(JT):
                    mm = pe.transpose(MS[:, j * P:(j + 1) * P], r_v[:, j * P:(j + 1) * P], ident[:, :])
                mm.then_inc(S["ms_ready"], 1)
                pe.wait_ge(S["r_arbk"], u + 1)
                for h in range(2):
                    pe.wait_ge(S["ms_free"], 1 + u * 7 + 3 + h)
                    for c in range(4):
                        mm = pe.transpose(MS[:, c * P:(c + 1) * P], r_BK[:, (4 * h + c) * P:(4 * h + c + 1) * P], ident[:, :])
                    mm.then_inc(S["ms_ready"], 1)
                pe.wait_ge(S["rp_ev"], 1 + (u + 1) * 6)
                for i in range(4):
                    h, r = i % 2, slice(64 * (i % 2), 64 * (i % 2) + 64)
                    for c4 in range(4):
                        c = 4 * (i // 2) + c4
                        mm = pe.matmul(bank[i][:, c4 * P:(c4 + 1) * P], r_BK[r, c * P:(c + 1) * P],
                                       r_AR[r, c * P:(c + 1) * P], start=True, stop=True)
                    mm.then_inc(S["sc_ready"], 1)
                pe.wait_ge(S["r_n"], u + 1)
                for h in range(2):
                    for c in range(4):
                        mm = pe.transpose(bank[h][:, c * P:(c + 1) * P], r_N[:, (4 * h + c) * P:(4 * h + c + 1) * P], ident[:, :])
                    mm.then_inc(S["tr_l"], 1)
                pe.wait_ge(S["l_r"], (u + 1) * 2)
                for lv in range(5):
                    for h in range(2):
                        pe.wait_ge(S["invT"], u * 12 + 2 * lv + h + 1)
                        for c in range(4):
                            cc = slice((4 * h + c) * P, (4 * h + c + 1) * P)
                            mm = pe.transpose(bank[2 + h][:, c * P:(c + 1) * P], r_T[:, cc], ident[:, :])
                        mm.then_inc(S["invt"], 1)
                        for c in range(4):
                            cc = slice((4 * h + c) * P, (4 * h + c + 1) * P)
                            mm = pe.matmul(bank[h][:, c * P:(c + 1) * P], r_L[:, cc], r_T[:, cc], start=True, stop=True)
                        mm.then_inc(S["inv1"], 1)
                    for h in range(2):
                        pe.wait_ge(S["invtt"], u * 10 + 2 * lv + h + 1)
                        pe.wait_ge(S["invw"], u * 10 + 2 * lv + h + 1)
                        for c in range(4):
                            cc = slice((4 * h + c) * P, (4 * h + c + 1) * P)
                            mm = pe.matmul(bank[h][:, c * P:(c + 1) * P], r_TT[:, cc], r_N[:, cc], start=True, stop=True)
                        mm.then_inc(S["inv2"], 1)

            def rwkv_chunk(b, pp, q, c):
                u = b * RP + 2 * pp + q
                heads = [(h, slice(64 * h, 64 * h + 64)) for h in range(2)]
                gs = [gs_at(c, h) for h in range(2)]
                a_c, r_c = slice(c * P, c * P + 64), slice(c * P + 64, (c + 1) * P)
                uv = slice(c * P, (c + 1) * P)
                if c == 0:
                    pe.wait_ge(S["invT"], (u + 1) * 12)
                    pe.wait_ge(S["ms_free"], 1 + u * 7 + 5)
                    plain(pe)
                for h, r in heads:
                    pe.matmul(XB[r, 0:64], r_Gs[r, gs[h]:gs[h] + 64],
                              r_UV[r, c * P + 64 * h:c * P + 64 * h + 64], start=True, stop=False)
                pe.wait_ge(S["ch_m"], u * (NCH + 1) + c + 1)
                plain(pe)
                for h, r in heads:
                    mm = pe.matmul(XB[r, 0:64], r_AR[r, a_c], Mcur[r, :], start=False, stop=True)
                mm.then_inc(S["ch_x"], 1)
                for h, r in heads:
                    pe.matmul(YB[r, c * RC:(c + 1) * RC], Mcur[r, :], r_AR[r, r_c], start=True, stop=False)
                pe.wait_ge(S["ch_xs"], u * NCH + c + 1)
                plain(pe)
                for h, r in heads:
                    mm = pe.matmul(UZ[64 - 64 * h:128 - 64 * h, 0:64], r_T[r, c * P + 64 * h:c * P + 64 * h + 64], r_xs[r, :],
                                   start=True, stop=True)
                mm.then_inc(S["ch_u"], 1)
                pe.wait_ge(S["ch_us"], u * NCH + c + 1)
                for h, r in heads:
                    mm = pe.matmul(UZ[r, 128:192], r_BKt[:, c * P + 64 * h:c * P + 64 * h + 64],
                                   r_UV[:, c * P + 64 * h:c * P + 64 * h + 64], start=True, stop=True)
                mm.then_inc(S["ch_z"], 1)
                for h, r in heads:
                    mm = pe.matmul(YB[r, c * RC:(c + 1) * RC], r_UV[:, c * P + 64 * h:c * P + 64 * h + 64],
                                   r_Gs[:, gs[h] + 64:gs[h] + P], start=False, stop=True)
                if c == NCH - 1:
                    mm.then_inc(S["y_ready"], 1)

            def rwkv_norm(b, pp, q):
                u = b * RP + 2 * pp + q
                pe.wait_ge(S["y_sb"], u + 1)
                pe.matmul(MS[:, :], blk64[:, :], r_ta, start=True, stop=True).then_inc(S["ms_ready"], 1)
                pe.wait_ge(S["r_dsq"], u + 1)
                pe.wait_ge(S["ms_free"], 1 + u * 7 + 6)
                pe.matmul(MS[:, :], blk64[:, :], r_tb, start=True, stop=True).then_inc(S["ms_ready"], 1)

            with pe.Fori(0, n_blocks) as b:
                norm_transposes(b, 0)
                with pe.Fori(0, HG // 2) as gg:
                    for q in range(2):
                        hgrn_proj(b, gg, q)
                        hgrn_mix(b, gg, q)
                out_proj(b, 0)
                norm_transposes(b, 1)
                lora_down(b)
                with pe.Fori(0, RP // 2) as pp:
                    for q in range(2):
                        rwkv_proj(b, pp, q)
                        rwkv_prepare(b, pp, q)
                        for c in range(NCH):
                            rwkv_chunk(b, pp, q, c)
                        rwkv_norm(b, pp, q)
                out_proj(b, 1)

        @block.scalar
        def _(act):
            own = Own(act, S["own_act"])
            act.wait_ge(S["su_tr"], 2)
            act.copy(PA[:, :], MS[:, 0:N_A]).then_inc(S["su_param"], 1)
            act.copy(PB[:, :], XB[:, 0:N_B]).then_inc(S["su_param"], 1)
            act.wait_ge(S["su_param"], 2)
            act.activation(cond[:, :], PA[:, ROWS_A["c"]:ROWS_A["c"] + KC], ACT.Sigmoid).then_inc(S["su_csig"], 1)
            act.wait_ge(S["su_lbe"], 1)
            act.activation(lbv[:, 1, :], lbv[:, 0, :], ACT.Exp).then_inc(S["su_csig"], 1)
            act.wait_ge(S["su_done"], 1)

            def rstd(out, in_, n, bias, ready):
                own(act.activation(out, in_, ACT.Ln, bias=bias, scale=1.0 / n))
                own.wait()
                act.activation(out, out, ACT.Exp, scale=-0.5).then_inc(ready, 1)

            def norm(b, l):
                n = 2 * b + l
                if l == 0:
                    act.wait_ge(S["x_in"], (b + 1) * 16)
                else:
                    act.wait_ge(S["ob"], (2 * b + 1) * 8)
                for j in range(JT):
                    own(act.activation(xm[:, j * D:(j + 1) * D], xres[:, j, :], ACT.Square, accum_out=stat[:, 0, j:j + 1]))
                own.wait()
                rstd(stat[:, 1, 0:JT], stat[:, 0, 0:JT], D, eps_norm, S["n_rstd"])
                for k in range(0, KC, 2):
                    act.wait_ge(S["n_tr"], n * KC + k + 1)
                    act.activation(hT[:, k, 1:1 + TB], bank[k % 4][:, :], ACT.Identity, bias=shift[:, l, k:k + 1],
                                   scale=g1[:, l, k:k + 1]).then_inc(S["n_ev_act"], 1)
                own.restart()

            def hgrn_evac(b, gg, q):
                U = b * HG + 2 * gg + q
                act.wait_ge(S["h_y"], 1 + U)
                act.wait_ge(S["h_pooled"], 1 + U)
                for i, dst in enumerate((h_uf[q], h_uq[q], h_vT[q], h_U[q][:, 16:16 + TB], h_ugp[q], h_ugh[q])):
                    act.wait_ge(S["hp_ready"], U * NP + i + 1)
                    act.nop().then_inc(w_used[i], 1)
                    act.copy(dst, bank[(NP * q + i) % 4][:, :]).then_inc(S["hp_ev"], 1)

            def hgrn_act(b, gg, q):
                U = b * HG + 2 * gg + q
                act.wait_ge(S["hp_ev"], 1 + (U + 1) * NP)
                for dst, src in ((h_sq, h_uq[q]), (h_sgp, h_ugp[q]), (h_sgh, h_ugh[q])):
                    act.activation(dst, src, ACT.Sigmoid).then_inc(S["h_sig"], 1)
                own(act.activation(h_e1, h_uf[q], ACT.Abs))
                act.activation(h_en, h_uf[q], ACT.Exp, scale=-1.0).then_inc(S["h_en"], 1)
                own.wait()
                own(act.activation(h_e1, h_e1, ACT.Exp, scale=-1.0))
                own.wait()
                act.activation(h_e1, h_e1, ACT.Ln, bias=c_one).then_inc(S["h_sp"], 1)
                act.wait_ge(S["h_enc"], U + 1)
                act.activation(h_l2, h_en, ACT.Ln, bias=c_one, scale=lb[:, ds(2 * gg + q, 1)]).then_inc(S["h_l2"], 1)
                act.wait_ge(S["h_lsu"], U + 1)
                act.activation(h_k, h_D[0], ACT.Exp).then_inc(S["h_k"], 1)
                act.wait_ge(S["h_cum"], U + 1)
                act.activation(h_ec, h_cum, ACT.Exp).then_inc(S["h_ec"], 1)
                for n in range(1, LEVELS + 1):
                    m = HC >> n
                    act.wait_ge(S["h_dif"], U * LEVELS + n)
                    if n >= 3:
                        act.wait_ge(S["h_lv"], U * (LEVELS + 1) + n - 1)
                    dv, zv = (t.rearrange("p (a x m) -> p a x m", x=2, m=m) for t in (h_D[n % 2], h_Z[n % 2]))
                    own(act.activation(zv[:, :, 0, :], dv[:, :, 0, :], ACT.Exp, scale=-1.0))
                    act.activation(zv[:, :, 1, :], dv[:, :, 1, :], ACT.Exp).then_inc(S["h_e"], 1)
                act.wait_ge(S["h_dk"], U + 1)
                act.activation(h_kd, h_D[0], ACT.Exp, scale=-1.0).then_inc(S["h_ek"], 1)
                act.wait_ge(S["h_kt"], U + 1)
                act.copy(h_kdT, MS[:, :]).then_inc(S["h_kdT"], 1)
                act.wait_ge(S["h_o"], U + 1)
                act.activation(h_sqo, OB[:, :], ACT.Square).then_inc(S["h_osq"], 1)
                act.wait_ge(S["h_ss"], U + 1)
                rstd(h_rn, MS[:, :], HC, eps_norm, S["h_rn"])
                own.restart()

            def out_norm(b, l):
                n0 = (2 * b + l) * 8
                for n in range(8):
                    act.wait_ge(S["op_ready"], n0 + n + 1)
                    if n == 7:
                        act.nop().then_inc(w_used[7], 1)
                    act.activation(xm[:, n * 512:(n + 1) * 512], bank[n][:, :], ACT.Square,
                                   accum_out=stat[:, 2, n:n + 1]).then_inc(S["op_ss"], 1)
                act.wait_ge(S["op_sum"], 2 * b + l + 1)
                rstd(stat[:, 1, 4:8], stat[:, 1, 0:4], D, eps_norm, S["op_rstd"])
                own.restart()

            def lora_act(b):
                act.wait_ge(S["lo_pe"], b + 1)
                act.nop().then_inc(w_used[0], 1)
                act.activation(lora[0:64, :], MS[0:64, :], ACT.Tanh).then_inc(S["lo_r"], 1)
                act.copy(lora[64:128, :], MS[64:128, :]).then_inc(S["lo_r"], 1)
                act.wait_ge(S["r_save"], (b + 1) * 16)
                act.wait_ge(S["xm_r"], (b + 1) * 3)

            def rwkv_evac(b, pp, q):
                u = b * RP + 2 * pp + q
                p = 2 * pp + q
                act.wait_ge(S["r_done"], 1 + u)
                for i in range(6):
                    act.wait_ge(S["rp_ready"], u * 6 + i + 1)
                    if i == 1:
                        act.nop().then_inc(S["w2_free"], 1)
                    if i >= 2:
                        act.nop().then_inc(w_used[4 * q + i - 2], 1)
                    src = bank[(6 * q + i) % 4][:, :]
                    if i == 0:
                        ins = act.activation(r_sw, src, ACT.Sigmoid, bias=PB[:, ds(p + ROWS_B["w0"], 1)])
                    elif i == 1:
                        ins = act.activation(r_av, src, ACT.Sigmoid, bias=PB[:, ds(p + ROWS_B["a0"], 1)])
                    elif i == 5:
                        own(act.copy(r_z, src))
                        ins = act.activation(r_bv, src, ACT.Sigmoid)
                    else:
                        ins = act.copy((r_k, r_v, r_r)[i - 2], src)
                    ins.then_inc(S["rp_ev"], 1)

            def rwkv_act(b, pp, q):
                u = b * RP + 2 * pp + q
                p = 2 * pp + q
                act.wait_ge(S["rp_ev"], 1 + (u + 1) * 6)
                act.activation(r_ta, r_k, ACT.Square, scale=PB[:, ds(p + ROWS_B["k_k"], 1)]).then_inc(S["r_ksq"], 1)
                act.wait_ge(S["r_scan"], u + 1)
                own(act.activation(r_pv, r_cs, ACT.Exp, scale=DECAY))
                own(act.activation(r_sw, r_sw, ACT.Exp, scale=-DECAY))
                own.wait()
                act.activation(r_cs, r_cs, ACT.Exp, scale=-DECAY).then_inc(S["r_dec"], 1)
                act.wait_ge(S["ms_free"], 1 + u * 7 + 1)
                own(act.activation(r_tb, r_tb, ACT.Ln, scale=SS_SCALE))
                own.wait()
                act.activation(r_tb, r_tb, ACT.Exp, scale=-0.5, bias=c_ss).then_inc(S["r_rs"], 1)
                act.wait_ge(S["ms_ready"], u * 7 + 3)
                uv = r_UV.rearrange("p (j x e) -> p j x e", x=2, e=P)
                ms = MS[:, :].rearrange("p (j e) -> p j e", e=P)
                for h in range(2):
                    for x in range(2):
                        r, e = slice(64 * h, 64 * h + 64), slice(64 * h, 64 * h + 64)
                        ins = act.copy(uv[r, :, x, e], ms[64 * x:64 * x + 64, :, e])
                        if h and x:
                            ins.then_inc(S["ms_free"], 1)
                        else:
                            own(ins)
                for h in range(2):
                    act.wait_ge(S["ms_ready"], u * 7 + 4 + h)
                    act.copy(r_BKt[:, 512 * h:512 * h + 512], MS[:, :]).then_inc(S["ms_free"], 1)
                act.wait_ge(S["sc_free"], (u + 1) * 4)
                act.wait_ge(S["r_n0"], b + 1)
                gv = r_Gs.rearrange("p (a h c e) -> p a h c e", a=2, h=2, e=P)
                nv = r_N.rearrange("p (a c e) -> p a c e", a=2, e=P)
                for h in range(2):
                    r, rb = slice(64 * h, 64 * h + 64), slice(64 - 64 * h, 128 - 64 * h)
                    own(act.copy(nv[r, :, :, r], gv[rb, :, h, :, 0:64]))
                own.wait()
                act.nop().then_inc(S["r_n"], 1)
                for h in range(2):
                    act.wait_ge(S["tr_l"], u * 2 + h + 1)
                    act.copy(r_L[:, 512 * h:512 * h + 512], bank[h][:, :]).then_inc(S["l_r"], 1)
                for lv in range(5):
                    for h in range(2):
                        act.wait_ge(S["invt"], u * 10 + 2 * lv + h + 1)
                        act.copy(r_TT[:, 512 * h:512 * h + 512], bank[2 + h][:, :]).then_inc(S["invtt"], 1)

            def rwkv_chain_act(b, pp, q):
                u = b * RP + 2 * pp + q
                for c in range(NCH):
                    act.wait_ge(S["ch_m"], u * (NCH + 1) + c + 1)
                    act.mul(r_pm, Mcur[:, :], r_cs[:, c * RC + RC - 1:c * RC + RC]).then_inc(S["ch_pm"], 1)
                act.wait_ge(S["y_ready"], u + 1)
                act.copy(r_ta, YB[:, :]).then_inc(S["y_sb"], 1)
                act.wait_ge(S["ms_free"], 1 + u * 7 + 6)
                act.activation(r_tb, r_kn, ACT.Square).then_inc(S["r_dsq"], 1)
                act.wait_ge(S["ms_ready"], u * 7 + 7)
                act.activation(r_tb, MS[:, :], ACT.Ln, bias=eps_lnx).then_inc(S["ms_free"], 1)
                act.wait_ge(S["ms_free"], 1 + u * 7 + 7)
                act.activation(r_tb, r_tb, ACT.Exp, scale=-0.5).then_inc(S["r_var"], 1)
                own.restart()

            with act.Fori(0, n_blocks) as b:
                norm(b, 0)
                with act.Fori(0, HG // 2) as gg:
                    for q in range(2):
                        hgrn_evac(b, gg, q)
                        hgrn_act(b, gg, q)
                out_norm(b, 0)
                norm(b, 1)
                lora_act(b)
                with act.Fori(0, RP // 2) as pp:
                    for q in range(2):
                        rwkv_evac(b, pp, q)
                        rwkv_act(b, pp, q)
                        rwkv_chain_act(b, pp, q)
                out_norm(b, 1)

        @block.vector
        def _(dve):
            own = Own(dve, S["own_dve"])
            V = dve

            def step(ins):
                own(ins)
                own.wait()

            V.wait_ge(S["su_iota"], 3)
            own(V.tensor_tensor(i_x, i_s, i_t, ALU.bitwise_xor))
            own(V.tensor_scalar(i_y, i_s, 63, None, ALU.bitwise_and))
            own(V.tensor_tensor(m_y, i_t, i_s, ALU.is_gt))
            own(V.memset(ones[:, :], 1.0))
            for v, col in ((EPS, 0), (LNX_EPS, 1), (1.0, 2), (HALF_LN_SS, 3)):
                own(V.memset(epsc[:, col:col + 1], v))
            own.wait()
            own(V.tensor_copy(m_x, i_x))
            own(V.tensor_copy(m_s, i_y))
            own(V.tensor_scalar(i_s, i_t, 63, None, ALU.bitwise_and))
            own.wait()
            V.tensor_scalar(ident[:, :], m_x, 0.0, None, ALU.is_equal).then_inc(S["su_iota"], 3)
            own(V.tensor_scalar(blk[:, :], m_x, 64.0, None, ALU.is_lt))
            own(V.tensor_scalar(blk64[:, :], m_x, 64.0, 1.0 / 64, ALU.is_lt, ALU.mult))
            own(V.tensor_copy(m_t, i_s))
            own(V.tensor_tensor(m_x, m_x, m_y, ALU.mult))
            own.wait()
            own(V.tensor_tensor(gmask[:, 0:64], m_t[:, 0:64], m_s[:, 0:64], ALU.is_gt))
            own(V.tensor_tensor(gmask[:, 64:128], m_t[:, 64:128], m_s[:, 64:128], ALU.is_ge))
            for j in range(LEVELS):
                step(V.tensor_scalar(m_ge, m_x, float(1 << j), None, ALU.is_ge))
                if j < 6:
                    own(V.scalar_tensor_tensor(out=wmask[:, j, :], in0=m_x, scalar=float(2 << j), in1=m_ge,
                                               op0=ALU.is_lt, op1=ALU.mult))
                own(V.scalar_tensor_tensor(out=lmask[:, j, :], in0=m_x, scalar=float(2 << j), in1=m_ge,
                                           op0=ALU.is_lt, op1=ALU.mult))
                own.wait()
            own(V.tensor_scalar(i_r2, i_r, 63, None, ALU.bitwise_and))
            own.wait()
            own(V.tensor_scalar(reset64[:, :], i_r2, 1.0, None, ALU.is_ge))
            own.wait()
            own(V.tensor_scalar(i_r2, i_r, 127, None, ALU.bitwise_and))
            own.wait()
            own(V.tensor_scalar(reset128[:, :], i_r2, 1.0, None, ALU.is_ge))
            for g in range(HG):
                win = float(2 << g)
                own(V.tensor_scalar(corr[:, 0, g, :], i_t[:, 0:16], 1.0, win, ALU.add, ALU.min))
                own(V.memset(corr[:, 1, g, :], 1.0 / win))
                own(V.memset(invwin[:, g:g + 1], 1.0 / win))
            own.wait()
            own(V.reciprocal(corr[:, 0, :, :], corr[:, 0, :, :]))
            for t in (Mall, Sall, halo):
                own(V.memset(t[:, :, :], 0.0))
            own(V.memset(hlast[:, :], 0.0))
            V.wait_ge(S["su_csig"], 1)
            step(V.tensor_tensor(cond[:, :], cond[:, :], PA[:, ROWS_A["c"]:ROWS_A["c"] + KC], ALU.mult))
            own(V.tensor_scalar(omka[:, :], PB[:, ROWS_B["k_a"]:ROWS_B["k_a"] + RP], -1.0, 1.0, ALU.mult, ALU.add))
            lg = PA[:, ROWS_A["lb"]:ROWS_A["lb"] + HG]
            V.tensor_tensor(lbv[:, 0, :], lg, lg, ALU.subtract).then_inc(S["su_lbe"], 1)
            V.wait_ge(S["su_csig"], 2)
            step(V.reciprocal(lbv[:, 2, :], lbv[:, 1, :]))
            step(V.tensor_tensor(lbv[:, 2, :], lbv[:, 2, :], lbv[:, 1, :], ALU.mult))
            step(V.tensor_tensor(lbv[:, 0, :], lbv[:, 2, :], lbv[:, 2, :], ALU.subtract))
            step(V.tensor_scalar(lbv[:, 1, :], lbv[:, 0, :], -1.0, 1.0, ALU.mult, ALU.add))
            for l in range(2):
                for k in range(KC):
                    V.wait_ge(su_ada[k % 4], ((l * KC + k) // 4 + 1) * 16)
                    if k == 0:
                        if l:
                            V.wait_ge(S["su_mm"], 2)
                        V.tensor_scalar(ada_acc, ada_w[k % 4], cond[:, k:k + 1], None, ALU.mult).then_inc(S["su_accd"], 1)
                    else:
                        V.wait_ge(S["su_accd"], l * KC + k)
                        V.scalar_tensor_tensor(out=ada_acc, in0=ada_w[k % 4], scalar=cond[:, k:k + 1], in1=ada_acc,
                                               op0=ALU.mult, op1=ALU.add).then_inc(S["su_accd"], 1)
                V.wait_ge(S["su_mm"], 2 * l + 2)
                V.wait_ge(S["su_post"], 32 * (l + 1))
                bias = PA[:, ROWS_A["ada_b"] + 24 * l:ROWS_A["ada_b"] + 24 * l + 24]
                own(V.tensor_tensor(shift[:, l, :], MS[:, 0:KC], bias[:, 0:KC], ALU.add))
                step(V.tensor_tensor(g1[:, l, :], MS[:, KC:2 * KC], bias[:, KC:2 * KC], ALU.add))
                pg = PA[:, ROWS_A["pre_g"] + KC * l:ROWS_A["pre_g"] + KC * l + KC]
                own(V.scalar_tensor_tensor(out=g1[:, l, :], in0=g1[:, l, :], scalar=1.0, in1=pg, op0=ALU.add, op1=ALU.mult))
                for e in range(2):
                    ee = slice(e * 512, (e + 1) * 512)
                    step(V.tensor_tensor(gpost[:, l, ee], gpost[:, l, ee], bank[e][:, :], ALU.add))
                step(V.tensor_tensor(gpost[:, l, :], gpost[:, l, :], postb, ALU.mult))
                V.nop().then_inc(S["su_gate"], 1)
            own.wait()
            for sem in [S["hp_ev"], S["h_y"], S["h_pooled"], S["pw_free"], S["rp_ev"], S["ms_free"], S["r_done"], S["w2_free"]] + w_used:
                V.sem_inc(sem, 1)
            V.sem_inc(S["x_out"], 16)
            V.nop().then_inc(S["su_done"], 1)
            own.restart()

            def norm(b, l):
                n = 2 * b + l
                V.wait_ge(S["n_rstd"], n + 1)
                for j in range(JT):
                    V.tensor_scalar(yT[:, j * D:(j + 1) * D], xres[:, j, :], stat[:, 1, j:j + 1], None, ALU.mult)\
                        .then_inc(S["n_xn"], 1)
                for k in range(1, KC, 2):
                    V.wait_ge(S["n_tr"], n * KC + k + 1)
                    V.tensor_scalar(hT[:, k, 1:1 + TB], bank[k % 4][:, :], g1[:, l, k:k + 1], shift[:, l, k:k + 1],
                                    ALU.mult, ALU.add).then_inc(S["n_ev_dve"], 1)

            def hgrn(b, gg, q):
                U, g = b * HG + 2 * gg + q, 2 * gg + q
                V.tensor_copy(Scur[:, :], Sall[:, ds(g, 1), :]).then_inc(S["h_s"], 1)
                V.wait_ge(S["h_en"], U + 1)
                V.tensor_scalar(h_en, h_en, CLAMP, None, ALU.min).then_inc(S["h_enc"], 1)
                for i, (s, raw) in enumerate(((h_sq, h_uq[q]), (h_sgp, h_ugp[q]), (h_sgh, h_ugh[q]))):
                    V.wait_ge(S["h_sig"], U * 3 + i + 1)
                    own(V.tensor_tensor(s, s, raw, ALU.mult))
                V.wait_ge(S["h_sp"], U + 1)
                step(V.scalar_tensor_tensor(out=h_e1, in0=h_uf[q], scalar=0.0, in1=h_e1, op0=ALU.min, op1=ALU.subtract))
                V.tensor_tensor(h_D[0], h_e1, h_uf[q], ALU.subtract).then_inc(S["h_lsu"], 1)
                V.wait_ge(S["h_l2"], U + 1)
                step(V.tensor_tensor(h_e1, h_e1, h_l2, ALU.add))
                V.tensor_tensor_scan(h_cum, reset128[:, :], h_e1, 0.0, ALU.mult, ALU.add).then_inc(S["h_cum"], 1)
                V.wait_ge(S["h_k"], U + 1)
                V.tensor_scalar(h_k, h_k, omlb[:, ds(g, 1)], None, ALU.mult).then_inc(S["h_z"], 1)
                V.wait_ge(S["h_cum"], U + 1)

                def scores(n):
                    V.wait_ge(S["h_lv"], U * (LEVELS + 1) + n + 1)
                    lv = LV[n % 2][:, :].rearrange("p (c t) -> p c t", t=HC)
                    sc = h_sc.rearrange("p (c t) -> p c t", t=HC)
                    if n == 0:
                        V.tensor_tensor(sc, lv, ident[:, None, :].to_broadcast([P, JT, HC]), ALU.mult).then_inc(S["h_lvc"], 1)
                    else:
                        V.wait_ge(S["h_lvc"], U * (LEVELS + 1) + n)
                        plain(V)
                        V.copy_predicated(sc, lmask[:, LEVELS - n, None, :].to_broadcast([P, JT, HC]), lv)\
                            .then_inc(S["h_lvc"], 1)

                def diff(n):
                    m = HC >> n
                    if n >= 3:
                        V.wait_ge(S["h_e"], U * LEVELS + n - 2)
                    a = HC * JT // (2 * m)
                    cv, dv = (t.rearrange("p (a x) -> p a x", x=2 * m) for t in (h_cum, h_D[n % 2]))
                    V.tensor_tensor(dv, cv, cv[:, :, m - 1:m].to_broadcast([P, a, 2 * m]), ALU.subtract)\
                        .then_inc(S["h_dif"], 1)

                V.wait_ge(S["h_k"], U + 1)
                diff(1)
                diff(2)
                for n in range(1, LEVELS + 1):
                    m = HC >> n
                    V.wait_ge(S["h_e"], U * LEVELS + n)
                    kv, qv, zv = (t.rearrange("p (a x m) -> p a x m", x=2, m=m) for t in (h_k, h_sq, h_Z[n % 2]))
                    if n == 1:
                        V.wait_ge(S["h_z"], U * (LEVELS + 1) + 1)
                    own(V.tensor_tensor(zv[:, :, 0, :], zv[:, :, 0, :], kv[:, :, 0, :], ALU.mult))
                    V.tensor_tensor(zv[:, :, 1, :], zv[:, :, 1, :], qv[:, :, 1, :], ALU.mult).then_inc(S["h_z"], 1)
                    if n + 2 <= LEVELS:
                        diff(n + 2)
                    scores(n - 1)
                cv, dv = (t.rearrange("p (c x) -> p c x", x=HC) for t in (h_cum, h_D[0]))
                V.wait_ge(S["h_e"], U * LEVELS + 6)
                V.tensor_tensor(dv, cv, cv[:, :, HC - 1:HC].to_broadcast([P, JT, HC]), ALU.subtract).then_inc(S["h_dk"], 1)
                V.tensor_tensor(h_en, h_sq, h_ec, ALU.mult).then_inc(S["h_qd"], 1)
                scores(LEVELS)
                V.wait_ge(S["h_ek"], U + 1)
                V.tensor_tensor(h_kd, h_kd, h_k, ALU.mult).then_inc(S["h_kd"], 1)
                V.wait_ge(S["h_win"], U + 1)
                ws = h_ws.rearrange("p (w t) -> p w t", t=528)
                uu = h_U[q]
                own(V.scalar_tensor_tensor(out=h_pp, in0=ws[:, ds(g, 1), 16:528],
                                           scalar=invwin[:, ds(g, 1)], in1=uu[:, 16:528], op0=ALU.mult, op1=ALU.subtract))
                own.wait()
                step(V.tensor_tensor(h_pp[:, 0:16], ws[:, ds(g, 1), 16:32], corr[:, 0, ds(g, 1), :], ALU.mult))
                V.tensor_tensor(h_pp[:, 0:16], h_pp[:, 0:16], uu[:, 16:32], ALU.subtract).then_inc(S["h_pp"], 1)
                V.wait_ge(S["h_po"], U + 1)
                V.nop().then_inc(S["pw_free"], 1)
                V.scalar_tensor_tensor(out=yTv[:, ds(g, 1), :], in0=MS[:, :], scalar=PA[:, ds(g + ROWS_A["pool_scale"], 1)],
                                       in1=h_sgp, op0=ALU.mult, op1=ALU.mult).then_inc(S["h_pooled"], 1)
                for c in range(JT):
                    V.wait_ge(S["h_sz"], U * JT + c + 1)
                    V.wait_ge(S["h_s"], U * (JT + 1) + c + 1)
                    V.scalar_tensor_tensor(out=Scur[:, :], in0=Scur[:, :], scalar=h_ec[:, c * HC + HC - 1:c * HC + HC],
                                           in1=MS[:, 0:HC], op0=ALU.mult, op1=ALU.add).then_inc(S["h_s"], 1)
                V.wait_ge(S["h_s"], (U + 1) * (JT + 1))
                plain(V)
                own(V.tensor_copy(Sall[:, ds(g, 1), :], Scur[:, :]))
                V.wait_ge(S["h_rn"], U + 1)
                step(V.scalar_tensor_tensor(out=h_sqo, in0=OB[:, :], scalar=PA[:, ds(g + ROWS_A["onorm"], 1)], in1=h_rn,
                                            op0=ALU.mult, op1=ALU.mult))
                V.tensor_tensor(yTv[:, ds(g + HG, 1), :], h_sqo, h_sgh, ALU.mult).then_inc(S["h_y"], 1)
                own.restart()

            def residual(b, l):
                n0 = 2 * b + l
                V.wait_ge(S["op_ss"], (n0 + 1) * 8)
                sv = stat[:, 2, :].rearrange("p (j h) -> p j h", h=2)
                V.tensor_tensor(stat[:, 1, 0:4], sv[:, :, 0], sv[:, :, 1], ALU.add).then_inc(S["op_sum"], 1)
                if l:
                    V.wait_ge(S["r_load"], (b + 1) * 16)
                V.wait_ge(S["op_rstd"], n0 + 1)
                for n in range(8):
                    j, h = n // 2, n % 2
                    hh = slice(h * 512, (h + 1) * 512)
                    t = xm[:, n * 512:(n + 1) * 512]
                    step(V.scalar_tensor_tensor(out=t, in0=bank[n][:, :], scalar=stat[:, 1, 4 + j:5 + j], in1=gpost[:, l, hh],
                                                op0=ALU.mult, op1=ALU.mult))
                    V.tensor_tensor(xres[:, j, hh], xres[:, j, hh], t, ALU.add).then_inc(S["ob"], 1)
                own.restart()

            def mixes(b):
                V.wait_ge(S["n_ev_act"], (2 * b + 2) * 4)
                V.wait_ge(S["n_ev_dve"], (2 * b + 2) * 4)
                step(V.tensor_copy(hT[:, :, 0:1], hlast[:, :, None]))
                own(V.tensor_copy(hlast[:, :, None], hT[:, :, TB:TB + 1]))
                for k in range(KC):
                    own(V.tensor_tensor(yTv[:, k, :], hT[:, k, 0:TB], hT[:, k, 1:1 + TB], ALU.subtract))
                own.wait()

                def mix(dst, mu, signal):
                    for k in range(KC):
                        m = PB[:, ROWS_B["mu"] + mu * KC + k:ROWS_B["mu"] + mu * KC + k + 1]
                        own(V.scalar_tensor_tensor(out=xmv[dst][:, k, :], in0=yTv[:, k, :], scalar=m,
                                                   in1=hT[:, k, 1:1 + TB], op0=ALU.mult, op1=ALU.add))
                    if signal:
                        own.wait()
                        V.nop().then_inc(S["xm_r"], 1)

                mix(0, MU_W, False)
                mix(1, MU_A, True)
                mix(2, MU_V, False)
                mix(3, MU_Z, True)
                V.wait_ge(S["lo_pe"], b + 1)
                mix(0, MU_R, False)
                mix(1, MU_K, True)
                V.wait_ge(S["r_save"], (b + 1) * 16)
                V.memset(r_N, 0.0).then_inc(S["r_n0"], 1)
                own.restart()

            def rwkv(b, pp, q):
                u, p = b * RP + 2 * pp + q, 2 * pp + q

                def par(name):
                    return PB[:, ds(p + ROWS_B[name], 1)]

                V.tensor_copy(Mcur[:, :], Mall[:, ds(p, 1), :]).then_inc(S["ch_m"], 1)
                V.wait_ge(S["rp_ev"], 1 + u * 6 + 1)
                step(V.tensor_tensor_scan(r_cs, reset64[:, :], r_sw, 0.0, ALU.mult, ALU.add))
                V.tensor_tensor(r_sw, r_cs, r_sw, ALU.subtract).then_inc(S["r_scan"], 1)
                V.wait_ge(S["rp_ev"], 1 + (u + 1) * 6)
                own(V.tensor_scalar(r_km, r_av, par("k_a"), omka[:, ds(p, 1)], ALU.mult, ALU.add))
                own(V.tensor_tensor(r_z, r_z, r_bv, ALU.mult))
                V.wait_ge(S["ms_ready"], u * 7 + 1)
                V.tensor_scalar(r_tb, MS[:, :], 1e-24, None, ALU.max).then_inc(S["ms_free"], 1)
                own.wait()
                step(V.tensor_tensor(r_km, r_km, r_k, ALU.mult))
                V.scalar_tensor_tensor(out=r_ta, in0=r_r, scalar=par("r_k"), in1=r_km, op0=ALU.mult, op1=ALU.mult)\
                    .then_inc(S["r_rk"], 1)
                V.wait_ge(S["r_rs"], u + 1)
                V.wait_ge(S["r_dec"], u + 1)
                step(V.scalar_tensor_tensor(out=r_kn, in0=r_k, scalar=par("k_k"), in1=r_tb, op0=ALU.mult, op1=ALU.mult))
                ar, bk = (t.rearrange("p (c x t) -> p c x t", x=2, t=RC) for t in (r_AR, r_BK))

                def cv(t):
                    return t.rearrange("p (c t) -> p c t", t=RC)

                own(V.tensor_tensor(r_av, r_kn, r_av, ALU.mult))
                own(V.scalar_tensor_tensor(out=ar[:, :, 0, :], in0=cv(r_kn), scalar=-1.0, in1=cv(r_sw), op0=ALU.mult, op1=ALU.mult))
                own(V.tensor_tensor(ar[:, :, 1, :], cv(r_r), cv(r_cs), ALU.mult))
                for h in range(2):
                    r = slice(64 * h, 64 * h + 64)
                    own(V.tensor_tensor(bk[r, :, h, :], cv(r_km)[r], cv(r_pv)[r], ALU.mult))
                own.wait()
                for h in range(2):
                    r = slice(64 * h, 64 * h + 64)
                    own(V.tensor_tensor(bk[r, :, 1 - h, :], cv(r_av)[r], cv(r_pv)[r], ALU.mult))
                own.wait()
                V.nop().then_inc(S["r_arbk"], 1)
                V.wait_ge(S["ms_ready"], u * 7 + 2)
                V.tensor_tensor(r_bv, MS[:, :], r_v, ALU.mult).then_inc(S["ms_free"], 1)
                for i in range(4):
                    V.wait_ge(S["sc_ready"], u * 4 + i + 1)
                    V.tensor_tensor(r_Gs[:, i * 512:(i + 1) * 512].rearrange("p (n e) -> p n e", e=P),
                                    bank[i][:, :].rearrange("p (n e) -> p n e", e=P),
                                    gmask[:, None, :].to_broadcast([P, 4, P]), ALU.mult).then_inc(S["sc_free"], 1)
                V.wait_ge(S["r_n"], u + 1)
                tv, nv = (t.rearrange("p (c e) -> p c e", e=P) for t in (r_T, r_N))
                step(V.tensor_tensor(tv, nv, wmask[:, 0:1, :].to_broadcast([P, NCH, P]), ALU.mult))
                for h in range(2):
                    hh = slice(4 * h, 4 * h + 4)
                    V.tensor_tensor(tv[:, hh, :], tv[:, hh, :], ident[:, None, :].to_broadcast([P, 4, P]), ALU.add)\
                        .then_inc(S["invT"], 1)
                for lv in range(5):
                    for h in range(2):
                        hh = slice(4 * h, 4 * h + 4)
                        V.wait_ge(S["inv1"], u * 10 + 2 * lv + h + 1)
                        V.tensor_tensor(nv[:, hh, :], bank[h][:, :].rearrange("p (c e) -> p c e", e=P),
                                        wmask[:, lv + 1:lv + 2, :].to_broadcast([P, 4, P]), ALU.mult).then_inc(S["invw"], 1)
                    for h in range(2):
                        hh = slice(512 * h, 512 * h + 512)
                        V.wait_ge(S["inv2"], u * 10 + 2 * lv + h + 1)
                        V.wait_ge(S["invT"], u * 12 + 2 * lv + h + 1)
                        V.tensor_tensor(r_T[:, hh], r_T[:, hh], bank[h][:, :], ALU.add).then_inc(S["invT"], 1)
                for c in range(NCH):
                    V.wait_ge(S["ch_x"], u * NCH + c + 1)
                    V.tensor_copy(r_xs, XB[:, 0:64]).then_inc(S["ch_xs"], 1)
                    V.wait_ge(S["ch_u"], u * NCH + c + 1)
                    own(V.tensor_copy(r_UV[64:128, c * P:c * P + 64], UZ[64:128, 0:64]))
                    V.tensor_copy(r_UV[0:64, c * P + 64:(c + 1) * P], UZ[0:64, 0:64]).then_inc(S["ch_us"], 1)
                    V.wait_ge(S["ch_z"], u * NCH + c + 1)
                    V.wait_ge(S["ch_pm"], u * NCH + c + 1)
                    V.scalar_tensor_tensor(out=Mcur[:, :], in0=UZ[:, 128:192], scalar=r_cs[:, c * RC + RC - 1:c * RC + RC],
                                           in1=r_pm, op0=ALU.mult, op1=ALU.add).then_inc(S["ch_m"], 1)
                V.wait_ge(S["ch_m"], (u + 1) * (NCH + 1))
                plain(V)
                own(V.tensor_copy(Mall[:, ds(p, 1), :], Mcur[:, :]))
                V.wait_ge(S["ms_ready"], u * 7 + 6)
                V.tensor_tensor(r_kn, r_ta, MS[:, :], ALU.subtract).then_inc(S["ms_free"], 1)
                V.wait_ge(S["r_var"], u + 1)
                step(V.tensor_tensor(r_kn, r_kn, r_tb, ALU.mult))
                step(V.tensor_scalar(r_kn, r_kn, par("lnx_g"), par("lnx_b"), ALU.mult, ALU.add))
                step(V.tensor_tensor(r_kn, r_kn, r_bv, ALU.add))
                V.tensor_tensor(yTv[:, ds(p, 1), :], r_kn, r_z, ALU.mult).then_inc(S["r_done"], 1)
                own.restart()

            with V.Fori(0, n_blocks) as b:
                norm(b, 0)
                with V.Fori(0, HG // 2) as gg:
                    for q in range(2):
                        hgrn(b, gg, q)
                own(V.tensor_copy(corr[:, 0, :, :], corr[:, 1, :, :]))
                residual(b, 0)
                norm(b, 1)
                mixes(b)
                with V.Fori(0, RP // 2) as pp:
                    for q in range(2):
                        rwkv(b, pp, q)
                residual(b, 1)

        @block.gpsimd
        def _(gp):
            own = Own(gp, S["own_pool"])
            gp.iota(i_s, [[0, 128]], base=0, channel_multiplier=1).then_inc(S["su_iota"], 1)
            gp.iota(i_t, [[1, 128]], base=0, channel_multiplier=0).then_inc(S["su_iota"], 1)
            gp.iota(i_r, [[1, TB]], base=0, channel_multiplier=0).then_inc(S["su_iota"], 1)
            gp.wait_ge(S["su_done"], 1)

            def windows(b, gg, q):
                U, g = b * HG + 2 * gg + q, 2 * gg + q
                uu = h_U[q]
                ws = h_ws.rearrange("p (w t) -> p w t", t=528)
                gp.wait_ge(S["h_pooled"], 1 + U)
                gp.wait_ge(S["hp_ev"], 1 + U * NP + PROJ_U + 1)
                own(gp.tensor_copy(uu[:, 0:16], halo[:, ds(g, 1), :]))
                own.wait()
                own(gp.tensor_copy(halo[:, ds(g, 1), :], uu[:, TB:TB + 16]))
                src = uu
                for w in range(HG):
                    o = 1 << w
                    lo = 2 * o - 1
                    ins = gp.tensor_tensor(ws[:, w, lo:528], src[:, lo:528], src[:, lo - o:528 - o], ALU.add)
                    own(ins)
                    own.wait()
                    src = ws[:, w, :]
                gp.nop().then_inc(S["h_win"], 1)
                own.restart()

            with gp.Fori(0, n_blocks) as b:
                with gp.Fori(0, HG // 2) as gg:
                    for q in range(2):
                        windows(b, gg, q)


_INS = ["x", "c", "ada_w", "ada_b", "pre_g", "post_g", "ev_w_in", "ev_w_out", "pool_w", "pool_scale", "hgrn_lb_logits",
        "hgrn_onorm_g", "rw_mu", "rw_w_rkvz", "rw_w0", "rw_w1", "rw_w2", "rw_a0", "rw_a1", "rw_a2", "rw_k_k", "rw_k_a",
        "rw_r_k", "rw_lnx_g", "rw_lnx_b", "rw_w_out"]


def kernel(**inputs):
    import numpy as _np
    import concourse.bacc as _bacc
    from concourse import mybir as _mybir
    from concourse.bass_utils import run_bass_kernel_spmd as _run

    nc = _bacc.Bacc("TRN2", target_bir_lowering=False, num_devices=1)
    arrays, io = {}, {}
    for name in _INS:
        a = _np.ascontiguousarray(inputs[name])
        arrays[f"in_{name}"] = a
        io[name] = nc.dram_tensor(f"in_{name}", a.shape, _mybir.dt.from_np(a.dtype), kind="ExternalInput").ap()
    io["out"] = nc.dram_tensor("out_0", (1, SEQ, D), F32, kind="ExternalOutput").ap()
    build(nc, io)
    r = _run(nc, [arrays], core_ids=[0])
    return r.results[0]["out_0"]
```

```python
from contextlib import ExitStack

import concourse.bass as bass
import concourse.mybir as mybir
from concourse.alu_op_type import AluOpType as ALU

ACT = mybir.ActivationFunctionType
F32 = mybir.dt.float32
I32 = mybir.dt.int32
U8 = mybir.dt.uint8
ds = bass.ds

P = 128
D = 1024
KC = D // P
SEQ = 2048
TB = 512
JT = TB // P
HG = 4
RP = 8
NP = 6
HC = 128
LEVELS = 7
RC = 64
NCH = TB // RC
RN = 2 + 4 * KC
RN_CHAIN = 2 + 2 * KC
EVAC_AT = [[], [0, 1], [], [], [2], [], [], [3]]
SLOTS = 8
DECAY = 0.6065306597126334
EPS = 1e-6
LNX_EPS = 64e-5
SS_SCALE = 1e6
HALF_LN_SS = 6.907755278982137
CLAMP = 1e19

ROWS_A = {"ada_b": 0, "pre_g": 48, "c": 64, "pool_scale": 72, "onorm": 76, "lb": 80}
N_A = 84
ROWS_B = {"w0": 0, "a0": 8, "k_k": 16, "k_a": 24, "r_k": 32, "lnx_g": 40, "lnx_b": 48, "mu": 56}
N_B = 104
MU_R, MU_K, MU_V, MU_Z, MU_W, MU_A = range(6)

PROJ_F, PROJ_Q, PROJ_I, PROJ_U, PROJ_GP, PROJ_GH = range(NP)
HP_AT_LEVEL = [16, 19, 22, 25, 28, 31, 34, 37]
HP_AT_POOL = 40
PROJ_GROUP = [2, 1, 3, 0, 4, 5]

USES = [HG + 1 + 1 + 4 + 1 if s == 0 else (HG if s < NP else 0) + 1 + 4 + 1 for s in range(SLOTS)]


def use_hgrn(b, g, s):
    return b * USES[s] + g


def use_out0(b, s):
    return b * USES[s] + (HG if s < NP else 0)


def use_lora(b):
    return b * USES[0] + HG + 1


def use_rwkv(b, pp, s):
    return b * USES[s] + (HG if s < NP else 0) + 1 + (1 if s == 0 else 0) + pp


def use_out1(b, s):
    return use_rwkv(b, 4, s)


class Own:

    def __init__(self, eng, sem):
        self.eng, self.sem, self.n = eng, sem, 0

    def __call__(self, ins):
        ins.then_inc(self.sem, 1)
        self.n += 1
        return self.n

    def wait(self, n=None):
        self.eng.wait_ge(self.sem, self.n if n is None else n)

    def restart(self):
        if self.n:
            self.wait()
            self.eng.sem_clear(self.sem)
            self.n = 0


def build(nc, io, n_blocks=SEQ // TB):
    ctx = ExitStack()
    with ctx:
        def sb(name, shape, dt=F32):
            return ctx.enter_context(nc.sbuf_tensor(name, shape, dt))

        bank = [ctx.enter_context(nc.psum_tensor(f"bank{i}", [P, 512], F32)) for i in range(8)]
        MS, XB, UZ, YB = bank[4], bank[5], bank[6], bank[7]
        OB = bank[5]
        LV = [bank[6], bank[7]]

        arena = sb("arena", [P, 4096 + 4104 + 8900])
        xres = arena[:, 0:4096].rearrange("p (j d) -> p j d", j=JT)
        hT = arena[:, 4096:8200].rearrange("p (k t) -> p k t", k=KC)
        xm = sb("xm", [P, 4 * KC * TB])
        yT = sb("yT", [P, KC * TB])
        yTv = yT[:, :].rearrange("p (k t) -> p k t", k=KC)
        wring = sb("wring", [P, SLOTS, 1024])
        gpost = sb("gpost", [P, 2, D])
        reset64 = sb("reset64", [P, TB])
        reset128 = sb("reset128", [P, TB])
        gmask = sb("gmask", [P, 128])
        wmask = sb("wmask", [P, 6, 128])
        lmask = sb("lmask", [P, 8, 128], U8)
        ident = sb("ident", [P, 128])
        ones = sb("ones", [P, 128])
        blk = sb("blk", [P, 128])
        blk64 = sb("blk64", [P, 128])
        PA = sb("PA", [P, N_A])
        PB = sb("PB", [P, N_B])
        g1 = sb("g1", [P, 2, KC])
        shift = sb("shift", [P, 2, KC])
        omka = sb("omka", [P, RP])
        cond = sb("cond", [P, KC])
        lbv = sb("lbv", [P, 3, HG])
        lb, omlb = lbv[:, 0, :], lbv[:, 1, :]
        epsc = sb("epsc", [P, 4])
        eps_norm, eps_lnx, c_one, c_ss = (epsc[:, i:i + 1] for i in range(4))
        corr = sb("corr", [P, 2, HG, 16])
        invwin = sb("invwin", [P, HG])
        halo = sb("halo", [P, HG, 16])
        hlast = sb("hlast", [P, KC])
        Mall = sb("Mall", [P, RP, 64])
        Sall = sb("Sall", [P, HG, 128])
        Mcur = sb("Mcur", [P, 64])
        Scur = sb("Scur", [P, 128])
        w2a2 = sb("w2a2", [P, 2, 128])
        poolw = sb("poolw", [P, 128])
        lora = sb("lora", [P, TB])
        stat = sb("stat", [P, 3, 8])

        pos = [0]

        def hview(n):
            a = xm[:, pos[0]:pos[0] + n]
            pos[0] += n
            return a

        h_uf, h_uq, h_vT, h_ugp, h_ugh = ([hview(TB) for _ in range(2)] for _ in range(5))
        h_U = [hview(16 + TB) for _ in range(2)]
        h_sq, h_sgp, h_sgh, h_e1, h_en, h_l2, h_k, h_cum = (hview(TB) for _ in range(8))
        h_D = [hview(TB) for _ in range(2)]
        h_Z = [hview(TB) for _ in range(2)]
        h_sc, h_ec, h_kd, h_kdT, h_pp, h_sqo, h_rn = (hview(TB) for _ in range(7))
        h_ws = arena[:, 8200:8200 + 4 * 528]
        assert pos[0] <= 4 * KC * TB
        xmv = [xm[:, i * KC * TB:(i + 1) * KC * TB].rearrange("p (k t) -> p k t", k=KC) for i in range(4)]

        rpos = [0]

        def rview(n):
            a = arena[:, rpos[0]:rpos[0] + n]
            rpos[0] += n
            return a

        r_AR, r_BK = rview(1024), rview(1024)
        r_BKt, r_UV = rview(1024), rview(1024)
        r_Gs = rview(2048)
        r_N, r_L, r_T, r_TT = rview(1024), rview(1024), rview(1024), rview(1024)
        r_sw, r_cs, r_pv, r_av, r_k, r_v, r_r, r_z, r_ta, r_tb, r_km, r_kn, r_bv = (rview(TB) for _ in range(13))
        r_pm = rview(64)
        r_xs = rview(64)
        r_ec = rview(NCH)
        r_y, r_yd = r_L[:, 0:TB], r_L[:, TB:2 * TB]
        r_zs = r_TT[:, 0:TB]
        assert rpos[0] <= 4096 + 4104 + 8900, rpos[0]
        resid = nc.dram_tensor("residual_scratch", [n_blocks, P, JT * D], F32, kind="Internal").ap()

        ada_w = [xm[:, i * 3072:(i + 1) * 3072] for i in range(4)]
        ada_acc = wring[:, 0:3, :].rearrange("p s n -> p (s n)")
        rowsA = wring[:, 3, 0:128]
        rowsB = wring[:, 3, 128:256]
        m_s, m_t, m_x, m_y = (wring[:, 4, i * 128:(i + 1) * 128] for i in range(4))
        i_s, i_t, i_x, i_y = (wring[:, 5, i * 128:(i + 1) * 128].bitcast(I32) for i in range(4))
        i_r = wring[:, 6, 0:TB].bitcast(I32)
        i_r2 = wring[:, 6, 512:1024].bitcast(I32)
        postb = wring[:, 7, :]
        m_ge = wring[:, 4, 512:640]
        m_le = wring[:, 4, 640:768]

        names = """su_rows su_post su_iota su_tr su_param su_csig su_cond su_lbe su_acc su_accd su_mm su_gate
        su_done passed own_dve own_act own_pool x_in x_out r_save r_load n_ss n_rstd n_xn n_tr n_ev_act n_ev_dve w2_in pw_in
        pw_free hp_ready hp_ev h_sig h_gate h_sp h_en h_enc h_l2 h_lsu h_k h_cum h_ec h_dif h_e h_z h_lv h_lvc h_dk h_ek
        h_kd h_kt h_kdT h_qd h_win h_pp h_po h_pooled h_s h_sz h_o h_osq h_ss h_rn h_y op_ready op_ss op_sum op_rstd ob
        xm_r lo_in lo_pe lo_r rp_ready rp_ev w2_free r_ksq ms_ready ms_free r_sig rk_sum v_tok v_tr y_mean y_cent y_var r_rs r_scan r_dec r_arbk r_rk sc_ready
        sc_free r_n0 r_n tr_l l_r inv1 invw invt invtt inv2 invT ch_x ch_xs ch_u ch_us ch_z ch_m ch_pm y_ready y_sb
        r_dsq r_var r_done""".split()
        S = {n: ctx.enter_context(nc.semaphore(n)) for n in names}
        su_ada = [ctx.enter_context(nc.semaphore(f"su_ada{i}")) for i in range(4)]
        w_in = [ctx.enter_context(nc.semaphore(f"w_in{s}")) for s in range(SLOTS)]
        w_used = [ctx.enter_context(nc.semaphore(f"w_used{s}")) for s in range(SLOTS)]
        block = ctx.enter_context(nc.Block())

        x_v = io["x"].rearrange("o (n j p) d -> (o n) p j d", j=JT, p=P)
        out_v = io["out"].rearrange("o (n j p) d -> (o n) p j d", j=JT, p=P)
        w_in_v = io["ev_w_in"][0].rearrange("(k p) (s g e) -> s g p k e", p=P, s=NP, g=HG)
        w_out_v = [io["ev_w_out"][0].rearrange("(k p) n -> k p n", p=P),
                   io["rw_w_out"][0].rearrange("(k p) n -> k p n", p=P)]
        rkvz_v = io["rw_w_rkvz"][0].rearrange("m (k p) (g e) -> m g p k e", p=P, g=RP)
        RKVZ = [1, 0, 2, 3]

        def gs_at(c, h):
            return ((2 * (c // 4) + h) * 4 + c % 4) * P

        def second_half(t, lv):
            m = 2 << lv
            return t.rearrange("p (c a x m) -> p c a x m", x=2, m=m, a=P // (2 * m))[:, :, :, 1, :]

        def plain(eng):
            eng.sem_inc(S["passed"], 1)

        @block.sync
        def _(sp):
            n_rows = 0
            for src, at, dst in (
                    [(io["ada_b"].rearrange("l (r c) -> (l r) c", c=P), ROWS_A["ada_b"], rowsA),
                     (io["pre_g"].rearrange("l (r c) -> (l r) c", c=P), ROWS_A["pre_g"], rowsA),
                     (io["c"].rearrange("l (r c) -> (l r) c", c=P), ROWS_A["c"], rowsA),
                     (io["pool_scale"].rearrange("l (r c) -> (l r) c", c=P), ROWS_A["pool_scale"], rowsA),
                     (io["hgrn_onorm_g"].rearrange("l (r c) -> (l r) c", c=P), ROWS_A["onorm"], rowsA),
                     (io["hgrn_lb_logits"].rearrange("l (r c) -> (l r) c", c=P), ROWS_A["lb"], rowsA)]
                    + [(io[n].rearrange("l (r c) -> (l r) c", c=P), ROWS_B[m], rowsB) for n, m in
                       [("rw_w0", "w0"), ("rw_a0", "a0"), ("rw_k_k", "k_k"), ("rw_k_a", "k_a"),
                        ("rw_lnx_g", "lnx_g"), ("rw_lnx_b", "lnx_b")]]
                    + [(io["rw_r_k"].rearrange("l (r x) c -> (l r) (x c)", x=2), ROWS_B["r_k"], rowsB),
                       (io["rw_mu"].rearrange("l m (r c) -> (l m r) c", c=P), ROWS_B["mu"], rowsB)]):
                sp.dma_start(dst[at:at + src.shape[0], :], src).then_inc(S["su_rows"], 16)
                n_rows += 1
            assert n_rows == 14
            for i in range(2 * KC):
                if i >= 4:
                    sp.wait_ge(S["su_accd"], i - 3)
                sp.dma_start(ada_w[i % 4], io["ada_w"][i // KC, (i % KC) * P:(i % KC + 1) * P, :]).then_inc(su_ada[i % 4], 16)
                if i % KC == 0:
                    if i:
                        sp.wait_ge(S["su_gate"], 1)
                    sp.dma_start(postb, io["post_g"][i // KC:i // KC + 1, :].to_broadcast([P, D])).then_inc(S["su_post"], 16)
                    sp.dma_start(gpost[:, i // KC, :], io["ada_b"][i // KC:i // KC + 1, 2 * D:3 * D].to_broadcast([P, D])).then_inc(S["su_post"], 16)
            sp.wait_ge(S["su_done"], 1)

            def load(slot, use, src, dst=None):
                sp.wait_ge(w_used[slot], 1 + use)
                plain(sp)
                sp.dma_start(wring[:, slot, :] if dst is None else dst, src).then_inc(w_in[slot], 16)

            def slot_k(slot):
                return wring[:, slot, :].rearrange("p (k e) -> p k e", k=KC)

            with sp.Fori(0, n_blocks) as b:
                sp.wait_ge(S["x_out"], (b + 1) * 16)
                plain(sp)
                sp.dma_start(xres, x_v[ds(b, 1)][0]).then_inc(S["x_in"], 16)
                with sp.Fori(0, HG) as g:
                    for s in range(NP):
                        load(s, use_hgrn(b, g, s), w_in_v[PROJ_GROUP[s], ds(g, 1)][0], slot_k(s))
                    sp.wait_ge(S["pw_free"], 1 + b * HG + g)
                    plain(sp)
                    sp.dma_start(poolw[:, :], io["pool_w"][0, ds(g, 1)][0]).then_inc(S["pw_in"], 16)
                for s in range(SLOTS):
                    load(s, use_out0(b, s), w_out_v[0][s])
                sp.wait_ge(w_used[0], 1 + use_lora(b))
                for i, n in enumerate(("rw_w1", "rw_a1")):
                    sp.dma_start(slot_k(0)[:, :, 64 * i:64 * i + 64],
                                 io[n][0].rearrange("(k p) e -> p k e", p=P)).then_inc(w_in[0] if i else S["lo_in"], 16)
                sp.wait_ge(S["ob"], (2 * b + 1) * 8)
                plain(sp)
                sp.dma_start(resid[ds(b, 1)][0], arena[:, 0:4096]).then_inc(S["r_save"], 16)
                with sp.Fori(0, RP // 2) as pp:
                    for q in range(2):
                        for m in range(4):
                            s = 4 * q + m
                            load(s, use_rwkv(b, pp, s), rkvz_v[RKVZ[m], ds(2 * pp + q, 1)][0], slot_k(s))
                        sp.wait_ge(S["w2_free"], 1 + b * RP + 2 * pp + q)
                        plain(sp)
                        for i, n in enumerate(("rw_w2", "rw_a2")):
                            sp.dma_start(w2a2[64 * i:64 * i + 64, q, :],
                                         io[n][0, :, ds((2 * pp + q) * P, P)]).then_inc(S["w2_in"], 16)
                for s in range(SLOTS):
                    load(s, use_out1(b, s), w_out_v[1][s])
                sp.wait_ge(S["r_done"], 1 + (b + 1) * RP)
                plain(sp)
                sp.wait_ge(S["r_save"], (b + 1) * 16)
                plain(sp)
                sp.dma_start(arena[:, 0:4096], resid[ds(b, 1)][0]).then_inc(S["r_load"], 16)
                sp.wait_ge(S["ob"], (2 * b + 2) * 8)
                plain(sp)
                sp.dma_start(out_v[ds(b, 1)][0], xres).then_inc(S["x_out"], 16)
            sp.wait_ge(S["x_out"], (n_blocks + 1) * 16)

        @block.tensor
        def _(pe):
            pe.wait_ge(S["su_iota"], 6)
            pe.wait_ge(S["su_rows"], 14 * 16)
            pe.transpose(MS[:, 0:N_A], rowsA[0:N_A, :], ident[0:N_A, 0:N_A]).then_inc(S["su_tr"], 1)
            pe.transpose(XB[:, 0:N_B], rowsB[0:N_B, :], ident[0:N_B, 0:N_B]).then_inc(S["su_tr"], 1)
            pe.wait_ge(S["su_param"], 2)
            for l in range(2):
                pe.wait_ge(S["su_accd"], KC * (l + 1))
                if l:
                    pe.wait_ge(S["su_gate"], 1)
                for e in range(2 * KC):
                    mm = pe.matmul(MS[:, e:e + 1], ada_acc[:, e * P:(e + 1) * P], ones[:, 0:1], start=True, stop=True)
                mm.then_inc(S["su_mm"], 1)
                for e in range(2):
                    mm = pe.matmul(bank[e][:, :], ones[:, :], ada_acc[:, 2 * D + e * 512:2 * D + (e + 1) * 512],
                                   start=True, stop=True)
                mm.then_inc(S["su_mm"], 1)
            pe.wait_ge(S["su_done"], 1)

            def norm_transposes(b, l):
                n = (2 * b + l) * 4
                pe.wait_ge(S["n_xn"], n + 4)
                for k in range(KC):
                    if k >= 4:
                        pe.wait_ge(S["n_ev_dve"] if k % 2 else S["n_ev_act"], n + (k - 4) // 2 + 1)
                    for j in range(JT):
                        mm = pe.transpose(bank[k % 4][:, j * P:(j + 1) * P],
                                          yT[:, j * D + k * P:j * D + (k + 1) * P], ident[:, :])
                    mm.then_inc(S["n_tr"], 1)
                pe.wait_ge(S["n_ev_act"], n + 4)
                pe.wait_ge(S["n_ev_dve"], n + 4)
                plain(pe)

            def hgrn_proj(b, g, n0, n1):
                U, q = b * HG + g, g % 2
                for n in range(n0, n1):
                    i, k = n // KC, n % KC
                    pj = bank[(NP * q + i) % 4]
                    if k == 0:
                        pe.wait_ge(w_in[i], (use_hgrn(b, g, i) + 1) * 16)
                        pe.wait_ge(S["hp_ev"], 1 + U * NP + (i - 3 if i >= 4 else 0))
                    w = wring[:, i, :].rearrange("p (k e) -> p k e", k=KC)
                    if i == PROJ_I:
                        j = k // 2
                        for kk in range(k % 2 * 4, k % 2 * 4 + 4):
                            mm = pe.matmul(pj[:, j * P:(j + 1) * P], hT[:, kk, 1 + j * P:1 + (j + 1) * P], w[:, kk, :],
                                           start=(kk == 0), stop=(kk == KC - 1))
                    else:
                        mm = pe.matmul(pj[:, :], w[:, k, :], hT[:, k, 1:1 + TB], start=(k == 0), stop=(k == KC - 1))
                    if k == KC - 1:
                        mm.then_inc(S["hp_ready"], 1)

            def hgrn_mix(b, g):
                U, q = b * HG + g, g % 2
                done = 0

                def ahead(n):
                    nonlocal done
                    if g + 1 < HG:
                        hgrn_proj(b, g + 1, done, n)
                    done = n

                ahead(HP_AT_LEVEL[0])
                pe.wait_ge(S["h_y"], 1 + U)
                for n in range(LEVELS + 1):
                    ahead(HP_AT_LEVEL[n])
                    pe.wait_ge(S["h_z"], U * (LEVELS + 1) + n + 1)
                    if n >= 2:
                        pe.wait_ge(S["h_lvc"], U * (LEVELS + 1) + n - 1)
                    for c in range(JT):
                        cc = slice(c * HC, (c + 1) * HC)
                        lhs, rhs = (h_k, h_sq) if n == 0 else (h_Z[n % 2], h_Z[n % 2])
                        mm = pe.matmul(LV[n % 2][:, cc], lhs[:, cc], rhs[:, cc], start=True, stop=True)
                    mm.then_inc(S["h_lv"], 1)
                ahead(HP_AT_POOL)
                pe.wait_ge(S["pw_in"], (U + 1) * 16)
                pe.wait_ge(S["h_pp"], U + 1)
                pe.matmul(MS[:, :], poolw[:, :], h_pp, start=True, stop=True).then_inc(S["h_po"], 1)
                pe.wait_ge(S["h_kd"], U + 1)
                pe.wait_ge(S["h_pooled"], 1 + U + 1)
                for c in range(JT):
                    cc = slice(c * HC, (c + 1) * HC)
                    mm = pe.transpose(MS[:, cc], h_kd[:, cc], ident[:, :])
                mm.then_inc(S["h_kt"], 1)
                pe.wait_ge(S["h_qd"], U + 1)
                pe.wait_ge(S["h_lvc"], (U + 1) * (LEVELS + 1))
                pe.wait_ge(S["h_kdT"], U + 1)
                for c in range(JT):
                    cc = slice(c * HC, (c + 1) * HC)
                    if c:
                        ahead(HP_AT_POOL + c)
                    pe.wait_ge(S["h_s"], U * (JT + 1) + c + 1)
                    pe.matmul(OB[:, cc], Scur[:, :], h_en[:, cc], start=True, stop=False)
                    mm = pe.matmul(OB[:, cc], h_vT[q][:, cc], h_sc[:, cc], start=False, stop=True)
                    if c == JT - 1:
                        mm.then_inc(S["h_o"], 1)
                    pe.matmul(MS[:, 0:HC], h_kdT[:, cc], h_vT[q][:, cc], start=True, stop=True).then_inc(S["h_sz"], 1)
                ahead(NP * KC)
                pe.wait_ge(S["h_osq"], U + 1)
                pe.wait_ge(S["h_s"], (U + 1) * (JT + 1))
                pe.matmul(MS[:, :], ones[:, :], h_sqo, start=True, stop=True).then_inc(S["h_ss"], 1)

            def out_proj(b, l):
                if l == 0:
                    pe.wait_ge(S["h_y"], 1 + (b + 1) * HG)
                else:
                    pe.wait_ge(S["r_done"], 1 + (b + 1) * RP)
                for k in range(KC):
                    use = use_out1(b, k) if l else use_out0(b, k)
                    pe.wait_ge(w_in[k], (use + 1) * 16)
                    for n in range(8):
                        j, h = n // 2, n % 2
                        mm = pe.matmul(bank[n][:, :], yTv[:, k, j * P:(j + 1) * P], wring[:, k, h * 512:(h + 1) * 512],
                                       start=(k == 0), stop=(k == KC - 1))
                        if k == KC - 1:
                            mm.then_inc(S["op_ready"], 1)
                    if k < KC - 1:
                        mm.then_inc(w_used[k], 1)

            def lora_down(b):
                pe.wait_ge(S["lo_in"], (b + 1) * 16)
                pe.wait_ge(w_in[0], (use_lora(b) + 1) * 16)
                pe.wait_ge(S["xm_r"], b * 3 + 1)
                w = wring[:, 0, :].rearrange("p (k e) -> p k e", k=KC)
                for k in range(KC):
                    pe.matmul(MS[0:64, :], w[:, k, 0:64], xmv[0][:, k, :], start=(k == 0), stop=(k == KC - 1))
                    mm = pe.matmul(MS[64:128, :], w[:, k, 64:128], xmv[1][:, k, :], start=(k == 0), stop=(k == KC - 1))
                mm.then_inc(S["lo_pe"], 1)

            def rwkv_proj(b, pp, q, n0, n1):
                u = b * RP + 2 * pp + q
                for n in range(n0, n1):
                    i, k = (n, 0) if n < 2 else (2 + (n - 2) // KC, (n - 2) % KC)
                    pj = YB if i == 5 else bank[(6 * q + i) % 4]
                    if k == 0 and i < 5:
                        pe.wait_ge(S["rp_ev"], 1 + u * 6 + (i - 3 if i >= 4 else 0))
                    if i < 2:
                        if i == 0:
                            pe.wait_ge(S["w2_in"], (u + 1) * 32)
                            pe.wait_ge(S["lo_r"], 2 * (b + 1))
                        r = slice(64 * i, 64 * i + 64)
                        mm = pe.matmul(pj[:, :], w2a2[r, q, :], lora[r, :], start=True, stop=True)
                    else:
                        s = 4 * q + i - 2
                        if n == 2:
                            pe.wait_ge(S["xm_r"], (b + 1) * 3)
                        if k == 0:
                            pe.wait_ge(w_in[s], (use_rwkv(b, pp, s) + 1) * 16)
                        w = wring[:, s, :].rearrange("p (k e) -> p k e", k=KC)
                        mm = pe.matmul(pj[:, :], w[:, k, :], xmv[RKVZ[i - 2]][:, k, :],
                                       start=(k == 0), stop=(k == KC - 1))
                    if i < 2 or k == KC - 1:
                        mm.then_inc(S["rp_ready"], 1)

            def rwkv_norm_mean(u):
                pe.wait_ge(S["y_sb"], u + 1)
                pe.matmul(YB[:, :], blk64[:, :], r_y, start=True, stop=True).then_inc(S["y_mean"], 1)

            def rwkv_norm_var(u):
                pe.wait_ge(S["r_dsq"], u + 1)
                pe.matmul(YB[:, :], blk64[:, :], r_yd, start=True, stop=True).then_inc(S["y_var"], 1)

            def rwkv_prepare(b, pp, q, prev):
                u = b * RP + 2 * pp + q
                if prev:
                    rwkv_norm_mean(u - 1)
                pe.wait_ge(S["r_ksq"], u + 1)
                pe.wait_ge(S["ms_free"], 1 + u * 3)
                pe.matmul(MS[:, :], blk[:, :], r_ta, start=True, stop=True).then_inc(S["ms_ready"], 1)
                rwkv_proj(b, pp, q, RN_CHAIN, RN_CHAIN + 2)
                if prev:
                    rwkv_norm_var(u - 1)
                rwkv_proj(b, pp, q, RN_CHAIN + 2, RN_CHAIN + 6)
                pe.wait_ge(S["r_rk"], u + 1)
                pe.matmul(XB[:, :], blk[:, :], r_ta, start=True, stop=True).then_inc(S["rk_sum"], 1)
                rwkv_proj(b, pp, q, RN_CHAIN + 6, RN - KC)
                if prev:
                    pe.wait_ge(S["r_var"], u)
                rwkv_proj(b, pp, q, RN - KC, RN - KC + 2)
                pe.wait_ge(S["rp_ev"], 1 + u * 6 + 5)
                for j in range(JT):
                    mm = pe.transpose(UZ[:, j * P:(j + 1) * P], r_v[:, j * P:(j + 1) * P], ident[:, :])
                mm.then_inc(S["v_tr"], 1)
                rwkv_proj(b, pp, q, RN - KC + 2, RN - KC + 5)
                pe.wait_ge(S["r_arbk"], u + 1)
                for h in range(2):
                    if h:
                        rwkv_proj(b, pp, q, RN - KC + 5, RN - KC + 6)
                    pe.wait_ge(S["ms_free"], 1 + u * 3 + 1 + h)
                    for c in range(4):
                        mm = pe.transpose(MS[:, c * P:(c + 1) * P], r_BK[:, (4 * h + c) * P:(4 * h + c + 1) * P], ident[:, :])
                    mm.then_inc(S["ms_ready"], 1)
                for i in range(4):
                    h, r = i % 2, slice(64 * (i % 2), 64 * (i % 2) + 64)
                    for c4 in range(4):
                        c = 4 * (i // 2) + c4
                        mm = pe.matmul(bank[i][:, c4 * P:(c4 + 1) * P], r_BK[r, c * P:(c + 1) * P],
                                       r_AR[r, c * P:(c + 1) * P], start=True, stop=True)
                    mm.then_inc(S["sc_ready"], 1)
                for h in range(2):
                    rwkv_proj(b, pp, q, RN - KC + 6 + h, RN - KC + 7 + h)
                    pe.wait_ge(S["r_n"], u * 2 + h + 1)
                    for c in range(4):
                        mm = pe.transpose(bank[h][:, c * P:(c + 1) * P], r_N[:, (4 * h + c) * P:(4 * h + c + 1) * P], ident[:, :])
                    mm.then_inc(S["tr_l"], 1)
                pe.wait_ge(S["l_r"], (u + 1) * 2)
                for lv in range(5):
                    for h in range(2):
                        pe.wait_ge(S["invT"], u * 12 + 2 * lv + h + 1)
                        for c in range(4):
                            cc = slice((4 * h + c) * P, (4 * h + c + 1) * P)
                            mm = pe.transpose(bank[2 + h][:, c * P:(c + 1) * P], r_T[:, cc], ident[:, :])
                        mm.then_inc(S["invt"], 1)
                        for c in range(4):
                            cc = slice((4 * h + c) * P, (4 * h + c + 1) * P)
                            mm = pe.matmul(bank[h][:, c * P:(c + 1) * P], r_L[:, cc], r_T[:, cc], start=True, stop=True)
                        mm.then_inc(S["inv1"], 1)
                    for h in range(2):
                        pe.wait_ge(S["invtt"], u * 10 + 2 * lv + h + 1)
                        pe.wait_ge(S["invw"], u * 10 + 2 * lv + h + 1)
                        for c in range(4):
                            cc = slice((4 * h + c) * P, (4 * h + c + 1) * P)
                            mm = pe.matmul(bank[h][:, c * P:(c + 1) * P], r_TT[:, cc], r_N[:, cc], start=True, stop=True)
                        mm.then_inc(S["inv2"], 1)

            def rwkv_chunk(b, pp, q, c, nxt):

                def ahead(gap):
                    if nxt:
                        rwkv_proj(b, *nxt, -(-RN_CHAIN * (3 * c + gap) // (3 * NCH)), -(-RN_CHAIN * (3 * c + gap + 1) // (3 * NCH)))

                u = b * RP + 2 * pp + q
                heads = [(h, slice(64 * h, 64 * h + 64)) for h in range(2)]
                gs = [gs_at(c, h) for h in range(2)]
                a_c, r_c = slice(c * P, c * P + 64), slice(c * P + 64, (c + 1) * P)
                uv = slice(c * P, (c + 1) * P)
                if c == 0:
                    pe.wait_ge(S["invT"], (u + 1) * 12)
                    pe.wait_ge(S["ms_free"], 1 + (u + 1) * 3)
                    pe.wait_ge(S["v_tok"], u + 1)
                    pe.wait_ge(S["rp_ev"], 1 + (u + 1) * 6)
                    pe.wait_ge(S["r_done"], 1 + u)
                    plain(pe)
                for h, r in heads:
                    pe.matmul(XB[r, 0:64], r_Gs[r, gs[h]:gs[h] + 64],
                              r_UV[r, c * P + 64 * h:c * P + 64 * h + 64], start=True, stop=False)
                pe.wait_ge(S["ch_m"], u * (NCH + 1) + c + 1)
                plain(pe)
                for h, r in heads:
                    mm = pe.matmul(XB[r, 0:64], r_AR[r, a_c], Mcur[r, :], start=False, stop=True)
                mm.then_inc(S["ch_x"], 1)
                for h, r in heads:
                    pe.matmul(YB[r, c * RC:(c + 1) * RC], Mcur[r, :], r_AR[r, r_c], start=True, stop=False)
                ahead(0)
                pe.wait_ge(S["ch_xs"], u * NCH + c + 1)
                plain(pe)
                for h, r in heads:
                    mm = pe.matmul(UZ[64 - 64 * h:128 - 64 * h, 0:64], r_T[r, c * P + 64 * h:c * P + 64 * h + 64], r_xs[r, :],
                                   start=True, stop=True)
                mm.then_inc(S["ch_u"], 1)
                ahead(1)
                pe.wait_ge(S["ch_us"], u * NCH + c + 1)
                for h, r in heads:
                    mm = pe.matmul(UZ[r, 128:192], r_BKt[:, c * P + 64 * h:c * P + 64 * h + 64],
                                   r_UV[:, c * P + 64 * h:c * P + 64 * h + 64], start=True, stop=True)
                mm.then_inc(S["ch_z"], 1)
                for h, r in heads:
                    mm = pe.matmul(YB[r, c * RC:(c + 1) * RC], r_UV[:, c * P + 64 * h:c * P + 64 * h + 64],
                                   r_Gs[:, gs[h] + 64:gs[h] + P], start=False, stop=True)
                if c == NCH - 1:
                    mm.then_inc(S["y_ready"], 1)
                ahead(2)

            with pe.Fori(0, n_blocks) as b:
                norm_transposes(b, 0)
                hgrn_proj(b, 0, 0, NP * KC)
                for g in range(HG):
                    hgrn_mix(b, g)
                out_proj(b, 0)
                norm_transposes(b, 1)
                lora_down(b)

                def chain(pp, q, nxt):
                    for c in range(NCH):
                        rwkv_chunk(b, pp, q, c, nxt)

                last = RP // 2 - 1
                rwkv_proj(b, 0, 0, 0, RN_CHAIN)
                rwkv_prepare(b, 0, 0, False)
                with pe.Fori(0, last) as pp:
                    chain(pp, 0, (pp, 1))
                    rwkv_prepare(b, pp, 1, True)
                    chain(pp, 1, (pp + 1, 0))
                    rwkv_prepare(b, pp + 1, 0, True)
                chain(last, 0, (last, 1))
                rwkv_prepare(b, last, 1, True)
                chain(last, 1, None)
                rwkv_norm_mean((b + 1) * RP - 1)
                rwkv_norm_var((b + 1) * RP - 1)
                out_proj(b, 1)

        @block.scalar
        def _(act):
            own = Own(act, S["own_act"])
            act.wait_ge(S["su_tr"], 2)
            act.copy(PA[:, :], MS[:, 0:N_A]).then_inc(S["su_param"], 1)
            act.copy(PB[:, :], XB[:, 0:N_B]).then_inc(S["su_param"], 1)
            act.wait_ge(S["su_param"], 2)
            act.activation(cond[:, :], PA[:, ROWS_A["c"]:ROWS_A["c"] + KC], ACT.Sigmoid).then_inc(S["su_csig"], 1)
            act.wait_ge(S["su_lbe"], 1)
            act.activation(lbv[:, 1, :], lbv[:, 0, :], ACT.Exp).then_inc(S["su_csig"], 1)
            act.wait_ge(S["su_done"], 1)

            def rstd(out, in_, n, bias, ready):
                own(act.activation(out, in_, ACT.Ln, bias=bias, scale=1.0 / n))
                own.wait()
                act.activation(out, out, ACT.Exp, scale=-0.5).then_inc(ready, 1)

            def norm(b, l):
                n = 2 * b + l
                if l == 0:
                    act.wait_ge(S["x_in"], (b + 1) * 16)
                else:
                    act.wait_ge(S["ob"], (2 * b + 1) * 8)
                for j in range(JT):
                    own(act.activation(xm[:, j * D:(j + 1) * D], xres[:, j, :], ACT.Square, accum_out=stat[:, 0, j:j + 1]))
                own.wait()
                rstd(stat[:, 1, 0:JT], stat[:, 0, 0:JT], D, eps_norm, S["n_rstd"])
                for k in range(0, KC, 2):
                    act.wait_ge(S["n_tr"], n * KC + k + 1)
                    act.activation(hT[:, k, 1:1 + TB], bank[k % 4][:, :], ACT.Identity, bias=shift[:, l, k:k + 1],
                                   scale=g1[:, l, k:k + 1]).then_inc(S["n_ev_act"], 1)
                own.restart()

            def hgrn_evac(b, g, i):
                U, q = b * HG + g, g % 2
                dst = (h_uf[q], h_uq[q], h_vT[q], h_U[q][:, 16:16 + TB], h_ugp[q], h_ugh[q])[i]
                act.wait_ge(S["hp_ready"], U * NP + i + 1)
                act.nop().then_inc(w_used[i], 1)
                act.copy(dst, bank[(NP * q + i) % 4][:, :]).then_inc(S["hp_ev"], 1)

            def hgrn_act(b, g):
                U, q = b * HG + g, g % 2

                def ahead(i):
                    if g + 1 < HG:
                        hgrn_evac(b, g + 1, i)

                act.wait_ge(S["h_y"], 1 + U)
                act.wait_ge(S["h_pooled"], 1 + U)
                act.wait_ge(S["hp_ev"], 1 + (U + 1) * NP)
                for dst, src in ((h_sq, h_uq[q]), (h_sgp, h_ugp[q]), (h_sgh, h_ugh[q])):
                    act.activation(dst, src, ACT.Sigmoid).then_inc(S["h_sig"], 1)
                own(act.activation(h_e1, h_uf[q], ACT.Abs))
                act.activation(h_en, h_uf[q], ACT.Exp, scale=-1.0).then_inc(S["h_en"], 1)
                own.wait()
                own(act.activation(h_e1, h_e1, ACT.Exp, scale=-1.0))
                own.wait()
                act.activation(h_e1, h_e1, ACT.Ln, bias=c_one).then_inc(S["h_sp"], 1)
                act.wait_ge(S["h_enc"], U + 1)
                act.activation(h_l2, h_en, ACT.Ln, bias=c_one, scale=lb[:, g:g + 1]).then_inc(S["h_l2"], 1)
                ahead(0)
                act.wait_ge(S["h_lsu"], U + 1)
                act.activation(h_k, h_D[0], ACT.Exp).then_inc(S["h_k"], 1)
                act.wait_ge(S["h_cum"], U + 1)
                act.activation(h_ec, h_cum, ACT.Exp).then_inc(S["h_ec"], 1)
                ahead(1)
                for n in range(1, LEVELS + 1):
                    m = HC >> n
                    act.wait_ge(S["h_dif"], U * LEVELS + n)
                    if n >= 3:
                        act.wait_ge(S["h_lv"], U * (LEVELS + 1) + n - 1)
                    dv, zv = (t.rearrange("p (a x m) -> p a x m", x=2, m=m) for t in (h_D[n % 2], h_Z[n % 2]))
                    own(act.activation(zv[:, :, 0, :], dv[:, :, 0, :], ACT.Exp, scale=-1.0))
                    act.activation(zv[:, :, 1, :], dv[:, :, 1, :], ACT.Exp).then_inc(S["h_e"], 1)
                    if n in (3, 6):
                        ahead(2 if n == 3 else 3)
                act.wait_ge(S["h_dk"], U + 1)
                act.activation(h_kd, h_D[0], ACT.Exp, scale=-1.0).then_inc(S["h_ek"], 1)
                ahead(4)
                act.wait_ge(S["h_kt"], U + 1)
                act.copy(h_kdT, MS[:, :]).then_inc(S["h_kdT"], 1)
                act.wait_ge(S["h_o"], U + 1)
                act.activation(h_sqo, OB[:, :], ACT.Square).then_inc(S["h_osq"], 1)
                ahead(5)
                act.wait_ge(S["h_ss"], U + 1)
                rstd(h_rn, MS[:, :], HC, eps_norm, S["h_rn"])
                own.restart()

            def out_norm(b, l):
                n0 = (2 * b + l) * 8
                for n in range(8):
                    act.wait_ge(S["op_ready"], n0 + n + 1)
                    if n == 7:
                        act.nop().then_inc(w_used[7], 1)
                    act.activation(xm[:, n * 512:(n + 1) * 512], bank[n][:, :], ACT.Square,
                                   accum_out=stat[:, 2, n:n + 1]).then_inc(S["op_ss"], 1)
                act.wait_ge(S["op_sum"], 2 * b + l + 1)
                rstd(stat[:, 1, 4:8], stat[:, 1, 0:4], D, eps_norm, S["op_rstd"])
                own.restart()

            def lora_act(b):
                act.wait_ge(S["lo_pe"], b + 1)
                act.nop().then_inc(w_used[0], 1)
                act.activation(lora[0:64, :], MS[0:64, :], ACT.Tanh).then_inc(S["lo_r"], 1)
                act.copy(lora[64:128, :], MS[64:128, :]).then_inc(S["lo_r"], 1)
                act.wait_ge(S["r_save"], (b + 1) * 16)
                act.wait_ge(S["xm_r"], (b + 1) * 3)

            def rwkv_evac(b, pp, q, i):
                u, p = b * RP + 2 * pp + q, 2 * pp + q
                act.wait_ge(S["rp_ready"], u * 6 + i + 1)
                if i == 1:
                    act.nop().then_inc(S["w2_free"], 1)
                if i >= 2:
                    act.nop().then_inc(w_used[4 * q + i - 2], 1)
                src = YB[:, :] if i == 5 else bank[(6 * q + i) % 4][:, :]
                if i == 0:
                    ins = act.activation(r_sw, src, ACT.Sigmoid, bias=PB[:, ds(p + ROWS_B["w0"], 1)])
                elif i == 1:
                    ins = act.activation(r_av, src, ACT.Sigmoid, bias=PB[:, ds(p + ROWS_B["a0"], 1)])
                elif i == 5:
                    ins = act.copy(r_z, src)
                else:
                    ins = act.copy((r_k, r_r, r_v)[i - 2], src)
                ins.then_inc(S["rp_ev"], 1)

            def rwkv_norm_copy(u):
                act.wait_ge(S["y_ready"], u + 1)
                act.copy(r_y, YB[:, :]).then_inc(S["y_sb"], 1)

            def rwkv_norm_square(u):
                act.wait_ge(S["y_cent"], u + 1)
                act.activation(r_yd, r_y, ACT.Square).then_inc(S["r_dsq"], 1)

            def rwkv_norm_ln(u):
                act.wait_ge(S["y_var"], u + 1)
                own(act.activation(r_yd, YB[:, :], ACT.Ln, bias=eps_lnx))

            def rwkv_act(b, pp, q, prev):
                u = b * RP + 2 * pp + q
                p = 2 * pp + q
                if prev:
                    rwkv_norm_copy(u - 1)
                act.wait_ge(S["rp_ev"], 1 + u * 6 + 4)
                act.activation(r_ta, r_k, ACT.Square, scale=PB[:, ds(p + ROWS_B["k_k"], 1)]).then_inc(S["r_ksq"], 1)
                if prev:
                    rwkv_norm_square(u - 1)
                act.wait_ge(S["ms_free"], 1 + u * 3 + 1)
                own(act.activation(r_tb, r_tb, ACT.Ln, scale=SS_SCALE))
                if prev:
                    rwkv_norm_ln(u - 1)
                own.wait()
                act.activation(r_tb, r_tb, ACT.Exp, scale=-0.5, bias=c_ss).then_inc(S["r_rs"], 1)
                act.wait_ge(S["r_scan"], u + 1)
                own(act.activation(r_pv, r_cs, ACT.Exp, scale=DECAY))
                own(act.activation(r_sw, r_sw, ACT.Exp, scale=-DECAY))
                own.wait()
                act.activation(r_cs, r_cs, ACT.Exp, scale=-DECAY).then_inc(S["r_dec"], 1)
                if prev:
                    act.activation(r_yd, r_yd, ACT.Exp, scale=-0.5).then_inc(S["r_var"], 1)
                rwkv_evac(b, pp, q, 4)
                act.wait_ge(S["v_tr"], u + 1)
                uv = r_UV.rearrange("p (j x e) -> p j x e", x=2, e=P)
                vt = UZ[:, :].rearrange("p (j e) -> p j e", e=P)
                for h in range(2):
                    for x in range(2):
                        r, e = slice(64 * h, 64 * h + 64), slice(64 * h, 64 * h + 64)
                        own(act.copy(uv[r, :, x, e], vt[64 * x:64 * x + 64, :, e]))
                own.wait()
                act.nop().then_inc(S["v_tok"], 1)
                for h in range(2):
                    act.wait_ge(S["ms_ready"], u * 3 + 2 + h)
                    act.copy(r_BKt[:, 512 * h:512 * h + 512], MS[:, :]).then_inc(S["ms_free"], 1)
                act.wait_ge(S["r_n0"], b + 1)
                gv = r_Gs.rearrange("p (a h c e) -> p a h c e", a=2, h=2, e=P)
                nv = r_N.rearrange("p (a c e) -> p a c e", a=2, e=P)
                for a in range(2):
                    act.wait_ge(S["sc_free"], u * 4 + 2 * a + 2)
                    for h in range(2):
                        r, rb = slice(64 * h, 64 * h + 64), slice(64 - 64 * h, 128 - 64 * h)
                        own(act.copy(nv[r, a, :, r], gv[rb, a, h, :, 0:64]))
                    own.wait()
                    act.nop().then_inc(S["r_n"], 1)
                for h in range(2):
                    act.wait_ge(S["tr_l"], u * 2 + h + 1)
                    act.copy(r_L[:, 512 * h:512 * h + 512], bank[h][:, :]).then_inc(S["l_r"], 1)
                act.wait_ge(S["r_done"], 1 + u)
                rwkv_evac(b, pp, q, 5)
                for lv in range(5):
                    for h in range(2):
                        act.wait_ge(S["invt"], u * 10 + 2 * lv + h + 1)
                        act.copy(r_TT[:, 512 * h:512 * h + 512], bank[2 + h][:, :]).then_inc(S["invtt"], 1)

            def rwkv_chain_act(b, pp, q, nxt):
                u = b * RP + 2 * pp + q
                for c in range(NCH):
                    act.wait_ge(S["ch_m"], u * (NCH + 1) + c + 1)
                    act.mul(r_pm, Mcur[:, :], r_ec[:, c:c + 1]).then_inc(S["ch_pm"], 1)
                    if c == 0:
                        act.wait_ge(S["invT"], (u + 1) * 12)
                        act.wait_ge(S["rp_ev"], 1 + (u + 1) * 6)
                        act.activation(r_zs, r_z, ACT.Sigmoid).then_inc(S["r_sig"], 1)
                    if nxt:
                        for i in EVAC_AT[c]:
                            rwkv_evac(b, *nxt, i)
                own.restart()

            with act.Fori(0, n_blocks) as b:
                norm(b, 0)
                for i in range(NP):
                    hgrn_evac(b, 0, i)
                for g in range(HG):
                    hgrn_act(b, g)
                out_norm(b, 0)
                norm(b, 1)
                lora_act(b)

                last = RP // 2 - 1
                for i in range(4):
                    rwkv_evac(b, 0, 0, i)
                rwkv_act(b, 0, 0, False)
                own.restart()
                with act.Fori(0, last) as pp:
                    rwkv_chain_act(b, pp, 0, (pp, 1))
                    rwkv_act(b, pp, 1, True)
                    rwkv_chain_act(b, pp, 1, (pp + 1, 0))
                    rwkv_act(b, pp + 1, 0, True)
                    own.restart()
                rwkv_chain_act(b, last, 0, (last, 1))
                rwkv_act(b, last, 1, True)
                rwkv_chain_act(b, last, 1, None)
                rwkv_norm_copy((b + 1) * RP - 1)
                rwkv_norm_square((b + 1) * RP - 1)
                rwkv_norm_ln((b + 1) * RP - 1)
                own.wait()
                act.activation(r_yd, r_yd, ACT.Exp, scale=-0.5).then_inc(S["r_var"], 1)
                own.restart()
                out_norm(b, 1)

        @block.vector
        def _(dve):
            own = Own(dve, S["own_dve"])
            V = dve

            def step(ins):
                own(ins)
                own.wait()

            V.wait_ge(S["su_iota"], 3)
            own(V.tensor_tensor(i_x, i_s, i_t, ALU.bitwise_xor))
            own(V.tensor_scalar(i_y, i_s, 63, None, ALU.bitwise_and))
            own(V.tensor_tensor(m_y, i_t, i_s, ALU.is_gt))
            own(V.memset(ones[:, :], 1.0))
            for v, col in ((EPS, 0), (LNX_EPS, 1), (1.0, 2), (HALF_LN_SS, 3)):
                own(V.memset(epsc[:, col:col + 1], v))
            own.wait()
            own(V.tensor_copy(m_x, i_x))
            own(V.tensor_copy(m_s, i_y))
            own(V.tensor_scalar(i_s, i_t, 63, None, ALU.bitwise_and))
            own.wait()
            V.tensor_scalar(ident[:, :], m_x, 0.0, None, ALU.is_equal).then_inc(S["su_iota"], 3)
            own(V.tensor_scalar(blk[:, :], m_x, 64.0, None, ALU.is_lt))
            own(V.tensor_scalar(blk64[:, :], m_x, 64.0, 1.0 / 64, ALU.is_lt, ALU.mult))
            own(V.tensor_copy(m_t, i_s))
            own(V.tensor_tensor(m_x, m_x, m_y, ALU.mult))
            own.wait()
            own(V.tensor_tensor(gmask[:, 0:64], m_t[:, 0:64], m_s[:, 0:64], ALU.is_gt))
            own(V.tensor_tensor(gmask[:, 64:128], m_t[:, 64:128], m_s[:, 64:128], ALU.is_ge))
            for j in range(LEVELS):
                step(V.tensor_scalar(m_ge, m_x, float(1 << j), None, ALU.is_ge))
                if j < 6:
                    own(V.scalar_tensor_tensor(out=wmask[:, j, :], in0=m_x, scalar=float(2 << j), in1=m_ge,
                                               op0=ALU.is_lt, op1=ALU.mult))
                own(V.scalar_tensor_tensor(out=lmask[:, j, :], in0=m_x, scalar=float(2 << j), in1=m_ge,
                                           op0=ALU.is_lt, op1=ALU.mult))
                own.wait()
            own(V.tensor_scalar(i_r2, i_r, 63, None, ALU.bitwise_and))
            own.wait()
            own(V.tensor_scalar(reset64[:, :], i_r2, 1.0, None, ALU.is_ge))
            own.wait()
            own(V.tensor_scalar(i_r2, i_r, 127, None, ALU.bitwise_and))
            own.wait()
            own(V.tensor_scalar(reset128[:, :], i_r2, 1.0, None, ALU.is_ge))
            for g in range(HG):
                win = float(2 << g)
                own(V.tensor_scalar(corr[:, 0, g, :], i_t[:, 0:16], 1.0, win, ALU.add, ALU.min))
                own(V.memset(corr[:, 1, g, :], 1.0 / win))
                own(V.memset(invwin[:, g:g + 1], 1.0 / win))
            own.wait()
            own(V.reciprocal(corr[:, 0, :, :], corr[:, 0, :, :]))
            for t in (Mall, Sall, halo):
                own(V.memset(t[:, :, :], 0.0))
            own(V.memset(hlast[:, :], 0.0))
            V.wait_ge(S["su_csig"], 1)
            step(V.tensor_tensor(cond[:, :], cond[:, :], PA[:, ROWS_A["c"]:ROWS_A["c"] + KC], ALU.mult))
            own(V.tensor_scalar(omka[:, :], PB[:, ROWS_B["k_a"]:ROWS_B["k_a"] + RP], -1.0, 1.0, ALU.mult, ALU.add))
            lg = PA[:, ROWS_A["lb"]:ROWS_A["lb"] + HG]
            V.tensor_tensor(lbv[:, 0, :], lg, lg, ALU.subtract).then_inc(S["su_lbe"], 1)
            V.wait_ge(S["su_csig"], 2)
            step(V.reciprocal(lbv[:, 2, :], lbv[:, 1, :]))
            step(V.tensor_tensor(lbv[:, 2, :], lbv[:, 2, :], lbv[:, 1, :], ALU.mult))
            step(V.tensor_tensor(lbv[:, 0, :], lbv[:, 2, :], lbv[:, 2, :], ALU.subtract))
            step(V.tensor_scalar(lbv[:, 1, :], lbv[:, 0, :], -1.0, 1.0, ALU.mult, ALU.add))
            for l in range(2):
                for k in range(KC):
                    V.wait_ge(su_ada[k % 4], ((l * KC + k) // 4 + 1) * 16)
                    if k == 0:
                        if l:
                            V.wait_ge(S["su_mm"], 2)
                        V.tensor_scalar(ada_acc, ada_w[k % 4], cond[:, k:k + 1], None, ALU.mult).then_inc(S["su_accd"], 1)
                    else:
                        V.wait_ge(S["su_accd"], l * KC + k)
                        V.scalar_tensor_tensor(out=ada_acc, in0=ada_w[k % 4], scalar=cond[:, k:k + 1], in1=ada_acc,
                                               op0=ALU.mult, op1=ALU.add).then_inc(S["su_accd"], 1)
                V.wait_ge(S["su_mm"], 2 * l + 2)
                V.wait_ge(S["su_post"], 32 * (l + 1))
                bias = PA[:, ROWS_A["ada_b"] + 24 * l:ROWS_A["ada_b"] + 24 * l + 24]
                own(V.tensor_tensor(shift[:, l, :], MS[:, 0:KC], bias[:, 0:KC], ALU.add))
                step(V.tensor_tensor(g1[:, l, :], MS[:, KC:2 * KC], bias[:, KC:2 * KC], ALU.add))
                pg = PA[:, ROWS_A["pre_g"] + KC * l:ROWS_A["pre_g"] + KC * l + KC]
                own(V.scalar_tensor_tensor(out=g1[:, l, :], in0=g1[:, l, :], scalar=1.0, in1=pg, op0=ALU.add, op1=ALU.mult))
                for e in range(2):
                    ee = slice(e * 512, (e + 1) * 512)
                    step(V.tensor_tensor(gpost[:, l, ee], gpost[:, l, ee], bank[e][:, :], ALU.add))
                step(V.tensor_tensor(gpost[:, l, :], gpost[:, l, :], postb, ALU.mult))
                V.nop().then_inc(S["su_gate"], 1)
            own.wait()
            for sem in [S["hp_ev"], S["h_y"], S["h_pooled"], S["pw_free"], S["rp_ev"], S["ms_free"], S["r_done"], S["w2_free"]] + w_used:
                V.sem_inc(sem, 1)
            V.sem_inc(S["x_out"], 16)
            V.nop().then_inc(S["su_done"], 1)
            own.restart()

            def norm(b, l):
                n = 2 * b + l
                V.wait_ge(S["n_rstd"], n + 1)
                for j in range(JT):
                    V.tensor_scalar(yT[:, j * D:(j + 1) * D], xres[:, j, :], stat[:, 1, j:j + 1], None, ALU.mult)\
                        .then_inc(S["n_xn"], 1)
                for k in range(1, KC, 2):
                    V.wait_ge(S["n_tr"], n * KC + k + 1)
                    V.tensor_scalar(hT[:, k, 1:1 + TB], bank[k % 4][:, :], g1[:, l, k:k + 1], shift[:, l, k:k + 1],
                                    ALU.mult, ALU.add).then_inc(S["n_ev_dve"], 1)

            def hgrn(b, gg, q):
                U, g = b * HG + 2 * gg + q, 2 * gg + q
                V.tensor_copy(Scur[:, :], Sall[:, ds(g, 1), :]).then_inc(S["h_s"], 1)
                V.wait_ge(S["h_en"], U + 1)
                V.tensor_scalar(h_en, h_en, CLAMP, None, ALU.min).then_inc(S["h_enc"], 1)
                for i, (s, raw) in enumerate(((h_sq, h_uq[q]), (h_sgp, h_ugp[q]), (h_sgh, h_ugh[q]))):
                    V.wait_ge(S["h_sig"], U * 3 + i + 1)
                    own(V.tensor_tensor(s, s, raw, ALU.mult))
                V.wait_ge(S["h_sp"], U + 1)
                step(V.scalar_tensor_tensor(out=h_e1, in0=h_uf[q], scalar=0.0, in1=h_e1, op0=ALU.min, op1=ALU.subtract))
                V.tensor_tensor(h_D[0], h_e1, h_uf[q], ALU.subtract).then_inc(S["h_lsu"], 1)
                V.wait_ge(S["h_l2"], U + 1)
                step(V.tensor_tensor(h_e1, h_e1, h_l2, ALU.add))
                V.tensor_tensor_scan(h_cum, reset128[:, :], h_e1, 0.0, ALU.mult, ALU.add).then_inc(S["h_cum"], 1)
                V.wait_ge(S["h_k"], U + 1)
                V.tensor_scalar(h_k, h_k, omlb[:, ds(g, 1)], None, ALU.mult).then_inc(S["h_z"], 1)
                V.wait_ge(S["h_cum"], U + 1)

                def scores(n):
                    V.wait_ge(S["h_lv"], U * (LEVELS + 1) + n + 1)
                    lv = LV[n % 2][:, :].rearrange("p (c t) -> p c t", t=HC)
                    sc = h_sc.rearrange("p (c t) -> p c t", t=HC)
                    if n == 0:
                        V.tensor_tensor(sc, lv, ident[:, None, :].to_broadcast([P, JT, HC]), ALU.mult).then_inc(S["h_lvc"], 1)
                    else:
                        V.wait_ge(S["h_lvc"], U * (LEVELS + 1) + n)
                        plain(V)
                        V.copy_predicated(sc, lmask[:, LEVELS - n, None, :].to_broadcast([P, JT, HC]), lv)\
                            .then_inc(S["h_lvc"], 1)

                def diff(n):
                    m = HC >> n
                    if n >= 3:
                        V.wait_ge(S["h_e"], U * LEVELS + n - 2)
                    a = HC * JT // (2 * m)
                    cv, dv = (t.rearrange("p (a x) -> p a x", x=2 * m) for t in (h_cum, h_D[n % 2]))
                    V.tensor_tensor(dv, cv, cv[:, :, m - 1:m].to_broadcast([P, a, 2 * m]), ALU.subtract)\
                        .then_inc(S["h_dif"], 1)

                V.wait_ge(S["h_k"], U + 1)
                diff(1)
                diff(2)
                for n in range(1, LEVELS + 1):
                    m = HC >> n
                    V.wait_ge(S["h_e"], U * LEVELS + n)
                    kv, qv, zv = (t.rearrange("p (a x m) -> p a x m", x=2, m=m) for t in (h_k, h_sq, h_Z[n % 2]))
                    if n == 1:
                        V.wait_ge(S["h_z"], U * (LEVELS + 1) + 1)
                    own(V.tensor_tensor(zv[:, :, 0, :], zv[:, :, 0, :], kv[:, :, 0, :], ALU.mult))
                    V.tensor_tensor(zv[:, :, 1, :], zv[:, :, 1, :], qv[:, :, 1, :], ALU.mult).then_inc(S["h_z"], 1)
                    if n + 2 <= LEVELS:
                        diff(n + 2)
                    scores(n - 1)
                cv, dv = (t.rearrange("p (c x) -> p c x", x=HC) for t in (h_cum, h_D[0]))
                V.wait_ge(S["h_e"], U * LEVELS + 6)
                V.tensor_tensor(dv, cv, cv[:, :, HC - 1:HC].to_broadcast([P, JT, HC]), ALU.subtract).then_inc(S["h_dk"], 1)
                V.tensor_tensor(h_en, h_sq, h_ec, ALU.mult).then_inc(S["h_qd"], 1)
                scores(LEVELS)
                V.wait_ge(S["h_ek"], U + 1)
                V.tensor_tensor(h_kd, h_kd, h_k, ALU.mult).then_inc(S["h_kd"], 1)
                V.wait_ge(S["h_win"], U + 1)
                ws = h_ws.rearrange("p (w t) -> p w t", t=528)
                uu = h_U[q]
                own(V.scalar_tensor_tensor(out=h_pp, in0=ws[:, ds(g, 1), 16:528],
                                           scalar=invwin[:, ds(g, 1)], in1=uu[:, 16:528], op0=ALU.mult, op1=ALU.subtract))
                own.wait()
                step(V.tensor_tensor(h_pp[:, 0:16], ws[:, ds(g, 1), 16:32], corr[:, 0, ds(g, 1), :], ALU.mult))
                V.tensor_tensor(h_pp[:, 0:16], h_pp[:, 0:16], uu[:, 16:32], ALU.subtract).then_inc(S["h_pp"], 1)
                V.wait_ge(S["h_po"], U + 1)
                V.nop().then_inc(S["pw_free"], 1)
                V.scalar_tensor_tensor(out=yTv[:, ds(g, 1), :], in0=MS[:, :], scalar=PA[:, ds(g + ROWS_A["pool_scale"], 1)],
                                       in1=h_sgp, op0=ALU.mult, op1=ALU.mult).then_inc(S["h_pooled"], 1)
                for c in range(JT):
                    V.wait_ge(S["h_sz"], U * JT + c + 1)
                    V.wait_ge(S["h_s"], U * (JT + 1) + c + 1)
                    V.scalar_tensor_tensor(out=Scur[:, :], in0=Scur[:, :], scalar=h_ec[:, c * HC + HC - 1:c * HC + HC],
                                           in1=MS[:, 0:HC], op0=ALU.mult, op1=ALU.add).then_inc(S["h_s"], 1)
                V.wait_ge(S["h_s"], (U + 1) * (JT + 1))
                plain(V)
                own(V.tensor_copy(Sall[:, ds(g, 1), :], Scur[:, :]))
                V.wait_ge(S["h_rn"], U + 1)
                step(V.scalar_tensor_tensor(out=h_sqo, in0=OB[:, :], scalar=PA[:, ds(g + ROWS_A["onorm"], 1)], in1=h_rn,
                                            op0=ALU.mult, op1=ALU.mult))
                V.tensor_tensor(yTv[:, ds(g + HG, 1), :], h_sqo, h_sgh, ALU.mult).then_inc(S["h_y"], 1)
                own.restart()

            def residual(b, l):
                n0 = 2 * b + l
                V.wait_ge(S["op_ss"], (n0 + 1) * 8)
                sv = stat[:, 2, :].rearrange("p (j h) -> p j h", h=2)
                V.tensor_tensor(stat[:, 1, 0:4], sv[:, :, 0], sv[:, :, 1], ALU.add).then_inc(S["op_sum"], 1)
                if l:
                    V.wait_ge(S["r_load"], (b + 1) * 16)
                V.wait_ge(S["op_rstd"], n0 + 1)
                for n in range(8):
                    j, h = n // 2, n % 2
                    hh = slice(h * 512, (h + 1) * 512)
                    t = xm[:, n * 512:(n + 1) * 512]
                    step(V.scalar_tensor_tensor(out=t, in0=bank[n][:, :], scalar=stat[:, 1, 4 + j:5 + j], in1=gpost[:, l, hh],
                                                op0=ALU.mult, op1=ALU.mult))
                    V.tensor_tensor(xres[:, j, hh], xres[:, j, hh], t, ALU.add).then_inc(S["ob"], 1)
                own.restart()

            def mixes(b):
                V.wait_ge(S["n_ev_act"], (2 * b + 2) * 4)
                V.wait_ge(S["n_ev_dve"], (2 * b + 2) * 4)
                step(V.tensor_copy(hT[:, :, 0:1], hlast[:, :, None]))
                own(V.tensor_copy(hlast[:, :, None], hT[:, :, TB:TB + 1]))
                for k in range(KC):
                    own(V.tensor_tensor(yTv[:, k, :], hT[:, k, 0:TB], hT[:, k, 1:1 + TB], ALU.subtract))
                own.wait()

                def mix(dst, mu, signal):
                    for k in range(KC):
                        m = PB[:, ROWS_B["mu"] + mu * KC + k:ROWS_B["mu"] + mu * KC + k + 1]
                        own(V.scalar_tensor_tensor(out=xmv[dst][:, k, :], in0=yTv[:, k, :], scalar=m,
                                                   in1=hT[:, k, 1:1 + TB], op0=ALU.mult, op1=ALU.add))
                    if signal:
                        own.wait()
                        V.nop().then_inc(S["xm_r"], 1)

                mix(0, MU_W, False)
                mix(1, MU_A, True)
                mix(2, MU_V, False)
                mix(3, MU_Z, True)
                V.wait_ge(S["lo_pe"], b + 1)
                mix(0, MU_R, False)
                mix(1, MU_K, True)
                V.wait_ge(S["r_save"], (b + 1) * 16)
                V.memset(r_N, 0.0).then_inc(S["r_n0"], 1)
                own.restart()

            def rwkv_norm_center(u):
                V.wait_ge(S["y_mean"], u + 1)
                V.tensor_tensor(r_y, r_y, YB[:, :], ALU.subtract).then_inc(S["y_cent"], 1)

            def rwkv_norm_finish(u, p):
                V.wait_ge(S["r_var"], u + 1)
                step(V.tensor_tensor(r_y, r_y, r_yd, ALU.mult))
                step(V.tensor_scalar(r_y, r_y, PB[:, ds(p + ROWS_B["lnx_g"], 1)], PB[:, ds(p + ROWS_B["lnx_b"], 1)],
                                     ALU.mult, ALU.add))
                step(V.tensor_tensor(r_y, r_y, r_bv, ALU.add))
                V.tensor_tensor(yTv[:, ds(p, 1), :], r_y, r_z, ALU.mult).then_inc(S["r_done"], 1)

            def rwkv_prepare(b, pp, q, prev):
                u, p = b * RP + 2 * pp + q, 2 * pp + q

                def par(name):
                    return PB[:, ds(p + ROWS_B[name], 1)]

                if prev:
                    rwkv_norm_center(u - 1)
                V.wait_ge(S["rp_ev"], 1 + u * 6 + 1)
                step(V.tensor_tensor_scan(r_cs, reset64[:, :], r_sw, 0.0, ALU.mult, ALU.add))
                V.tensor_tensor(r_sw, r_cs, r_sw, ALU.subtract).then_inc(S["r_scan"], 1)
                V.wait_ge(S["rp_ev"], 1 + u * 6 + 4)
                own(V.tensor_scalar(r_km, r_av, par("k_a"), omka[:, ds(p, 1)], ALU.mult, ALU.add))
                V.wait_ge(S["ms_ready"], u * 3 + 1)
                V.tensor_scalar(r_tb, MS[:, :], 1e-24, None, ALU.max).then_inc(S["ms_free"], 1)
                own.wait()
                step(V.tensor_tensor(r_km, r_km, r_k, ALU.mult))
                V.scalar_tensor_tensor(out=r_ta, in0=r_r, scalar=par("r_k"), in1=r_km, op0=ALU.mult, op1=ALU.mult)\
                    .then_inc(S["r_rk"], 1)
                V.wait_ge(S["r_rs"], u + 1)
                V.wait_ge(S["r_dec"], u + 1)
                step(V.scalar_tensor_tensor(out=r_kn, in0=r_k, scalar=par("k_k"), in1=r_tb, op0=ALU.mult, op1=ALU.mult))
                ar, bk = (t.rearrange("p (c x t) -> p c x t", x=2, t=RC) for t in (r_AR, r_BK))

                def cv(t):
                    return t.rearrange("p (c t) -> p c t", t=RC)

                own(V.tensor_tensor(r_av, r_kn, r_av, ALU.mult))
                own(V.tensor_copy(r_ec[:, :, None], cv(r_cs)[:, :, RC - 1:RC]))
                own(V.scalar_tensor_tensor(out=ar[:, :, 0, :], in0=cv(r_kn), scalar=-1.0, in1=cv(r_sw), op0=ALU.mult, op1=ALU.mult))
                own(V.tensor_tensor(ar[:, :, 1, :], cv(r_r), cv(r_cs), ALU.mult))
                for h in range(2):
                    r = slice(64 * h, 64 * h + 64)
                    own(V.tensor_tensor(bk[r, :, h, :], cv(r_km)[r], cv(r_pv)[r], ALU.mult))
                own.wait()
                for h in range(2):
                    r = slice(64 * h, 64 * h + 64)
                    own(V.tensor_tensor(bk[r, :, 1 - h, :], cv(r_av)[r], cv(r_pv)[r], ALU.mult))
                own.wait()
                V.nop().then_inc(S["r_arbk"], 1)
                if prev:
                    rwkv_norm_finish(u - 1, p - 1)
                V.wait_ge(S["rp_ev"], 1 + u * 6 + 5)
                V.wait_ge(S["rk_sum"], u + 1)
                own(V.tensor_tensor(r_bv, XB[:, :], r_v, ALU.mult))
                for i in range(4):
                    V.wait_ge(S["sc_ready"], u * 4 + i + 1)
                    V.tensor_tensor(r_Gs[:, i * 512:(i + 1) * 512].rearrange("p (n e) -> p n e", e=P),
                                    bank[i][:, :].rearrange("p (n e) -> p n e", e=P),
                                    gmask[:, None, :].to_broadcast([P, 4, P]), ALU.mult).then_inc(S["sc_free"], 1)
                V.tensor_copy(Mcur[:, :], Mall[:, ds(p, 1), :]).then_inc(S["ch_m"], 1)
                tv, nv = (t.rearrange("p (c e) -> p c e", e=P) for t in (r_T, r_N))
                for h in range(2):
                    hh = slice(4 * h, 4 * h + 4)
                    V.wait_ge(S["r_n"], u * 2 + h + 1)
                    step(V.tensor_tensor(tv[:, hh, :], nv[:, hh, :], wmask[:, 0:1, :].to_broadcast([P, 4, P]), ALU.mult))
                    V.tensor_tensor(tv[:, hh, :], tv[:, hh, :], ident[:, None, :].to_broadcast([P, 4, P]), ALU.add)\
                        .then_inc(S["invT"], 1)
                for lv in range(5):
                    m = 2 << lv
                    nc4, tc4 = (second_half(t, lv) for t in (r_N, r_T))
                    wm = second_half(wmask[:, lv + 1, :], lv).to_broadcast([P, 4, P // (2 * m), m])

                    def half(h):
                        return second_half(bank[h][:, :], lv)

                    for h in range(2):
                        hh = slice(4 * h, 4 * h + 4)
                        V.wait_ge(S["inv1"], u * 10 + 2 * lv + h + 1)
                        V.tensor_tensor(nc4[:, hh], half(h), wm, ALU.mult).then_inc(S["invw"], 1)
                    for h in range(2):
                        hh = slice(4 * h, 4 * h + 4)
                        V.wait_ge(S["inv2"], u * 10 + 2 * lv + h + 1)
                        V.wait_ge(S["invT"], u * 12 + 2 * lv + h + 1)
                        V.tensor_tensor(tc4[:, hh], tc4[:, hh], half(h), ALU.add).then_inc(S["invT"], 1)

            def rwkv_chain(b, pp, q):
                u, p = b * RP + 2 * pp + q, 2 * pp + q
                for c in range(NCH):
                    if c == 2:
                        V.wait_ge(S["r_sig"], u + 1)
                        own(V.tensor_tensor(r_z, r_z, r_zs, ALU.mult))
                    V.wait_ge(S["ch_x"], u * NCH + c + 1)
                    V.tensor_copy(r_xs, XB[:, 0:64]).then_inc(S["ch_xs"], 1)
                    V.wait_ge(S["ch_u"], u * NCH + c + 1)
                    own(V.tensor_copy(r_UV[64:128, c * P:c * P + 64], UZ[64:128, 0:64]))
                    V.tensor_copy(r_UV[0:64, c * P + 64:(c + 1) * P], UZ[0:64, 0:64]).then_inc(S["ch_us"], 1)
                    V.wait_ge(S["ch_z"], u * NCH + c + 1)
                    V.wait_ge(S["ch_pm"], u * NCH + c + 1)
                    V.scalar_tensor_tensor(out=Mcur[:, :], in0=UZ[:, 128:192], scalar=r_ec[:, c:c + 1],
                                           in1=r_pm, op0=ALU.mult, op1=ALU.add).then_inc(S["ch_m"], 1)
                V.wait_ge(S["ch_m"], (u + 1) * (NCH + 1))
                plain(V)
                own(V.tensor_copy(Mall[:, ds(p, 1), :], Mcur[:, :]))
            with V.Fori(0, n_blocks) as b:
                norm(b, 0)
                with V.Fori(0, HG // 2) as gg:
                    for q in range(2):
                        hgrn(b, gg, q)
                own(V.tensor_copy(corr[:, 0, :, :], corr[:, 1, :, :]))
                residual(b, 0)
                norm(b, 1)
                mixes(b)
                last = RP // 2 - 1
                rwkv_prepare(b, 0, 0, False)
                own.restart()
                with V.Fori(0, last) as pp:
                    rwkv_chain(b, pp, 0)
                    rwkv_prepare(b, pp, 1, True)
                    own.restart()
                    rwkv_chain(b, pp, 1)
                    rwkv_prepare(b, pp + 1, 0, True)
                    own.restart()
                rwkv_chain(b, last, 0)
                rwkv_prepare(b, last, 1, True)
                rwkv_chain(b, last, 1)
                rwkv_norm_center((b + 1) * RP - 1)
                rwkv_norm_finish((b + 1) * RP - 1, RP - 1)
                own.restart()
                residual(b, 1)

        @block.gpsimd
        def _(gp):
            own = Own(gp, S["own_pool"])
            gp.iota(i_s, [[0, 128]], base=0, channel_multiplier=1).then_inc(S["su_iota"], 1)
            gp.iota(i_t, [[1, 128]], base=0, channel_multiplier=0).then_inc(S["su_iota"], 1)
            gp.iota(i_r, [[1, TB]], base=0, channel_multiplier=0).then_inc(S["su_iota"], 1)
            gp.wait_ge(S["su_done"], 1)

            def windows(b, gg, q):
                U, g = b * HG + 2 * gg + q, 2 * gg + q
                uu = h_U[q]
                ws = h_ws.rearrange("p (w t) -> p w t", t=528)
                gp.wait_ge(S["h_pooled"], 1 + U)
                gp.wait_ge(S["hp_ev"], 1 + U * NP + PROJ_U + 1)
                own(gp.tensor_copy(uu[:, 0:16], halo[:, ds(g, 1), :]))
                own.wait()
                own(gp.tensor_copy(halo[:, ds(g, 1), :], uu[:, TB:TB + 16]))
                src = uu
                for w in range(HG):
                    o = 1 << w
                    lo = 2 * o - 1
                    ins = gp.tensor_tensor(ws[:, w, lo:528], src[:, lo:528], src[:, lo - o:528 - o], ALU.add)
                    own(ins)
                    own.wait()
                    src = ws[:, w, :]
                gp.nop().then_inc(S["h_win"], 1)
                own.restart()

            with gp.Fori(0, n_blocks) as b:
                with gp.Fori(0, HG // 2) as gg:
                    for q in range(2):
                        windows(b, gg, q)


_INS = ["x", "c", "ada_w", "ada_b", "pre_g", "post_g", "ev_w_in", "ev_w_out", "pool_w", "pool_scale", "hgrn_lb_logits",
        "hgrn_onorm_g", "rw_mu", "rw_w_rkvz", "rw_w0", "rw_w1", "rw_w2", "rw_a0", "rw_a1", "rw_a2", "rw_k_k", "rw_k_a",
        "rw_r_k", "rw_lnx_g", "rw_lnx_b", "rw_w_out"]


def kernel(**inputs):
    import numpy as _np
    import concourse.bacc as _bacc
    from concourse import mybir as _mybir
    from concourse.bass_utils import run_bass_kernel_spmd as _run

    nc = _bacc.Bacc("TRN2", target_bir_lowering=False, num_devices=1)
    arrays, io = {}, {}
    for name in _INS:
        a = _np.ascontiguousarray(inputs[name])
        arrays[f"in_{name}"] = a
        io[name] = nc.dram_tensor(f"in_{name}", a.shape, _mybir.dt.from_np(a.dtype), kind="ExternalInput").ap()
    io["out"] = nc.dram_tensor("out_0", (1, SEQ, D), F32, kind="ExternalOutput").ap()
    build(nc, io)
    r = _run(nc, [arrays], core_ids=[0])
    return r.results[0]["out_0"]
```

```python
from contextlib import ExitStack

import concourse.bass as bass
import concourse.mybir as mybir
from concourse.alu_op_type import AluOpType as ALU

ACT = mybir.ActivationFunctionType
F32 = mybir.dt.float32
I32 = mybir.dt.int32
U8 = mybir.dt.uint8
ds = bass.ds

P = 128
D = 1024
KC = D // P
SEQ = 2048
TB = 512
JT = TB // P
HG = 4
RP = 8
NP = 6
HC = 128
LEVELS = 7
RC = 64
NCH = TB // RC
RN = 2 + 4 * KC
RN_CHAIN = 2 + 2 * KC + 2
GROUPS = [(0, 1), (2,), (3,)]
EARLY_K = [[0, 1, 2, 4, 5, 6], [0, 1, 2, 3, 4, 5, 6]]
EVAC_AT = [[0, 1], [], [], [2], [], [], [3], []]
SLOTS = 8
DECAY = 0.6065306597126334
EPS = 1e-6
LNX_EPS = 64e-5
SS_SCALE = 1e6
HALF_LN_SS = 6.907755278982137
CLAMP = 1e19

ROWS_A = {"ada_b": 0, "pre_g": 48, "c": 64, "pool_scale": 72, "onorm": 76, "lb": 80}
N_A = 84
ROWS_B = {"w0": 0, "a0": 8, "k_k": 16, "k_a": 24, "r_k": 32, "lnx_g": 40, "lnx_b": 48, "mu": 56}
N_B = 104
MU_R, MU_K, MU_V, MU_Z, MU_W, MU_A = range(6)

PROJ_F, PROJ_Q, PROJ_I, PROJ_U, PROJ_GP, PROJ_GH = range(NP)
HP_AT_LEVEL = [12, 14, 17, 20, 23, 26, 29, 32]
HP_AT_POOL, HP_AT_KEYS, HP_AT_CHAIN = 36, 38, 40
PROJ_GROUP = [2, 1, 3, 0, 4, 5]

LORA_SLOT = 7
USES = [(HG if s < NP else 0) + 1 + (1 if s == LORA_SLOT else 0) + 4 + 1 for s in range(SLOTS)]


def use_hgrn(b, g, s):
    return b * USES[s] + g


def use_out0(b, s):
    return b * USES[s] + (HG if s < NP else 0)


def use_lora(b):
    return b * USES[LORA_SLOT] + 1


def use_rwkv(b, pp, s):
    return b * USES[s] + (HG if s < NP else 0) + 1 + (1 if s == LORA_SLOT else 0) + pp


def use_out1(b, s):
    return use_rwkv(b, 4, s)


class Own:

    def __init__(self, eng, sem):
        self.eng, self.sem, self.n = eng, sem, 0

    def __call__(self, ins):
        ins.then_inc(self.sem, 1)
        self.n += 1
        return self.n

    def wait(self, n=None):
        self.eng.wait_ge(self.sem, self.n if n is None else n)

    def restart(self):
        if self.n:
            self.wait()
            self.eng.sem_clear(self.sem)
            self.n = 0


def build(nc, io, n_blocks=SEQ // TB):
    ctx = ExitStack()
    with ctx:
        def sb(name, shape, dt=F32):
            return ctx.enter_context(nc.sbuf_tensor(name, shape, dt))

        bank = [ctx.enter_context(nc.psum_tensor(f"bank{i}", [P, 512], F32)) for i in range(8)]
        MS, XB, UZ, YB = bank[4], bank[5], bank[6], bank[7]
        OB = bank[5]
        LV = [bank[6], bank[7]]

        arena = sb("arena", [P, 4096 + 4104 + 8900])
        xres = arena[:, 0:4096].rearrange("p (j d) -> p j d", j=JT)
        hT = arena[:, 4096:8200].rearrange("p (k t) -> p k t", k=KC)
        xm = sb("xm", [P, 4 * KC * TB])
        yT = sb("yT", [P, KC * TB])
        yTv = yT[:, :].rearrange("p (k t) -> p k t", k=KC)
        wring = sb("wring", [P, SLOTS, 1024])
        gpost = sb("gpost", [P, 2, D])
        reset64 = sb("reset64", [P, TB])
        reset128 = sb("reset128", [P, TB])
        gmask = sb("gmask", [P, 128])
        wmask = sb("wmask", [P, 6, 128])
        lmask = sb("lmask", [P, 8, 128], U8)
        ident = sb("ident", [P, 128])
        ones = sb("ones", [P, 128])
        blk = sb("blk", [P, 128])
        blk64 = sb("blk64", [P, 128])
        PA = sb("PA", [P, N_A])
        PB = sb("PB", [P, N_B])
        g1 = sb("g1", [P, 2, KC])
        shift = sb("shift", [P, 2, KC])
        omka = sb("omka", [P, RP])
        cond = sb("cond", [P, KC])
        lbv = sb("lbv", [P, 3, HG])
        lb, omlb = lbv[:, 0, :], lbv[:, 1, :]
        epsc = sb("epsc", [P, 4])
        eps_norm, eps_lnx, c_one, c_ss = (epsc[:, i:i + 1] for i in range(4))
        corr = sb("corr", [P, 2, HG, 16])
        invwin = sb("invwin", [P, HG])
        halo = sb("halo", [P, HG, 16])
        hlast = sb("hlast", [P, KC])
        Mall = sb("Mall", [P, RP, 64])
        Sall = sb("Sall", [P, HG, 128])
        Mcur = sb("Mcur", [P, 64])
        Scur = sb("Scur", [P, 128])
        w2a2 = sb("w2a2", [P, 2, 128])
        poolw = sb("poolw", [P, 128])
        lora = sb("lora", [P, TB])
        stat = sb("stat", [P, 3, 8])

        pos = [0]

        def hview(n):
            a = xm[:, pos[0]:pos[0] + n]
            pos[0] += n
            return a

        h_uf, h_uq, h_vT, h_ugp, h_ugh = ([hview(TB) for _ in range(2)] for _ in range(5))
        h_U = [hview(16 + TB) for _ in range(2)]
        h_sq, h_sgp, h_e1, h_en, h_l2, h_k, h_cum = (hview(TB) for _ in range(7))
        h_D = [hview(TB) for _ in range(2)]
        h_Z = [hview(TB) for _ in range(2)]
        h_sc, h_ec, h_kd, h_kdT, h_pp, h_sqo, h_rn = (hview(TB) for _ in range(7))
        h_ws = arena[:, 8200:8200 + 4 * 528]
        h_sgh = [arena[:, 10312 + i * TB:10312 + (i + 1) * TB] for i in range(2)]
        assert pos[0] <= 4 * KC * TB
        XN = 4096
        XP = 12288
        XS = 8192
        xmv = [xm[:, i * KC * TB:(i + 1) * KC * TB].rearrange("p (k t) -> p k t", k=KC) for i in range(4)]

        rpos = [0]

        def rview(n):
            a = arena[:, rpos[0]:rpos[0] + n]
            rpos[0] += n
            return a

        r_AR, r_BK = rview(1024), rview(1024)
        r_BKt, r_UV = rview(1024), rview(1024)
        r_Gs = rview(2048)
        r_N, r_L, r_T, r_TT = rview(1024), rview(1024), rview(1024), rview(1024)
        r_sw, r_cs, r_pv, r_av, r_k, r_v, r_r, r_z, r_ta, r_tb, r_km, r_kn, r_bv = (rview(TB) for _ in range(13))
        r_pm = rview(64)
        r_xs = rview(64)
        r_ec = rview(NCH)
        r_y, r_yd = r_L[:, 0:TB], r_L[:, TB:2 * TB]
        r_zs = r_TT[:, 0:TB]
        assert rpos[0] <= 4096 + 4104 + 8900, rpos[0]
        resid = nc.dram_tensor("residual_scratch", [n_blocks, P, JT * D], F32, kind="Internal").ap()

        ada_w = [xm[:, i * 3072:(i + 1) * 3072] for i in range(4)]
        ada_acc = [wring[:, 3 * i:3 * i + 3, :].rearrange("p s n -> p (s n)") for i in range(2)]
        rowsA = wring[:, 3, 0:128]
        rowsB = wring[:, 3, 128:256]
        m_s, m_t, m_x, m_y = (wring[:, 4, i * 128:(i + 1) * 128] for i in range(4))
        i_s, i_t, i_x, i_y = (wring[:, 5, i * 128:(i + 1) * 128].bitcast(I32) for i in range(4))
        i_r = wring[:, 6, 0:TB].bitcast(I32)
        i_r2 = wring[:, 6, 512:1024].bitcast(I32)
        postb = [wring[:, 7 - i, :] for i in range(2)]
        m_ge = wring[:, 4, 512:640]
        m_le = wring[:, 4, 640:768]

        names = """su_rows su_post su_iota su_tr su_param su_csig su_cond su_lbe su_acc su_accd su_mm
        su_done passed own_dve own_act own_pool r_save r_load n_std n_xn n_tr n_ev_act n_ev_dve w2_in pw_in
        pw_free hp_ready hp_ev h_sig h_gate h_sp h_en h_enc h_l2 h_lsu h_k h_cum h_ec h_dif h_e h_z h_lv h_lvc h_dk h_ek
        h_kd h_kt h_kdT h_qd h_win h_pp h_po h_pooled h_s h_sz h_o h_osq h_ss h_rn h_y op_ready op_std ob
        xm_k xm_r xa_m xa_r lo_in lo_pe lo_r rp_ready rp_ev w2_free r_ksq ms_ready ms_free r_sig rk_sum v_tok v_tr y_mean y_cent y_var r_rs r_scan r_dec r_arbk r_rk sc_ready
        sc_free r_n0 r_n tr_l l_r inv1 invw invt invtt inv2 invT ch_x ch_xs ch_u ch_us ch_z ch_m ch_pm y_ready y_sb
        r_dsq r_var r_done""".split()
        S = {n: ctx.enter_context(nc.semaphore(n)) for n in names}
        su_ada = [ctx.enter_context(nc.semaphore(f"su_ada{i}")) for i in range(4)]
        x_in = [ctx.enter_context(nc.semaphore(f"x_in{j}")) for j in range(JT)]
        x_pre = [ctx.enter_context(nc.semaphore(f"x_pre{j}")) for j in range(JT)]
        x_out = [ctx.enter_context(nc.semaphore(f"x_out{j}")) for j in range(JT)]
        w_in = [ctx.enter_context(nc.semaphore(f"w_in{s}")) for s in range(SLOTS)]
        w_used = [ctx.enter_context(nc.semaphore(f"w_used{s}")) for s in range(SLOTS)]
        block = ctx.enter_context(nc.Block())

        x_v = io["x"].rearrange("o (n j p) d -> (o n) p j d", j=JT, p=P)
        out_v = io["out"].rearrange("o (n j p) d -> (o n) p j d", j=JT, p=P)
        w_in_v = io["ev_w_in"][0].rearrange("(k p) (s g e) -> s g p k e", p=P, s=NP, g=HG)
        w_out_v = [io["ev_w_out"][0].rearrange("(k p) n -> k p n", p=P),
                   io["rw_w_out"][0].rearrange("(k p) n -> k p n", p=P)]
        rkvz_v = io["rw_w_rkvz"][0].rearrange("m (k p) (g e) -> m g p k e", p=P, g=RP)
        RKVZ = [1, 0, 2, 3]

        MIX_OF = [2, 3, 0, 1]

        def gs_at(c, h):
            return ((2 * (c // 4) + h) * 4 + c % 4) * P

        def second_half(t, lv):
            m = 2 << lv
            return t.rearrange("p (c a x m) -> p c a x m", x=2, m=m, a=P // (2 * m))[:, :, :, 1, :]

        def plain(eng):
            eng.sem_inc(S["passed"], 1)

        @block.sync
        def _(sp):
            n_rows = 0
            for src, at, dst in (
                    [(io["ada_b"].rearrange("l (r c) -> (l r) c", c=P), ROWS_A["ada_b"], rowsA),
                     (io["pre_g"].rearrange("l (r c) -> (l r) c", c=P), ROWS_A["pre_g"], rowsA),
                     (io["c"].rearrange("l (r c) -> (l r) c", c=P), ROWS_A["c"], rowsA),
                     (io["pool_scale"].rearrange("l (r c) -> (l r) c", c=P), ROWS_A["pool_scale"], rowsA),
                     (io["hgrn_onorm_g"].rearrange("l (r c) -> (l r) c", c=P), ROWS_A["onorm"], rowsA),
                     (io["hgrn_lb_logits"].rearrange("l (r c) -> (l r) c", c=P), ROWS_A["lb"], rowsA)]
                    + [(io[n].rearrange("l (r c) -> (l r) c", c=P), ROWS_B[m], rowsB) for n, m in
                       [("rw_w0", "w0"), ("rw_a0", "a0"), ("rw_k_k", "k_k"), ("rw_k_a", "k_a"),
                        ("rw_lnx_g", "lnx_g"), ("rw_lnx_b", "lnx_b")]]
                    + [(io["rw_r_k"].rearrange("l (r x) c -> (l r) (x c)", x=2), ROWS_B["r_k"], rowsB),
                       (io["rw_mu"].rearrange("l m (r c) -> (l m r) c", c=P), ROWS_B["mu"], rowsB)]):
                sp.dma_start(dst[at:at + src.shape[0], :], src).then_inc(S["su_rows"], 16)
                n_rows += 1
            assert n_rows == 14
            for i in range(2 * KC):
                if i >= 4:
                    sp.wait_ge(S["su_accd"], i - 3)
                sp.dma_start(ada_w[i % 4], io["ada_w"][i // KC, (i % KC) * P:(i % KC + 1) * P, :]).then_inc(su_ada[i % 4], 16)
                if i % KC == 0:
                    if i:
                        sp.wait_ge(S["su_accd"], 1)
                    sp.dma_start(postb[i // KC], io["post_g"][i // KC:i // KC + 1, :].to_broadcast([P, D])).then_inc(S["su_post"], 16)
                    sp.dma_start(gpost[:, i // KC, :], io["ada_b"][i // KC:i // KC + 1, 2 * D:3 * D].to_broadcast([P, D])).then_inc(S["su_post"], 16)
            sp.wait_ge(S["su_done"], 1)

            def load(slot, use, src, dst=None):
                sp.wait_ge(w_used[slot], 1 + use)
                plain(sp)
                sp.dma_start(wring[:, slot, :] if dst is None else dst, src).then_inc(w_in[slot], 16)

            def slot_k(slot):
                return wring[:, slot, :].rearrange("p (k e) -> p k e", k=KC)

            with sp.Fori(0, n_blocks) as b:
                with sp.Fori(0, HG) as g:
                    for s in range(NP):
                        load(s, use_hgrn(b, g, s), w_in_v[PROJ_GROUP[s], ds(g, 1)][0], slot_k(s))
                    sp.wait_ge(S["pw_free"], 1 + b * HG + g)
                    plain(sp)
                    sp.dma_start(poolw[:, :], io["pool_w"][0, ds(g, 1)][0]).then_inc(S["pw_in"], 16)
                for j in range(JT):
                    sp.wait_ge(x_out[j], (b + 1) * 16)
                    plain(sp)
                    sp.dma_start(xres[:, j, :], x_v[ds(b, 1)][0][:, j, :]).then_inc(x_in[j], 16)
                for s in range(SLOTS):
                    load(s, use_out0(b, s), w_out_v[0][s])
                sp.wait_ge(w_used[LORA_SLOT], 1 + use_lora(b))
                for i, n in enumerate(("rw_w1", "rw_a1")):
                    sp.dma_start(slot_k(LORA_SLOT)[:, :, 64 * i:64 * i + 64],
                                 io[n][0].rearrange("(k p) e -> p k e", p=P)).then_inc(w_in[LORA_SLOT] if i else S["lo_in"], 16)
                sp.wait_ge(S["ob"], (2 * b + 1) * 8)
                plain(sp)
                sp.dma_start(resid[ds(b, 1)][0], arena[:, 0:4096]).then_inc(S["r_save"], 16)
                with sp.Fori(0, RP // 2) as pp:
                    for q in range(2):
                        for m in range(4):
                            s = 4 * q + m
                            load(s, use_rwkv(b, pp, s), rkvz_v[RKVZ[m], ds(2 * pp + q, 1)][0], slot_k(s))
                        sp.wait_ge(S["w2_free"], 1 + b * RP + 2 * pp + q)
                        plain(sp)
                        for i, n in enumerate(("rw_w2", "rw_a2")):
                            sp.dma_start(w2a2[64 * i:64 * i + 64, q, :],
                                         io[n][0, :, ds((2 * pp + q) * P, P)]).then_inc(S["w2_in"], 16)
                for s in range(SLOTS):
                    load(s, use_out1(b, s), w_out_v[1][s])
                sp.wait_ge(S["y_ready"], (b + 1) * RP)
                plain(sp)
                sp.wait_ge(S["r_save"], (b + 1) * 16)
                plain(sp)
                sp.dma_start(arena[:, 0:4096], resid[ds(b, 1)][0]).then_inc(S["r_load"], 16)
                for j in range(JT):
                    sp.wait_ge(S["ob"], (2 * b + 1) * 8 + 2 * (j + 1))
                    plain(sp)
                    sp.dma_start(out_v[ds(b, 1)][0][:, j, :], xres[:, j, :]).then_inc(x_out[j], 16)
            for j in range(JT):
                sp.wait_ge(x_out[j], (n_blocks + 1) * 16)

        @block.tensor
        def _(pe):
            pe.wait_ge(S["su_iota"], 6)
            pe.wait_ge(S["su_rows"], 14 * 16)
            pe.transpose(MS[:, 0:N_A], rowsA[0:N_A, :], ident[0:N_A, 0:N_A]).then_inc(S["su_tr"], 1)
            pe.transpose(XB[:, 0:N_B], rowsB[0:N_B, :], ident[0:N_B, 0:N_B]).then_inc(S["su_tr"], 1)
            pe.wait_ge(S["su_param"], 2)
            for l in range(2):
                pe.wait_ge(S["su_accd"], KC * (l + 1))
                for e in range(2 * KC):
                    mm = pe.matmul(bank[4 + l][:, e:e + 1], ada_acc[l][:, e * P:(e + 1) * P], ones[:, 0:1], start=True, stop=True)
                mm.then_inc(S["su_mm"], 1)
                for e in range(2):
                    mm = pe.matmul(bank[2 * l + e][:, :], ones[:, :], ada_acc[l][:, 2 * D + e * 512:2 * D + (e + 1) * 512],
                                   start=True, stop=True)
                mm.then_inc(S["su_mm"], 1)
            pe.wait_ge(S["su_done"], 1)

            def norm_transposes(b, l):
                n = (2 * b + l) * 4
                pe.wait_ge(S["n_xn"], n + 4)
                for k in range(KC):
                    if k >= 4:
                        pe.wait_ge(S["n_ev_dve"] if k % 2 else S["n_ev_act"], n + (k - 4) // 2 + 1)
                    for j in range(JT):
                        mm = pe.transpose(bank[k % 4][:, j * P:(j + 1) * P],
                                          xm[:, XN + j * D + k * P:XN + j * D + (k + 1) * P], ident[:, :])
                    mm.then_inc(S["n_tr"], 1)
                pe.wait_ge(S["n_ev_act"], n + 4)
                pe.wait_ge(S["n_ev_dve"], n + 4)
                plain(pe)

            def hgrn_proj(b, g, n0, n1):
                U, q = b * HG + g, g % 2
                for n in range(n0, n1):
                    i, k = n // KC, n % KC
                    pj = bank[(NP * q + i) % 4]
                    if k == 0:
                        pe.wait_ge(w_in[i], (use_hgrn(b, g, i) + 1) * 16)
                        pe.wait_ge(S["hp_ev"], 1 + U * NP + (i - 3 if i >= 4 else 0))
                    w = wring[:, i, :].rearrange("p (k e) -> p k e", k=KC)
                    if i == PROJ_I:
                        j = k // 2
                        for kk in range(k % 2 * 4, k % 2 * 4 + 4):
                            mm = pe.matmul(pj[:, j * P:(j + 1) * P], hT[:, kk, 1 + j * P:1 + (j + 1) * P], w[:, kk, :],
                                           start=(kk == 0), stop=(kk == KC - 1))
                    else:
                        mm = pe.matmul(pj[:, :], w[:, k, :], hT[:, k, 1:1 + TB], start=(k == 0), stop=(k == KC - 1))
                    if k == KC - 1:
                        mm.then_inc(S["hp_ready"], 1)

            def hgrn_mix(b, g):
                U, q = b * HG + g, g % 2
                done = 0

                def ahead(n):
                    nonlocal done
                    if g + 1 < HG:
                        hgrn_proj(b, g + 1, done, n)
                    elif n > HP_AT_LEVEL[0]:
                        if done <= HP_AT_LEVEL[0]:
                            pe.wait_ge(S["h_y"], 1 + U)
                            pe.wait_ge(S["hp_ev"], 1 + (U + 1) * NP)
                            done = 0
                        out_early(b, 0, done // 2, n // 2)
                    done = n

                if g:
                    ahead(HP_AT_LEVEL[0])
                    pe.wait_ge(S["h_lvc"], U * (LEVELS + 1))
                for n in range(LEVELS + 1):
                    ahead(HP_AT_LEVEL[n])
                    pe.wait_ge(S["h_z"], U * (LEVELS + 1) + n + 1)
                    if n >= 2:
                        pe.wait_ge(S["h_lvc"], U * (LEVELS + 1) + n - 1)
                    for c in range(JT):
                        cc = slice(c * HC, (c + 1) * HC)
                        lhs, rhs = (h_k, h_sq) if n == 0 else (h_Z[n % 2], h_Z[n % 2])
                        mm = pe.matmul(LV[n % 2][:, cc], lhs[:, cc], rhs[:, cc], start=True, stop=True)
                    mm.then_inc(S["h_lv"], 1)
                ahead(HP_AT_POOL)
                pe.wait_ge(S["h_y"], 1 + U)
                pe.wait_ge(S["pw_in"], (U + 1) * 16)
                pe.wait_ge(S["h_pp"], U + 1)
                pe.matmul(MS[:, :], poolw[:, :], h_pp, start=True, stop=True).then_inc(S["h_po"], 1)
                ahead(HP_AT_KEYS)
                pe.wait_ge(S["h_kd"], U + 1)
                pe.wait_ge(S["h_pooled"], 1 + U + 1)
                for c in range(JT):
                    cc = slice(c * HC, (c + 1) * HC)
                    mm = pe.transpose(MS[:, cc], h_kd[:, cc], ident[:, :])
                mm.then_inc(S["h_kt"], 1)
                ahead(HP_AT_CHAIN)
                pe.wait_ge(S["h_qd"], U + 1)
                pe.wait_ge(S["h_lvc"], (U + 1) * (LEVELS + 1))
                pe.wait_ge(S["h_kdT"], U + 1)
                for c in range(JT):
                    cc = slice(c * HC, (c + 1) * HC)
                    if c:
                        ahead(HP_AT_CHAIN + c)
                    pe.wait_ge(S["h_s"], U * (JT + 1) + c + 1)
                    pe.matmul(OB[:, cc], Scur[:, :], h_en[:, cc], start=True, stop=False)
                    mm = pe.matmul(OB[:, cc], h_vT[q][:, cc], h_sc[:, cc], start=False, stop=True)
                    if c == JT - 1:
                        mm.then_inc(S["h_o"], 1)
                    pe.matmul(MS[:, 0:HC], h_kdT[:, cc], h_vT[q][:, cc], start=True, stop=True).then_inc(S["h_sz"], 1)
                ahead(HP_AT_CHAIN + JT)
                pe.wait_ge(S["h_osq"], U + 1)
                pe.wait_ge(S["h_s"], (U + 1) * (JT + 1))
                pe.matmul(MS[:, :], ones[:, :], h_sqo, start=True, stop=True).then_inc(S["h_ss"], 1)
                ahead(NP * KC)

            def out_early(b, l, e0, e1):
                for e in range(e0, e1):
                    k, n = EARLY_K[l][e // 4], e % 4
                    if n == 0:
                        use = use_out1(b, k) if l else use_out0(b, k)
                        pe.wait_ge(w_in[k], (use + 1) * 16)
                    pe.matmul(bank[n][:, :], yTv[:, k, (n // 2) * P:(n // 2 + 1) * P],
                              wring[:, k, (n % 2) * 512:(n % 2 + 1) * 512], start=(e < 4), stop=False)

            def out_proj(b, l):
                if l == 0:
                    pe.wait_ge(S["h_y"], 1 + (b + 1) * HG)
                else:
                    pe.wait_ge(S["r_done"], 1 + (b + 1) * RP)
                for gi, tiles in enumerate(GROUPS):
                    for k in range(KC):
                        if gi == 0 and k in EARLY_K[l]:
                            continue
                        if gi == 0 or (gi == 1 and k in EARLY_K[l]):
                            use = use_out1(b, k) if l else use_out0(b, k)
                            pe.wait_ge(w_in[k], (use + 1) * 16)
                        for j in tiles:
                            for h in range(2):
                                mm = pe.matmul(bank[2 * j + h][:, :], yTv[:, k, j * P:(j + 1) * P],
                                               wring[:, k, h * 512:(h + 1) * 512], start=(gi > 0 and k == 0), stop=(k == KC - 1))
                                if k == KC - 1:
                                    mm.then_inc(S["op_ready"], 1)
                        if gi == len(GROUPS) - 1 and k < KC - 1:
                            mm.then_inc(w_used[k], 1)

            def lora_down(b):
                pe.wait_ge(S["lo_in"], (b + 1) * 16)
                pe.wait_ge(w_in[LORA_SLOT], (use_lora(b) + 1) * 16)
                pe.wait_ge(S["xm_r"], b * 4 + 1)
                pe.wait_ge(S["xa_r"], (b + 1) * KC)
                w = wring[:, LORA_SLOT, :].rearrange("p (k e) -> p k e", k=KC)
                for k in range(KC):
                    pe.matmul(MS[0:64, :], w[:, k, 0:64], xmv[0][:, k, :], start=(k == 0), stop=(k == KC - 1))
                    mm = pe.matmul(MS[64:128, :], w[:, k, 64:128], xmv[1][:, k, :], start=(k == 0), stop=(k == KC - 1))
                mm.then_inc(S["lo_pe"], 1)

            def rwkv_proj(b, pp, q, n0, n1, first=False):
                u = b * RP + 2 * pp + q
                for n in range(n0, n1):
                    i, k = (n, 0) if n < 2 else (2 + (n - 2) // KC, (n - 2) % KC)
                    pj = YB if i == 5 else bank[(6 * q + i) % 4]
                    if k == 0 and i < 5:
                        pe.wait_ge(S["rp_ev"], 1 + u * 6 + (i - 3 if i >= 4 else 0))
                    if i < 2:
                        if i == 0:
                            pe.wait_ge(S["w2_in"], (u + 1) * 32)
                            pe.wait_ge(S["lo_r"], 2 * (b + 1))
                        r = slice(64 * i, 64 * i + 64)
                        mm = pe.matmul(pj[:, :], w2a2[r, q, :], lora[r, :], start=True, stop=True)
                    else:
                        s = 4 * q + i - 2
                        if i == 2 and first:
                            pe.wait_ge(S["xm_k"], b * KC + k + 1)
                        if i > 2 and k == 0:
                            pe.wait_ge(S["xm_r"], b * 4 + i - 1)
                        if k == 0:
                            pe.wait_ge(w_in[s], (use_rwkv(b, pp, s) + 1) * 16)
                        w = wring[:, s, :].rearrange("p (k e) -> p k e", k=KC)
                        mm = pe.matmul(pj[:, :], w[:, k, :], xmv[MIX_OF[i - 2]][:, k, :],
                                       start=(k == 0), stop=(k == KC - 1))
                    if i < 2 or k == KC - 1:
                        mm.then_inc(S["rp_ready"], 1)

            def rwkv_norm_mean(u):
                pe.wait_ge(S["y_sb"], u + 1)
                pe.matmul(YB[:, :], blk64[:, :], r_y, start=True, stop=True).then_inc(S["y_mean"], 1)

            def rwkv_norm_var(u):
                pe.wait_ge(S["r_dsq"], u + 1)
                pe.matmul(YB[:, :], blk64[:, :], r_yd, start=True, stop=True).then_inc(S["y_var"], 1)

            def rwkv_prepare(b, pp, q, prev):
                u = b * RP + 2 * pp + q
                if prev:
                    rwkv_norm_mean(u - 1)
                pe.wait_ge(S["r_ksq"], u + 1)
                pe.wait_ge(S["ms_free"], 1 + u * 3)
                pe.matmul(MS[:, :], blk[:, :], r_ta, start=True, stop=True).then_inc(S["ms_ready"], 1)
                rwkv_proj(b, pp, q, RN_CHAIN, RN_CHAIN + 2)
                if prev:
                    rwkv_norm_var(u - 1)
                rwkv_proj(b, pp, q, RN_CHAIN + 2, RN - KC - 2)
                pe.wait_ge(S["r_rk"], u + 1)
                pe.matmul(XB[:, :], blk[:, :], r_ta, start=True, stop=True).then_inc(S["rk_sum"], 1)
                rwkv_proj(b, pp, q, RN - KC - 2, RN - KC)
                if prev:
                    pe.wait_ge(S["r_var"], u)
                rwkv_proj(b, pp, q, RN - KC, RN - KC + 2)
                pe.wait_ge(S["rp_ev"], 1 + u * 6 + 5)
                for j in range(JT):
                    mm = pe.transpose(UZ[:, j * P:(j + 1) * P], r_v[:, j * P:(j + 1) * P], ident[:, :])
                mm.then_inc(S["v_tr"], 1)
                rwkv_proj(b, pp, q, RN - KC + 2, RN - KC + 5)
                pe.wait_ge(S["r_arbk"], u + 1)
                for h in range(2):
                    if h:
                        rwkv_proj(b, pp, q, RN - KC + 5, RN - KC + 6)
                    pe.wait_ge(S["ms_free"], 1 + u * 3 + 1 + h)
                    for c in range(4):
                        mm = pe.transpose(MS[:, c * P:(c + 1) * P], r_BK[:, (4 * h + c) * P:(4 * h + c + 1) * P], ident[:, :])
                    mm.then_inc(S["ms_ready"], 1)
                for c in range(NCH):
                    for h in range(2):
                        r = slice(64 * h, 64 * h + 64)
                        mm = pe.matmul(bank[2 * (c // 4) + h][:, c % 4 * P:(c % 4 + 1) * P], r_BK[r, c * P:(c + 1) * P],
                                       r_AR[r, c * P:(c + 1) * P], start=True, stop=True)
                        if c % 4 == 3:
                            mm.then_inc(S["sc_ready"], 1)
                for h in range(2):
                    rwkv_proj(b, pp, q, RN - KC + 6 + h, RN - KC + 7 + h)
                    pe.wait_ge(S["r_n"], u * 2 + h + 1)
                    for c in range(4):
                        mm = pe.transpose(bank[h][:, c * P:(c + 1) * P], r_N[:, (4 * h + c) * P:(4 * h + c + 1) * P], ident[:, :])
                    mm.then_inc(S["tr_l"], 1)
                pe.wait_ge(S["l_r"], (u + 1) * 2)
                for lv in range(5):
                    for h in range(2):
                        pe.wait_ge(S["invT"], u * 12 + 2 * lv + h + 1)
                        for c in range(4):
                            cc = slice((4 * h + c) * P, (4 * h + c + 1) * P)
                            mm = pe.transpose(bank[2 + h][:, c * P:(c + 1) * P], r_T[:, cc], ident[:, :])
                        mm.then_inc(S["invt"], 1)
                        for c in range(4):
                            cc = slice((4 * h + c) * P, (4 * h + c + 1) * P)
                            mm = pe.matmul(bank[h][:, c * P:(c + 1) * P], r_L[:, cc], r_T[:, cc], start=True, stop=True)
                        mm.then_inc(S["inv1"], 1)
                    for h in range(2):
                        pe.wait_ge(S["invtt"], u * 10 + 2 * lv + h + 1)
                        pe.wait_ge(S["invw"], u * 10 + 2 * lv + h + 1)
                        for c in range(4):
                            cc = slice((4 * h + c) * P, (4 * h + c + 1) * P)
                            mm = pe.matmul(bank[h][:, c * P:(c + 1) * P], r_TT[:, cc], r_N[:, cc], start=True, stop=True)
                        mm.then_inc(S["inv2"], 1)

            def rwkv_chunk(b, pp, q, c, nxt):

                def ahead(gap):
                    if nxt is None:
                        e = 4 * len(EARLY_K[1])
                        out_early(b, 1, e * (3 * c + gap) // (3 * NCH), e * (3 * c + gap + 1) // (3 * NCH))
                    else:
                        rwkv_proj(b, *nxt, -(-RN_CHAIN * (3 * c + gap) // (3 * NCH)), -(-RN_CHAIN * (3 * c + gap + 1) // (3 * NCH)))

                u = b * RP + 2 * pp + q
                heads = [(h, slice(64 * h, 64 * h + 64)) for h in range(2)]
                gs = [gs_at(c, h) for h in range(2)]
                a_c, r_c = slice(c * P, c * P + 64), slice(c * P + 64, (c + 1) * P)
                uv = slice(c * P, (c + 1) * P)
                if c == 0:
                    pe.wait_ge(S["invT"], (u + 1) * 12)
                    pe.wait_ge(S["ms_free"], 1 + (u + 1) * 3)
                    pe.wait_ge(S["v_tok"], u + 1)
                    pe.wait_ge(S["rp_ev"], 1 + (u + 1) * 6)
                    pe.wait_ge(S["r_done"], 1 + u)
                    plain(pe)
                for h, r in heads:
                    pe.matmul(XB[r, 0:64], r_Gs[r, gs[h]:gs[h] + 64],
                              r_UV[r, c * P + 64 * h:c * P + 64 * h + 64], start=True, stop=False)
                pe.wait_ge(S["ch_m"], u * (NCH + 1) + c + 1)
                plain(pe)
                for h, r in heads:
                    mm = pe.matmul(XB[r, 0:64], r_AR[r, a_c], Mcur[r, :], start=False, stop=True)
                mm.then_inc(S["ch_x"], 1)
                for h, r in heads:
                    pe.matmul(YB[r, c * RC:(c + 1) * RC], Mcur[r, :], r_AR[r, r_c], start=True, stop=False)
                ahead(0)
                pe.wait_ge(S["ch_xs"], u * NCH + c + 1)
                plain(pe)
                for h, r in heads:
                    mm = pe.matmul(UZ[64 - 64 * h:128 - 64 * h, 0:64], r_T[r, c * P + 64 * h:c * P + 64 * h + 64], r_xs[r, :],
                                   start=True, stop=True)
                mm.then_inc(S["ch_u"], 1)
                ahead(1)
                pe.wait_ge(S["ch_us"], u * NCH + c + 1)
                for h, r in heads:
                    mm = pe.matmul(UZ[r, 128:192], r_BKt[:, c * P + 64 * h:c * P + 64 * h + 64],
                                   r_UV[:, c * P + 64 * h:c * P + 64 * h + 64], start=True, stop=True)
                mm.then_inc(S["ch_z"], 1)
                for h, r in heads:
                    mm = pe.matmul(YB[r, c * RC:(c + 1) * RC], r_UV[:, c * P + 64 * h:c * P + 64 * h + 64],
                                   r_Gs[:, gs[h] + 64:gs[h] + P], start=False, stop=True)
                if c == NCH - 1:
                    mm.then_inc(S["y_ready"], 1)
                ahead(2)

            with pe.Fori(0, n_blocks) as b:
                norm_transposes(b, 0)
                hgrn_proj(b, 0, 0, NP * KC)
                for g in range(HG):
                    hgrn_mix(b, g)
                out_proj(b, 0)
                norm_transposes(b, 1)

                def chain(pp, q, nxt):
                    for c in range(NCH):
                        rwkv_chunk(b, pp, q, c, nxt)

                last = RP // 2 - 1
                rwkv_proj(b, 0, 0, 2, 2 + KC, True)
                lora_down(b)
                rwkv_proj(b, 0, 0, 2 + KC, 2 + 2 * KC)
                rwkv_proj(b, 0, 0, 0, 2)
                pe.wait_ge(S["rp_ev"], 1 + b * RP * 6 + 3)
                rwkv_proj(b, 0, 0, 2 + 2 * KC, RN_CHAIN)
                rwkv_prepare(b, 0, 0, False)
                with pe.Fori(0, last) as pp:
                    chain(pp, 0, (pp, 1))
                    rwkv_prepare(b, pp, 1, True)
                    chain(pp, 1, (pp + 1, 0))
                    rwkv_prepare(b, pp + 1, 0, True)
                chain(last, 0, (last, 1))
                rwkv_prepare(b, last, 1, True)
                chain(last, 1, None)
                rwkv_norm_mean((b + 1) * RP - 1)
                rwkv_norm_var((b + 1) * RP - 1)
                out_proj(b, 1)

        @block.scalar
        def _(act):
            own = Own(act, S["own_act"])
            act.wait_ge(S["su_tr"], 2)
            act.copy(PA[:, :], MS[:, 0:N_A]).then_inc(S["su_param"], 1)
            act.copy(PB[:, :], XB[:, 0:N_B]).then_inc(S["su_param"], 1)
            act.wait_ge(S["su_param"], 2)
            act.activation(cond[:, :], PA[:, ROWS_A["c"]:ROWS_A["c"] + KC], ACT.Sigmoid).then_inc(S["su_csig"], 1)
            act.wait_ge(S["su_lbe"], 1)
            act.activation(lbv[:, 1, :], lbv[:, 0, :], ACT.Exp).then_inc(S["su_csig"], 1)
            act.wait_ge(S["su_done"], 1)

            def rstd(out, in_, n, bias, ready):
                own(act.activation(out, in_, ACT.Ln, bias=bias, scale=1.0 / n))
                own.wait()
                act.activation(out, out, ACT.Exp, scale=-0.5).then_inc(ready, 1)

            def norm_squares(b, l, gi):
                for j in GROUPS[gi]:
                    if l == 0:
                        act.wait_ge(x_pre[j], (b + 1) * 16)
                    else:
                        act.wait_ge(S["ob"], 2 * b * 8 + 2 * (j + 1))
                    x_at = xres[:, j, :] if l else xm[:, XP + j * D:XP + (j + 1) * D]
                    own(act.activation(xm[:, XS + j * D:XS + (j + 1) * D], x_at, ACT.Square, accum_out=stat[:, 0, j:j + 1]))
                own.wait()
                j0, j1 = GROUPS[gi][0], GROUPS[gi][-1] + 1
                act.activation(stat[:, 1, j0:j1], stat[:, 0, j0:j1], ACT.Sqrt, bias=eps_norm, scale=1.0 / D)\
                    .then_inc(S["n_std"], 1)

            def norm_evac(b, l):
                n = 2 * b + l
                for k in range(0, KC, 2):
                    act.wait_ge(S["n_tr"], n * KC + k + 1)
                    act.activation(hT[:, k, 1:1 + TB], bank[k % 4][:, :], ACT.Identity, bias=shift[:, l, k:k + 1],
                                   scale=g1[:, l, k:k + 1]).then_inc(S["n_ev_act"], 1)

            def hgrn_evac(b, g, i):
                U, q = b * HG + g, g % 2
                dst = (h_uf[q], h_uq[q], h_vT[q], h_U[q][:, 16:16 + TB], h_ugp[q], h_ugh[q])[i]
                act.wait_ge(S["hp_ready"], U * NP + i + 1)
                act.nop().then_inc(w_used[i], 1)
                act.copy(dst, bank[(NP * q + i) % 4][:, :]).then_inc(S["hp_ev"], 1)

            def hgrn_exps(b, g):
                U, q = b * HG + g, g % 2
                act.wait_ge(S["hp_ev"], 1 + U * NP + PROJ_F + 1)
                if g:
                    act.wait_ge(S["h_cum"], U)
                own(act.activation(h_e1, h_uf[q], ACT.Abs))
                act.activation(h_l2, h_uf[q], ACT.Exp, scale=-1.0).then_inc(S["h_en"], 1)
                own.wait()
                own(act.activation(h_e1, h_e1, ACT.Exp, scale=-1.0))

            def hgrn_gates(b, g):
                U, q = b * HG + g, g % 2
                if g:
                    act.wait_ge(S["h_ss"], U)
                    own(act.activation(h_rn, MS[:, :], ACT.Ln, bias=eps_norm, scale=1.0 / HC))
                own.wait()
                act.activation(h_e1, h_e1, ACT.Ln, bias=c_one).then_inc(S["h_sp"], 1)
                act.wait_ge(S["h_enc"], U + 1)
                act.activation(h_l2, h_l2, ACT.Ln, bias=c_one, scale=lb[:, g:g + 1]).then_inc(S["h_l2"], 1)
                if g:
                    hgrn_evac(b, g, PROJ_GH)
                    act.wait_ge(S["h_s"], U * (JT + 1))
                    act.wait_ge(S["h_pooled"], 1 + U)
                act.wait_ge(S["hp_ev"], 1 + (U + 1) * NP)
                for dst, src in ((h_sq, h_uq[q]), (h_sgp, h_ugp[q]), (h_sgh[q], h_ugh[q])):
                    act.activation(dst, src, ACT.Sigmoid).then_inc(S["h_sig"], 1)
                if g:
                    act.activation(h_rn, h_rn, ACT.Exp, scale=-0.5).then_inc(S["h_rn"], 1)
                act.wait_ge(S["h_lsu"], U + 1)
                act.activation(h_k, h_D[0], ACT.Exp).then_inc(S["h_k"], 1)
                act.wait_ge(S["h_cum"], U + 1)
                act.activation(h_ec, h_cum, ACT.Exp).then_inc(S["h_ec"], 1)

            def hgrn_act(b, g):
                U, q = b * HG + g, g % 2

                def ahead(i):
                    if g + 1 < HG:
                        hgrn_evac(b, g + 1, i)

                act.wait_ge(S["h_y"], 1 + U)
                ahead(0)
                for n in range(1, LEVELS + 1):
                    m = HC >> n
                    act.wait_ge(S["h_dif"], U * LEVELS + n)
                    if n >= 3:
                        act.wait_ge(S["h_lv"], U * (LEVELS + 1) + n - 1)
                    dv, zv = (t.rearrange("p (a x m) -> p a x m", x=2, m=m) for t in (h_D[n % 2], h_Z[n % 2]))
                    own(act.activation(zv[:, :, 0, :], dv[:, :, 0, :], ACT.Exp, scale=-1.0))
                    act.activation(zv[:, :, 1, :], dv[:, :, 1, :], ACT.Exp).then_inc(S["h_e"], 1)
                    if n in (2, 5, 7):
                        ahead({2: 1, 5: 2, 7: 3}[n])
                act.wait_ge(S["h_dk"], U + 1)
                act.activation(h_kd, h_D[0], ACT.Exp, scale=-1.0).then_inc(S["h_ek"], 1)
                if g + 1 < HG:
                    hgrn_exps(b, g + 1)
                act.wait_ge(S["h_kt"], U + 1)
                act.copy(h_kdT, MS[:, :]).then_inc(S["h_kdT"], 1)
                ahead(4)
                act.wait_ge(S["h_o"], U + 1)
                act.activation(h_sqo, OB[:, :], ACT.Square).then_inc(S["h_osq"], 1)
                if g + 1 < HG:
                    hgrn_gates(b, g + 1)
                else:
                    act.wait_ge(S["h_ss"], U + 1)
                    rstd(h_rn, MS[:, :], HC, eps_norm, S["h_rn"])
                own.restart()

            def out_squares(b, l, gi):
                n0 = (2 * b + l) * 8
                for j in GROUPS[gi]:
                    for n in (2 * j, 2 * j + 1):
                        act.wait_ge(S["op_ready"], n0 + n + 1)
                        if n == 7:
                            act.nop().then_inc(w_used[7], 1)
                        own(act.activation(xm[:, n * 512:(n + 1) * 512], bank[n][:, :], ACT.Square,
                                           accum_out=stat[:, 2, n:n + 1]))
                own.wait()
                j0, j1 = GROUPS[gi][0], GROUPS[gi][-1] + 1
                sv = stat[:, 2, 2 * j0:2 * j1].rearrange("p (j h) -> p j h", h=2)
                own(act.activation(stat[:, 0, 4 + j0:4 + j1], sv[:, :, 1], ACT.Identity, bias=eps_norm, scale=1.0 / D))
                own.wait()
                for j in GROUPS[gi]:
                    ins = act.activation(stat[:, 1, 4 + j:5 + j], stat[:, 2, 2 * j:2 * j + 1], ACT.Sqrt,
                                         bias=stat[:, 0, 4 + j:5 + j], scale=1.0 / D)
                    if j == j1 - 1:
                        ins.then_inc(S["op_std"], 1)
                    else:
                        own(ins)

            def lora_act(b):
                act.wait_ge(S["lo_pe"], b + 1)
                act.nop().then_inc(w_used[LORA_SLOT], 1)
                act.activation(lora[0:64, :], MS[0:64, :], ACT.Tanh).then_inc(S["lo_r"], 1)
                act.copy(lora[64:128, :], MS[64:128, :]).then_inc(S["lo_r"], 1)

            def rwkv_evac(b, pp, q, i, n=None):
                u, p = b * RP + 2 * pp + q, 2 * pp + q
                act.wait_ge(S["rp_ready"], u * 6 + (i if n is None else n) + 1)
                if i == 1:
                    act.nop().then_inc(S["w2_free"], 1)
                if i >= 2:
                    act.nop().then_inc(w_used[4 * q + i - 2], 1)
                src = YB[:, :] if i == 5 else bank[(6 * q + i) % 4][:, :]
                if i == 0:
                    ins = act.activation(r_sw, src, ACT.Sigmoid, bias=PB[:, ds(p + ROWS_B["w0"], 1)])
                elif i == 1:
                    ins = act.activation(r_av, src, ACT.Sigmoid, bias=PB[:, ds(p + ROWS_B["a0"], 1)])
                elif i == 5:
                    ins = act.copy(r_z, src)
                else:
                    ins = act.copy((r_k, r_r, r_v)[i - 2], src)
                ins.then_inc(S["rp_ev"], 1)

            def rwkv_norm_copy(u):
                act.wait_ge(S["y_ready"], u + 1)
                act.copy(r_y, YB[:, :]).then_inc(S["y_sb"], 1)

            def rwkv_norm_square(u):
                act.wait_ge(S["y_cent"], u + 1)
                act.activation(r_yd, r_y, ACT.Square).then_inc(S["r_dsq"], 1)

            def rwkv_norm_ln(u):
                act.wait_ge(S["y_var"], u + 1)
                own(act.activation(r_yd, YB[:, :], ACT.Ln, bias=eps_lnx))

            def rwkv_act(b, pp, q, prev):
                u = b * RP + 2 * pp + q
                p = 2 * pp + q
                if prev:
                    rwkv_norm_copy(u - 1)
                act.wait_ge(S["rp_ev"], 1 + u * 6 + 4)
                act.activation(r_ta, r_k, ACT.Square, scale=PB[:, ds(p + ROWS_B["k_k"], 1)]).then_inc(S["r_ksq"], 1)
                if prev:
                    rwkv_norm_square(u - 1)
                act.wait_ge(S["ms_free"], 1 + u * 3 + 1)
                own(act.activation(r_tb, r_tb, ACT.Ln, scale=SS_SCALE))
                if prev:
                    rwkv_norm_ln(u - 1)
                own.wait()
                act.activation(r_tb, r_tb, ACT.Exp, scale=-0.5, bias=c_ss).then_inc(S["r_rs"], 1)
                act.wait_ge(S["r_scan"], u + 1)
                own(act.activation(r_pv, r_cs, ACT.Exp, scale=DECAY))
                own(act.activation(r_sw, r_sw, ACT.Exp, scale=-DECAY))
                own.wait()
                act.activation(r_cs, r_cs, ACT.Exp, scale=-DECAY).then_inc(S["r_dec"], 1)
                if prev:
                    act.activation(r_yd, r_yd, ACT.Exp, scale=-0.5).then_inc(S["r_var"], 1)
                rwkv_evac(b, pp, q, 4)
                act.wait_ge(S["v_tr"], u + 1)
                uv = r_UV.rearrange("p (j x e) -> p j x e", x=2, e=P)
                vt = UZ[:, :].rearrange("p (j e) -> p j e", e=P)
                for h in range(2):
                    for x in range(2):
                        r, e = slice(64 * h, 64 * h + 64), slice(64 * h, 64 * h + 64)
                        own(act.copy(uv[r, :, x, e], vt[64 * x:64 * x + 64, :, e]))
                own.wait()
                act.nop().then_inc(S["v_tok"], 1)
                for h in range(2):
                    act.wait_ge(S["ms_ready"], u * 3 + 2 + h)
                    act.copy(r_BKt[:, 512 * h:512 * h + 512], MS[:, :]).then_inc(S["ms_free"], 1)
                act.wait_ge(S["r_n0"], b + 1)
                gv = r_Gs.rearrange("p (a h c e) -> p a h c e", a=2, h=2, e=P)
                nv = r_N.rearrange("p (a c e) -> p a c e", a=2, e=P)
                for a in range(2):
                    act.wait_ge(S["sc_free"], u * 4 + 2 * a + 2)
                    for h in range(2):
                        r, rb = slice(64 * h, 64 * h + 64), slice(64 - 64 * h, 128 - 64 * h)
                        own(act.copy(nv[r, a, :, r], gv[rb, a, h, :, 0:64]))
                    own.wait()
                    act.nop().then_inc(S["r_n"], 1)
                for h in range(2):
                    act.wait_ge(S["tr_l"], u * 2 + h + 1)
                    act.copy(r_L[:, 512 * h:512 * h + 512], bank[h][:, :]).then_inc(S["l_r"], 1)
                act.wait_ge(S["r_done"], 1 + u)
                rwkv_evac(b, pp, q, 5)
                for lv in range(5):
                    for h in range(2):
                        act.wait_ge(S["invt"], u * 10 + 2 * lv + h + 1)
                        act.copy(r_TT[:, 512 * h:512 * h + 512], bank[2 + h][:, :]).then_inc(S["invtt"], 1)

            def rwkv_chain_act(b, pp, q, nxt):
                u = b * RP + 2 * pp + q
                for c in range(NCH):
                    act.wait_ge(S["ch_m"], u * (NCH + 1) + c + 1)
                    act.mul(r_pm, Mcur[:, :], r_ec[:, c:c + 1]).then_inc(S["ch_pm"], 1)
                    if c == 0:
                        act.wait_ge(S["invT"], (u + 1) * 12)
                        act.wait_ge(S["rp_ev"], 1 + (u + 1) * 6)
                        act.activation(r_zs, r_z, ACT.Sigmoid).then_inc(S["r_sig"], 1)
                    if nxt:
                        for i in EVAC_AT[c]:
                            rwkv_evac(b, *nxt, i)
                own.restart()

            with act.Fori(0, n_blocks) as b:
                for gi in range(len(GROUPS)):
                    norm_squares(b, 0, gi)
                norm_evac(b, 0)
                own.restart()
                for i in range(NP):
                    hgrn_evac(b, 0, i)
                hgrn_exps(b, 0)
                hgrn_gates(b, 0)
                for g in range(HG):
                    hgrn_act(b, g)
                for gi in range(len(GROUPS)):
                    out_squares(b, 0, gi)
                    norm_squares(b, 1, gi)
                norm_evac(b, 1)
                own.restart()
                for k in range(KC):
                    act.wait_ge(S["xm_k"], b * KC + k + 1)
                    act.mul(xmv[1][:, k, :], yTv[:, k, :], PB[:, ROWS_B["mu"] + MU_A * KC + k:ROWS_B["mu"] + MU_A * KC + k + 1])\
                        .then_inc(S["xa_m"], 1)
                last = RP // 2 - 1
                act.wait_ge(S["r_save"], (b + 1) * 16)
                rwkv_evac(b, 0, 0, 2, 0)
                lora_act(b)
                for n, i in enumerate((3, 0, 1)):
                    rwkv_evac(b, 0, 0, i, n + 1)
                rwkv_act(b, 0, 0, False)
                own.restart()
                with act.Fori(0, last) as pp:
                    rwkv_chain_act(b, pp, 0, (pp, 1))
                    rwkv_act(b, pp, 1, True)
                    rwkv_chain_act(b, pp, 1, (pp + 1, 0))
                    rwkv_act(b, pp + 1, 0, True)
                    own.restart()
                rwkv_chain_act(b, last, 0, (last, 1))
                rwkv_act(b, last, 1, True)
                rwkv_chain_act(b, last, 1, None)
                rwkv_norm_copy((b + 1) * RP - 1)
                rwkv_norm_square((b + 1) * RP - 1)
                rwkv_norm_ln((b + 1) * RP - 1)
                own.wait()
                act.activation(r_yd, r_yd, ACT.Exp, scale=-0.5).then_inc(S["r_var"], 1)
                own.restart()
                for gi in range(len(GROUPS)):
                    out_squares(b, 1, gi)
                own.restart()

        @block.vector
        def _(dve):
            own = Own(dve, S["own_dve"])
            V = dve

            def step(ins):
                own(ins)
                own.wait()

            V.sem_inc(S["rp_ev"], 1)
            V.wait_ge(S["su_iota"], 3)
            own(V.tensor_tensor(i_x, i_s, i_t, ALU.bitwise_xor))
            own(V.tensor_scalar(i_y, i_s, 63, None, ALU.bitwise_and))
            own(V.tensor_tensor(m_y, i_t, i_s, ALU.is_gt))
            own(V.memset(ones[:, :], 1.0))
            for v, col in ((EPS, 0), (LNX_EPS, 1), (1.0, 2), (HALF_LN_SS, 3)):
                own(V.memset(epsc[:, col:col + 1], v))
            own.wait()
            own(V.tensor_copy(m_x, i_x))
            own(V.tensor_copy(m_s, i_y))
            own(V.tensor_scalar(i_s, i_t, 63, None, ALU.bitwise_and))
            own.wait()
            V.tensor_scalar(ident[:, :], m_x, 0.0, None, ALU.is_equal).then_inc(S["su_iota"], 3)
            own(V.tensor_scalar(blk[:, :], m_x, 64.0, None, ALU.is_lt))
            own(V.tensor_scalar(blk64[:, :], m_x, 64.0, 1.0 / 64, ALU.is_lt, ALU.mult))
            own(V.tensor_copy(m_t, i_s))
            own(V.tensor_tensor(m_x, m_x, m_y, ALU.mult))
            own.wait()
            own(V.tensor_tensor(gmask[:, 0:64], m_t[:, 0:64], m_s[:, 0:64], ALU.is_gt))
            own(V.tensor_tensor(gmask[:, 64:128], m_t[:, 64:128], m_s[:, 64:128], ALU.is_ge))
            for j in range(LEVELS):
                step(V.tensor_scalar(m_ge, m_x, float(1 << j), None, ALU.is_ge))
                if j < 6:
                    own(V.scalar_tensor_tensor(out=wmask[:, j, :], in0=m_x, scalar=float(2 << j), in1=m_ge,
                                               op0=ALU.is_lt, op1=ALU.mult))
                own(V.scalar_tensor_tensor(out=lmask[:, j, :], in0=m_x, scalar=float(2 << j), in1=m_ge,
                                           op0=ALU.is_lt, op1=ALU.mult))
                own.wait()
            own(V.tensor_scalar(i_r2, i_r, 63, None, ALU.bitwise_and))
            own.wait()
            own(V.tensor_scalar(reset64[:, :], i_r2, 1.0, None, ALU.is_ge))
            own.wait()
            own(V.tensor_scalar(i_r2, i_r, 127, None, ALU.bitwise_and))
            own.wait()
            own(V.tensor_scalar(reset128[:, :], i_r2, 1.0, None, ALU.is_ge))
            for g in range(HG):
                win = float(2 << g)
                own(V.tensor_scalar(corr[:, 0, g, :], i_t[:, 0:16], 1.0, win, ALU.add, ALU.min))
                own(V.memset(corr[:, 1, g, :], 1.0 / win))
                own(V.memset(invwin[:, g:g + 1], 1.0 / win))
            own.wait()
            own(V.reciprocal(corr[:, 0, :, :], corr[:, 0, :, :]))
            for t in (Mall, Sall, halo):
                own(V.memset(t[:, :, :], 0.0))
            own(V.memset(hlast[:, :], 0.0))
            V.wait_ge(S["su_csig"], 1)
            step(V.tensor_tensor(cond[:, :], cond[:, :], PA[:, ROWS_A["c"]:ROWS_A["c"] + KC], ALU.mult))
            own(V.tensor_scalar(omka[:, :], PB[:, ROWS_B["k_a"]:ROWS_B["k_a"] + RP], -1.0, 1.0, ALU.mult, ALU.add))
            lg = PA[:, ROWS_A["lb"]:ROWS_A["lb"] + HG]
            V.tensor_tensor(lbv[:, 0, :], lg, lg, ALU.subtract).then_inc(S["su_lbe"], 1)
            V.wait_ge(S["su_csig"], 2)
            step(V.reciprocal(lbv[:, 2, :], lbv[:, 1, :]))
            step(V.tensor_tensor(lbv[:, 2, :], lbv[:, 2, :], lbv[:, 1, :], ALU.mult))
            step(V.tensor_tensor(lbv[:, 0, :], lbv[:, 2, :], lbv[:, 2, :], ALU.subtract))
            step(V.tensor_scalar(lbv[:, 1, :], lbv[:, 0, :], -1.0, 1.0, ALU.mult, ALU.add))
            for l in range(2):
                for k in range(KC):
                    V.wait_ge(su_ada[k % 4], ((l * KC + k) // 4 + 1) * 16)
                    if k == 0:
                        V.tensor_scalar(ada_acc[l], ada_w[k % 4], cond[:, k:k + 1], None, ALU.mult).then_inc(S["su_accd"], 1)
                    else:
                        V.wait_ge(S["su_accd"], l * KC + k)
                        V.scalar_tensor_tensor(out=ada_acc[l], in0=ada_w[k % 4], scalar=cond[:, k:k + 1], in1=ada_acc[l],
                                               op0=ALU.mult, op1=ALU.add).then_inc(S["su_accd"], 1)
            for l in range(2):
                V.wait_ge(S["su_mm"], 2 * l + 2)
                V.wait_ge(S["su_post"], 32 * (l + 1))
                bias = PA[:, ROWS_A["ada_b"] + 24 * l:ROWS_A["ada_b"] + 24 * l + 24]
                own(V.tensor_tensor(shift[:, l, :], bank[4 + l][:, 0:KC], bias[:, 0:KC], ALU.add))
                step(V.tensor_tensor(g1[:, l, :], bank[4 + l][:, KC:2 * KC], bias[:, KC:2 * KC], ALU.add))
                pg = PA[:, ROWS_A["pre_g"] + KC * l:ROWS_A["pre_g"] + KC * l + KC]
                own(V.scalar_tensor_tensor(out=g1[:, l, :], in0=g1[:, l, :], scalar=1.0, in1=pg, op0=ALU.add, op1=ALU.mult))
                for e in range(2):
                    ee = slice(e * 512, (e + 1) * 512)
                    step(V.tensor_tensor(gpost[:, l, ee], gpost[:, l, ee], bank[2 * l + e][:, :], ALU.add))
                step(V.tensor_tensor(gpost[:, l, :], gpost[:, l, :], postb[l], ALU.mult))
            own.wait()
            for sem in [S["hp_ev"], S["h_y"], S["h_pooled"], S["pw_free"], S["ms_free"], S["r_done"], S["w2_free"]] + w_used:
                V.sem_inc(sem, 1)
            for sem in x_out:
                V.sem_inc(sem, 16)
            V.nop().then_inc(S["su_done"], 1)
            own.restart()

            def norm_scale(b, l, gi):
                j0, j1 = GROUPS[gi][0], GROUPS[gi][-1] + 1
                V.wait_ge(S["n_std"], (2 * b + l) * len(GROUPS) + gi + 1)
                step(V.reciprocal(stat[:, 1, j0:j1], stat[:, 1, j0:j1]))
                for j in range(j0, j1):
                    V.tensor_scalar(xm[:, XN + j * D:XN + (j + 1) * D],
                                    xres[:, j, :] if l else xm[:, XP + j * D:XP + (j + 1) * D], stat[:, 1, j:j + 1], None, ALU.mult)\
                        .then_inc(S["n_xn"], 1)

            def norm_evac(b, l):
                n = 2 * b + l
                for k in range(1, KC, 2):
                    V.wait_ge(S["n_tr"], n * KC + k + 1)
                    V.tensor_scalar(hT[:, k, 1:1 + TB], bank[k % 4][:, :], g1[:, l, k:k + 1], shift[:, l, k:k + 1],
                                    ALU.mult, ALU.add).then_inc(S["n_ev_dve"], 1)

            def hgrn_clamp(b, g):
                U = b * HG + g
                V.wait_ge(S["h_en"], U + 1)
                V.tensor_scalar(h_l2, h_l2, CLAMP, None, ALU.min).then_inc(S["h_enc"], 1)

            def hgrn_decays(b, g):
                U, q = b * HG + g, g % 2
                V.wait_ge(S["h_sp"], U + 1)
                step(V.scalar_tensor_tensor(out=h_e1, in0=h_uf[q], scalar=0.0, in1=h_e1, op0=ALU.min, op1=ALU.subtract))
                V.tensor_tensor(h_D[0], h_e1, h_uf[q], ALU.subtract).then_inc(S["h_lsu"], 1)
                V.wait_ge(S["h_l2"], U + 1)
                step(V.tensor_tensor(h_e1, h_e1, h_l2, ALU.add))
                V.tensor_tensor_scan(h_cum, reset128[:, :], h_e1, 0.0, ALU.mult, ALU.add).then_inc(S["h_cum"], 1)

            def hgrn_output(b, g):
                U, q = b * HG + g, g % 2
                V.wait_ge(S["h_rn"], U + 1)
                step(V.scalar_tensor_tensor(out=h_sqo, in0=OB[:, :], scalar=PA[:, ROWS_A["onorm"] + g:ROWS_A["onorm"] + g + 1],
                                            in1=h_rn, op0=ALU.mult, op1=ALU.mult))
                V.tensor_tensor(yTv[:, g + HG, :], h_sqo, h_sgh[q], ALU.mult).then_inc(S["h_y"], 1)

            def hgrn(b, g):
                U, q = b * HG + g, g % 2
                V.tensor_copy(Scur[:, :], Sall[:, g, :]).then_inc(S["h_s"], 1)
                for i, (s, raw) in enumerate(((h_sq, h_uq[q]), (h_sgp, h_ugp[q]), (h_sgh[q], h_ugh[q]))):
                    V.wait_ge(S["h_sig"], U * 3 + i + 1)
                    own(V.tensor_tensor(s, s, raw, ALU.mult))
                V.wait_ge(S["h_k"], U + 1)
                V.tensor_scalar(h_k, h_k, omlb[:, g:g + 1], None, ALU.mult).then_inc(S["h_z"], 1)
                V.wait_ge(S["h_cum"], U + 1)

                def scores(n):
                    V.wait_ge(S["h_lv"], U * (LEVELS + 1) + n + 1)
                    lv = LV[n % 2][:, :].rearrange("p (c t) -> p c t", t=HC)
                    sc = h_sc.rearrange("p (c t) -> p c t", t=HC)
                    if n == 0:
                        V.tensor_tensor(sc, lv, ident[:, None, :].to_broadcast([P, JT, HC]), ALU.mult).then_inc(S["h_lvc"], 1)
                    else:
                        V.wait_ge(S["h_lvc"], U * (LEVELS + 1) + n)
                        plain(V)
                        V.copy_predicated(sc, lmask[:, LEVELS - n, None, :].to_broadcast([P, JT, HC]), lv)\
                            .then_inc(S["h_lvc"], 1)

                def diff(n):
                    m = HC >> n
                    if n >= 3:
                        V.wait_ge(S["h_e"], U * LEVELS + n - 2)
                    a = HC * JT // (2 * m)
                    cv, dv = (t.rearrange("p (a x) -> p a x", x=2 * m) for t in (h_cum, h_D[n % 2]))
                    V.tensor_tensor(dv, cv, cv[:, :, m - 1:m].to_broadcast([P, a, 2 * m]), ALU.subtract)\
                        .then_inc(S["h_dif"], 1)

                V.wait_ge(S["h_k"], U + 1)
                diff(1)
                diff(2)
                for n in range(1, LEVELS + 1):
                    m = HC >> n
                    V.wait_ge(S["h_e"], U * LEVELS + n)
                    kv, qv, zv = (t.rearrange("p (a x m) -> p a x m", x=2, m=m) for t in (h_k, h_sq, h_Z[n % 2]))
                    if n == 1:
                        V.wait_ge(S["h_z"], U * (LEVELS + 1) + 1)
                    own(V.tensor_tensor(zv[:, :, 0, :], zv[:, :, 0, :], kv[:, :, 0, :], ALU.mult))
                    V.tensor_tensor(zv[:, :, 1, :], zv[:, :, 1, :], qv[:, :, 1, :], ALU.mult).then_inc(S["h_z"], 1)
                    if n + 2 <= LEVELS:
                        diff(n + 2)
                    scores(n - 1)
                cv, dv = (t.rearrange("p (c x) -> p c x", x=HC) for t in (h_cum, h_D[0]))
                V.wait_ge(S["h_e"], U * LEVELS + 6)
                V.tensor_tensor(dv, cv, cv[:, :, HC - 1:HC].to_broadcast([P, JT, HC]), ALU.subtract).then_inc(S["h_dk"], 1)
                V.tensor_tensor(h_en, h_sq, h_ec, ALU.mult).then_inc(S["h_qd"], 1)
                scores(LEVELS)
                V.wait_ge(S["h_ek"], U + 1)
                V.tensor_tensor(h_kd, h_kd, h_k, ALU.mult).then_inc(S["h_kd"], 1)
                V.wait_ge(S["h_win"], U + 1)
                ws = h_ws.rearrange("p (w t) -> p w t", t=528)
                uu = h_U[q]
                own(V.scalar_tensor_tensor(out=h_pp, in0=ws[:, g, 16:528],
                                           scalar=invwin[:, g:g + 1], in1=uu[:, 16:528], op0=ALU.mult, op1=ALU.subtract))
                own.wait()
                step(V.tensor_tensor(h_pp[:, 0:16], ws[:, g, 16:32], corr[:, 0, g, :], ALU.mult))
                V.tensor_tensor(h_pp[:, 0:16], h_pp[:, 0:16], uu[:, 16:32], ALU.subtract).then_inc(S["h_pp"], 1)
                V.wait_ge(S["h_po"], U + 1)
                V.nop().then_inc(S["pw_free"], 1)
                V.scalar_tensor_tensor(out=yTv[:, g, :], in0=MS[:, :], scalar=PA[:, ROWS_A["pool_scale"] + g:ROWS_A["pool_scale"] + g + 1],
                                       in1=h_sgp, op0=ALU.mult, op1=ALU.mult).then_inc(S["h_pooled"], 1)
                if g + 1 < HG:
                    hgrn_clamp(b, g + 1)
                for c in range(JT):
                    V.wait_ge(S["h_sz"], U * JT + c + 1)
                    V.wait_ge(S["h_s"], U * (JT + 1) + c + 1)
                    V.scalar_tensor_tensor(out=Scur[:, :], in0=Scur[:, :], scalar=h_ec[:, c * HC + HC - 1:c * HC + HC],
                                           in1=MS[:, 0:HC], op0=ALU.mult, op1=ALU.add).then_inc(S["h_s"], 1)
                V.wait_ge(S["h_s"], (U + 1) * (JT + 1))
                own(V.tensor_copy(Sall[:, g, :], Scur[:, :]))
                if g + 1 < HG:
                    hgrn_decays(b, g + 1)
                hgrn_output(b, g)
                own.restart()

            def residual(b, l, gi):
                j0, j1 = GROUPS[gi][0], GROUPS[gi][-1] + 1
                V.wait_ge(S["op_std"], (2 * b + l) * len(GROUPS) + gi + 1)
                step(V.reciprocal(stat[:, 1, 4 + j0:4 + j1], stat[:, 1, 4 + j0:4 + j1]))
                for j in range(j0, j1):
                    if l == 0:
                        V.wait_ge(x_in[j], (b + 1) * 16)
                    elif gi == 0:
                        V.wait_ge(S["r_load"], (b + 1) * 16)
                for n in range(2 * j0, 2 * j1):
                    j, h = n // 2, n % 2
                    hh = slice(h * 512, (h + 1) * 512)
                    t = xm[:, n * 512:(n + 1) * 512]
                    step(V.scalar_tensor_tensor(out=t, in0=bank[n][:, :], scalar=stat[:, 1, 4 + j:5 + j], in1=gpost[:, l, hh],
                                                op0=ALU.mult, op1=ALU.mult))
                    V.tensor_tensor(xres[:, j, hh], xres[:, j, hh], t, ALU.add).then_inc(S["ob"], 1)

            def mixes(b):
                V.wait_ge(S["n_ev_act"], (2 * b + 2) * 4)
                V.wait_ge(S["n_ev_dve"], (2 * b + 2) * 4)
                step(V.tensor_copy(hT[:, :, 0:1], hlast[:, :, None]))
                own(V.tensor_copy(hlast[:, :, None], hT[:, :, TB:TB + 1]))

                def diff(k):
                    return own(V.tensor_tensor(yTv[:, k, :], hT[:, k, 0:TB], hT[:, k, 1:1 + TB], ALU.subtract))

                def mix_k(dst, mu, k):
                    m = PB[:, ROWS_B["mu"] + mu * KC + k:ROWS_B["mu"] + mu * KC + k + 1]
                    return V.scalar_tensor_tensor(out=xmv[dst][:, k, :], in0=yTv[:, k, :], scalar=m,
                                                  in1=hT[:, k, 1:1 + TB], op0=ALU.mult, op1=ALU.add)

                def mix(dst, mu):
                    for k in range(KC):
                        own(mix_k(dst, mu, k))
                    own.wait()
                    V.nop().then_inc(S["xm_r"], 1)

                made = diff(0)
                for k in range(KC):
                    due, made = made, diff(k + 1) if k + 1 < KC else made
                    own.wait(due)
                    mix_k(2, MU_K, k).then_inc(S["xm_k"], 1)
                mix(0, MU_W)
                mix(3, MU_R)
                V.wait_ge(S["lo_pe"], b + 1)
                mix(0, MU_V)
                mix(1, MU_Z)
                V.wait_ge(S["r_save"], (b + 1) * 16)
                plain(V)
                own.restart()

            def rwkv_norm_center(u):
                V.wait_ge(S["y_mean"], u + 1)
                V.tensor_tensor(r_y, r_y, YB[:, :], ALU.subtract).then_inc(S["y_cent"], 1)

            def rwkv_norm_finish(u, p):
                V.wait_ge(S["r_var"], u + 1)
                step(V.tensor_tensor(r_y, r_y, r_yd, ALU.mult))
                step(V.tensor_scalar(r_y, r_y, PB[:, ds(p + ROWS_B["lnx_g"], 1)], PB[:, ds(p + ROWS_B["lnx_b"], 1)],
                                     ALU.mult, ALU.add))
                step(V.tensor_tensor(r_y, r_y, r_bv, ALU.add))
                V.tensor_tensor(yTv[:, ds(p, 1), :], r_y, r_z, ALU.mult).then_inc(S["r_done"], 1)

            def rwkv_prepare(b, pp, q, prev):
                u, p = b * RP + 2 * pp + q, 2 * pp + q

                def par(name):
                    return PB[:, ds(p + ROWS_B[name], 1)]

                if prev:
                    rwkv_norm_center(u - 1)
                V.wait_ge(S["rp_ev"], 1 + u * 6 + 4)
                step(V.tensor_tensor_scan(r_cs, reset64[:, :], r_sw, 0.0, ALU.mult, ALU.add))
                V.tensor_tensor(r_sw, r_cs, r_sw, ALU.subtract).then_inc(S["r_scan"], 1)
                own(V.tensor_scalar(r_km, r_av, par("k_a"), omka[:, ds(p, 1)], ALU.mult, ALU.add))
                V.wait_ge(S["ms_ready"], u * 3 + 1)
                V.tensor_scalar(r_tb, MS[:, :], 1e-24, None, ALU.max).then_inc(S["ms_free"], 1)
                own.wait()
                step(V.tensor_tensor(r_km, r_km, r_k, ALU.mult))
                V.scalar_tensor_tensor(out=r_ta, in0=r_r, scalar=par("r_k"), in1=r_km, op0=ALU.mult, op1=ALU.mult)\
                    .then_inc(S["r_rk"], 1)
                V.wait_ge(S["r_rs"], u + 1)
                V.wait_ge(S["r_dec"], u + 1)
                step(V.scalar_tensor_tensor(out=r_kn, in0=r_k, scalar=par("k_k"), in1=r_tb, op0=ALU.mult, op1=ALU.mult))
                ar, bk = (t.rearrange("p (c x t) -> p c x t", x=2, t=RC) for t in (r_AR, r_BK))

                def cv(t):
                    return t.rearrange("p (c t) -> p c t", t=RC)

                own(V.tensor_tensor(r_av, r_kn, r_av, ALU.mult))
                own(V.tensor_copy(r_ec[:, :, None], cv(r_cs)[:, :, RC - 1:RC]))
                own(V.scalar_tensor_tensor(out=ar[:, :, 0, :], in0=cv(r_kn), scalar=-1.0, in1=cv(r_sw), op0=ALU.mult, op1=ALU.mult))
                own(V.tensor_tensor(ar[:, :, 1, :], cv(r_r), cv(r_cs), ALU.mult))
                for h in range(2):
                    r = slice(64 * h, 64 * h + 64)
                    own(V.tensor_tensor(bk[r, :, h, :], cv(r_km)[r], cv(r_pv)[r], ALU.mult))
                own.wait()
                for h in range(2):
                    r = slice(64 * h, 64 * h + 64)
                    own(V.tensor_tensor(bk[r, :, 1 - h, :], cv(r_av)[r], cv(r_pv)[r], ALU.mult))
                own.wait()
                V.nop().then_inc(S["r_arbk"], 1)
                if prev:
                    rwkv_norm_finish(u - 1, p - 1)
                V.wait_ge(S["rp_ev"], 1 + u * 6 + 5)
                V.wait_ge(S["rk_sum"], u + 1)
                own(V.tensor_tensor(r_bv, XB[:, :], r_v, ALU.mult))
                if not prev:
                    V.memset(r_N, 0.0).then_inc(S["r_n0"], 1)
                for i in range(4):
                    V.wait_ge(S["sc_ready"], u * 4 + i + 1)
                    V.tensor_tensor(r_Gs[:, i * 512:(i + 1) * 512].rearrange("p (n e) -> p n e", e=P),
                                    bank[i][:, :].rearrange("p (n e) -> p n e", e=P),
                                    gmask[:, None, :].to_broadcast([P, 4, P]), ALU.mult).then_inc(S["sc_free"], 1)
                V.tensor_copy(Mcur[:, :], Mall[:, ds(p, 1), :]).then_inc(S["ch_m"], 1)
                tv, nv = (t.rearrange("p (c e) -> p c e", e=P) for t in (r_T, r_N))
                for h in range(2):
                    hh = slice(4 * h, 4 * h + 4)
                    V.wait_ge(S["r_n"], u * 2 + h + 1)
                    step(V.tensor_tensor(tv[:, hh, :], nv[:, hh, :], wmask[:, 0:1, :].to_broadcast([P, 4, P]), ALU.mult))
                    V.tensor_tensor(tv[:, hh, :], tv[:, hh, :], ident[:, None, :].to_broadcast([P, 4, P]), ALU.add)\
                        .then_inc(S["invT"], 1)
                for lv in range(5):
                    m = 2 << lv
                    nc4, tc4 = (second_half(t, lv) for t in (r_N, r_T))
                    wm = second_half(wmask[:, lv + 1, :], lv).to_broadcast([P, 4, P // (2 * m), m])

                    def half(h):
                        return second_half(bank[h][:, :], lv)

                    for h in range(2):
                        hh = slice(4 * h, 4 * h + 4)
                        V.wait_ge(S["inv1"], u * 10 + 2 * lv + h + 1)
                        V.tensor_tensor(nc4[:, hh], half(h), wm, ALU.mult).then_inc(S["invw"], 1)
                    for h in range(2):
                        hh = slice(4 * h, 4 * h + 4)
                        V.wait_ge(S["inv2"], u * 10 + 2 * lv + h + 1)
                        V.wait_ge(S["invT"], u * 12 + 2 * lv + h + 1)
                        V.tensor_tensor(tc4[:, hh], tc4[:, hh], half(h), ALU.add).then_inc(S["invT"], 1)

            def rwkv_chain(b, pp, q):
                u, p = b * RP + 2 * pp + q, 2 * pp + q
                for c in range(NCH):
                    if c == 2:
                        V.wait_ge(S["r_sig"], u + 1)
                        own(V.tensor_tensor(r_z, r_z, r_zs, ALU.mult))
                    V.wait_ge(S["ch_x"], u * NCH + c + 1)
                    V.tensor_copy(r_xs, XB[:, 0:64]).then_inc(S["ch_xs"], 1)
                    V.wait_ge(S["ch_u"], u * NCH + c + 1)
                    own(V.tensor_copy(r_UV[64:128, c * P:c * P + 64], UZ[64:128, 0:64]))
                    V.tensor_copy(r_UV[0:64, c * P + 64:(c + 1) * P], UZ[0:64, 0:64]).then_inc(S["ch_us"], 1)
                    V.wait_ge(S["ch_z"], u * NCH + c + 1)
                    V.wait_ge(S["ch_pm"], u * NCH + c + 1)
                    V.scalar_tensor_tensor(out=Mcur[:, :], in0=UZ[:, 128:192], scalar=r_ec[:, c:c + 1],
                                           in1=r_pm, op0=ALU.mult, op1=ALU.add).then_inc(S["ch_m"], 1)
                V.wait_ge(S["ch_m"], (u + 1) * (NCH + 1))
                plain(V)
                own(V.tensor_copy(Mall[:, ds(p, 1), :], Mcur[:, :]))
            with V.Fori(0, n_blocks) as b:
                for gi in range(len(GROUPS)):
                    norm_scale(b, 0, gi)
                norm_evac(b, 0)
                own.restart()
                hgrn_clamp(b, 0)
                hgrn_decays(b, 0)
                for g in range(HG):
                    hgrn(b, g)
                own(V.tensor_copy(corr[:, 0, :, :], corr[:, 1, :, :]))
                for gi in range(len(GROUPS)):
                    residual(b, 0, gi)
                    norm_scale(b, 1, gi)
                norm_evac(b, 1)
                own.restart()
                mixes(b)
                last = RP // 2 - 1
                rwkv_prepare(b, 0, 0, False)
                own.restart()
                with V.Fori(0, last) as pp:
                    rwkv_chain(b, pp, 0)
                    rwkv_prepare(b, pp, 1, True)
                    own.restart()
                    rwkv_chain(b, pp, 1)
                    rwkv_prepare(b, pp + 1, 0, True)
                    own.restart()
                rwkv_chain(b, last, 0)
                rwkv_prepare(b, last, 1, True)
                rwkv_chain(b, last, 1)
                rwkv_norm_center((b + 1) * RP - 1)
                rwkv_norm_finish((b + 1) * RP - 1, RP - 1)
                own.restart()
                for gi in range(len(GROUPS)):
                    residual(b, 1, gi)
                own.restart()

        @block.gpsimd
        def _(gp):
            own = Own(gp, S["own_pool"])
            gp.iota(i_s, [[0, 128]], base=0, channel_multiplier=1).then_inc(S["su_iota"], 1)
            gp.iota(i_t, [[1, 128]], base=0, channel_multiplier=0).then_inc(S["su_iota"], 1)
            gp.iota(i_r, [[1, TB]], base=0, channel_multiplier=0).then_inc(S["su_iota"], 1)

            def windows(b, gg, q):
                U, g = b * HG + 2 * gg + q, 2 * gg + q
                uu = h_U[q]
                ws = h_ws.rearrange("p (w t) -> p w t", t=528)
                gp.wait_ge(S["h_pooled"], 1 + U)
                gp.wait_ge(S["hp_ev"], 1 + U * NP + PROJ_U + 1)
                own(gp.tensor_copy(uu[:, 0:16], halo[:, ds(g, 1), :]))
                own.wait()
                own(gp.tensor_copy(halo[:, ds(g, 1), :], uu[:, TB:TB + 16]))
                src = uu
                for w in range(HG):
                    o = 1 << w
                    lo = 2 * o - 1
                    ins = gp.tensor_tensor(ws[:, w, lo:528], src[:, lo:528], src[:, lo - o:528 - o], ALU.add)
                    own(ins)
                    own.wait()
                    src = ws[:, w, :]
                gp.nop().then_inc(S["h_win"], 1)
                own.restart()

            with gp.Fori(0, n_blocks) as b:
                gp.wait_ge(S["rp_ev"], 1 + b * RP * 6)
                plain(gp)
                for j in range(JT):
                    gp.dma_start(xm[:, XP + j * D:XP + (j + 1) * D], x_v[ds(b, 1)][0][:, j, :]).then_inc(x_pre[j], 16)
                with gp.Fori(0, HG // 2) as gg:
                    for q in range(2):
                        windows(b, gg, q)
                for k in range(KC):
                    gp.wait_ge(S["xa_m"], b * KC + k + 1)
                    gp.tensor_tensor(xmv[1][:, k, :], xmv[1][:, k, :], hT[:, k, 1:1 + TB], ALU.add).then_inc(S["xa_r"], 1)


_INS = ["x", "c", "ada_w", "ada_b", "pre_g", "post_g", "ev_w_in", "ev_w_out", "pool_w", "pool_scale", "hgrn_lb_logits",
        "hgrn_onorm_g", "rw_mu", "rw_w_rkvz", "rw_w0", "rw_w1", "rw_w2", "rw_a0", "rw_a1", "rw_a2", "rw_k_k", "rw_k_a",
        "rw_r_k", "rw_lnx_g", "rw_lnx_b", "rw_w_out"]


def kernel(**inputs):
    import numpy as _np
    import concourse.bacc as _bacc
    from concourse import mybir as _mybir
    from concourse.bass_utils import run_bass_kernel_spmd as _run

    nc = _bacc.Bacc("TRN2", target_bir_lowering=False, num_devices=1)
    arrays, io = {}, {}
    for name in _INS:
        a = _np.ascontiguousarray(inputs[name])
        arrays[f"in_{name}"] = a
        io[name] = nc.dram_tensor(f"in_{name}", a.shape, _mybir.dt.from_np(a.dtype), kind="ExternalInput").ap()
    io["out"] = nc.dram_tensor("out_0", (1, SEQ, D), F32, kind="ExternalOutput").ap()
    build(nc, io)
    r = _run(nc, [arrays], core_ids=[0])
    return r.results[0]["out_0"]
```
